# Optimizing a Trainium2 kernel written in Bass

```python
import math
import jax, jax.numpy as jnp
from jax import lax
import numpy as np

D_MODEL = 2048
BATCH = 1
SEQ = 256
DEPTH = 2

SB_HEADS = 4
SB_HEAD_DIM = 128
SB_WIDTH = SB_HEADS * SB_HEAD_DIM
Q_BLOCK = 128
SSD_HEADS = 24
SSD_HEAD_DIM = 64
SSD_WIDTH = SSD_HEADS * SSD_HEAD_DIM
SSD_GROUPS = 4
SSD_STATE = 128
SSD_CONV = 4
SSD_CHUNK = 128
SSD_CONV_CH = SSD_WIDTH + 2 * SSD_GROUPS * SSD_STATE
AB_IN = 3 * SB_WIDTH + SSD_WIDTH + SSD_CONV_CH + SSD_HEADS
AB_SPLITS = [SB_WIDTH, 2 * SB_WIDTH, 3 * SB_WIDTH, 3 * SB_WIDTH + SSD_WIDTH, 3 * SB_WIDTH + SSD_WIDTH + SSD_CONV_CH]
AB_OUT = SB_WIDTH + SSD_WIDTH
LRU_WIDTH = 1536
LRU_BLOCK = 128
LRU_BLOCKS = LRU_WIDTH // LRU_BLOCK
LRU_CONV = 4
LRU_C = 8.0
S5_GROUPS = 32
S5_GROUP_CH = 16
S5_WIDTH = S5_GROUPS * S5_GROUP_CH
S5_STATE = 64
S5_CHUNK = 128
CD_IN = 2 * LRU_WIDTH + S5_WIDTH
CD_OUT = LRU_WIDTH + S5_WIDTH
D_FF = 4096
FFN_CONV = 3
EPS = 1e-6
N_EVEN = (DEPTH + 1) // 2
N_ODD = DEPTH // 2

kernel_name = 'hybrid_sb_ssd_rglru_s5_trunk'

def rmsnorm(x, g):
    xf = x.astype(jnp.float32)
    xf = xf * lax.rsqrt(jnp.mean(jnp.square(xf), axis=-1, keepdims=True) + EPS)
    return (xf * g.astype(jnp.float32)).astype(x.dtype)

def causal_dwconv(x, w, b):
    k, ch = w.shape
    y = lax.conv_general_dilated(x, w[:, None, :].astype(x.dtype), window_strides=(1,),
                                 padding=[(k - 1, 0)], dimension_numbers=('NWC', 'WIO', 'NWC'),
                                 feature_group_count=ch)
    return y + b.astype(y.dtype)

def _sb_schedule(nblk):
    half = (nblk + 1) // 2
    steps = nblk + 1
    ra = np.arange(half)[:, None]
    rb = nblk - 1 - ra
    k = np.arange(steps)[None, :]
    second = k > ra
    rows = np.where(second, rb, ra)
    kbs = np.where(second, rb - (k - ra - 1), ra - k)
    switch = k == ra + 1
    first = (k == 0) | switch
    return (jnp.asarray(ra[:, 0], jnp.int32), jnp.asarray(rb[:, 0], jnp.int32),
            jnp.asarray(rows, jnp.int32), jnp.asarray(kbs, jnp.int32),
            jnp.asarray(first), jnp.asarray(switch))

def stick_breaking_attention(q, k, v):
    f32 = jnp.float32
    bsz, nh, seq, dh = q.shape
    nblk = seq // Q_BLOCK
    qf = q.astype(f32) * (dh ** -0.5)
    kf = k.astype(f32)
    vf = v.astype(f32)
    ra, rb, rows, kbs, first, switch = _sb_schedule(nblk)
    tri = jnp.tril(jnp.ones((Q_BLOCK, Q_BLOCK), f32))
    loc = jnp.arange(Q_BLOCK)
    strict = loc[None, :] < loc[:, None]
    zeros_l = jnp.zeros((bsz, nh, Q_BLOCK), f32)
    zeros_a = jnp.zeros((bsz, nh, Q_BLOCK, dh), f32)

    def pair(args):
        rows_p, kbs_p, first_p, switch_p = args

        def step(carry, inp):
            logsum, acc, saved = carry
            row, kb, fst, sw = inp
            saved = jnp.where(sw, acc, saved)
            logsum = jnp.where(fst, 0.0, logsum)
            acc = jnp.where(fst, 0.0, acc)
            q_blk = lax.dynamic_slice_in_dim(qf, row * Q_BLOCK, Q_BLOCK, axis=2)
            k_blk = lax.dynamic_slice_in_dim(kf, kb * Q_BLOCK, Q_BLOCK, axis=2)
            v_blk = lax.dynamic_slice_in_dim(vf, kb * Q_BLOCK, Q_BLOCK, axis=2)
            z = jnp.einsum('bhqd,bhkd->bhqk', q_blk, k_blk)
            mask = (kb < row) | strict
            log_1mb = jnp.where(mask, -jax.nn.softplus(z), 0.0)
            suffix = log_1mb @ tri
            w = jnp.exp(jnp.where(mask, z + suffix + logsum[..., None], -jnp.inf))
            acc = acc + jnp.einsum('bhqk,bhkd->bhqd', w, v_blk)
            logsum = logsum + suffix[..., 0]
            return (logsum, acc, saved), None

        (_, acc, saved), _ = lax.scan(step, (zeros_l, zeros_a, zeros_a), (rows_p, kbs_p, first_p, switch_p))
        return saved, acc

    out_a, out_b = lax.map(pair, (rows, kbs, first, switch))
    out = jnp.zeros((nblk, bsz, nh, Q_BLOCK, dh), f32).at[ra].set(out_a).at[rb].set(out_b)
    return out.transpose(1, 0, 3, 2, 4).reshape(bsz, seq, nh * dh)

def ssd_mixer(z, xbc, dt_raw, conv_w, conv_b, dt_bias, a_log, d_skip, norm_g):
    f32 = jnp.float32
    bsz, seq, _ = xbc.shape
    nc, L = seq // SSD_CHUNK, SSD_CHUNK
    G, R, P, N = SSD_GROUPS, SSD_HEADS // SSD_GROUPS, SSD_HEAD_DIM, SSD_STATE
    xbc = jax.nn.silu(causal_dwconv(xbc, conv_w, conv_b).astype(f32))
    xs, bm, cm = jnp.split(xbc, [SSD_WIDTH, SSD_WIDTH + G * N], axis=-1)
    xs = xs.reshape(bsz, nc, L, G, R, P)
    bm = bm.reshape(bsz, nc, L, G, N)
    cm = cm.reshape(bsz, nc, L, G, N)
    dt = jax.nn.softplus(dt_raw.astype(f32) + dt_bias.astype(f32)).reshape(bsz, nc, L, G, R)
    a = -jnp.exp(a_log.astype(f32)).reshape(G, R)
    cs = jnp.cumsum(dt * a, axis=2)
    xdt = xs * dt[..., None]
    causal = jnp.tril(jnp.ones((L, L), dtype=bool))[:, :, None, None]
    decay = jnp.exp(jnp.where(causal, cs[:, :, :, None] - cs[:, :, None, :], -jnp.inf))
    cb = jnp.einsum('bclgn,bcsgn->bclsg', cm, bm)
    y_diag = jnp.einsum('bclsgr,bcsgrp->bclgrp', cb[..., None] * decay, xdt)
    to_end = jnp.exp(cs[:, :, -1:] - cs)
    chunk_states = jnp.einsum('bclgn,bclgrp->bcgrpn', bm, xdt * to_end[..., None])
    chunk_decay = jnp.exp(cs[:, :, -1])

    def carry_state(h, inp):
        st, dec = inp
        return h * dec[..., None, None] + st, h

    h0 = jnp.zeros((bsz, G, R, P, N), f32)
    _, prev = lax.scan(carry_state, h0, (jnp.moveaxis(chunk_states, 1, 0), jnp.moveaxis(chunk_decay, 1, 0)))
    prev = jnp.moveaxis(prev, 0, 1)
    y_off = jnp.einsum('bclgn,bcgrpn->bclgrp', cm, prev) * jnp.exp(cs)[..., None]
    y = y_diag + y_off + xs * d_skip.astype(f32).reshape(G, R)[:, :, None]
    y = y.reshape(bsz, seq, SSD_WIDTH) * jax.nn.silu(z.astype(f32))
    return rmsnorm(y, norm_g)

def rglru_mixer(gate_in, x_in, conv_w, conv_b, w_a, b_a, w_i, b_i, lam):
    f32 = jnp.float32
    bsz, seq, W = x_in.shape
    gate = jax.nn.gelu(gate_in.astype(f32))
    xc = causal_dwconv(x_in, conv_w, conv_b).astype(f32)
    xb = xc.reshape(bsz, seq, LRU_BLOCKS, LRU_BLOCK)
    r = jax.nn.sigmoid(jnp.einsum('bshi,hij->bshj', xb, w_a.astype(f32)).reshape(bsz, seq, W) + b_a.astype(f32))
    gate_i = jax.nn.sigmoid(jnp.einsum('bshi,hij->bshj', xb, w_i.astype(f32)).reshape(bsz, seq, W) + b_i.astype(f32))
    log_a = -LRU_C * r * jax.nn.softplus(-lam.astype(f32))
    a = jnp.exp(log_a)
    u = jnp.sqrt(-jnp.expm1(2.0 * log_a)) * (gate_i * xc)

    def step(h, inp):
        a_t, u_t = inp
        h = a_t * h + u_t
        return h, h

    _, hs = lax.scan(step, jnp.zeros((bsz, W), f32), (jnp.moveaxis(a, 1, 0), jnp.moveaxis(u, 1, 0)))
    return jnp.moveaxis(hs, 0, 1) * gate

def _complex_combine(e1, e2):
    a1r, a1i, b1r, b1i = e1
    a2r, a2i, b2r, b2i = e2
    return (a2r * a1r - a2i * a1i, a2r * a1i + a2i * a1r,
            a2r * b1r - a2i * b1i + b2r, a2r * b1i + a2i * b1r + b2i)

def s5_mixer(u, log_dt, a_re, a_im, b_re, b_im, c_re, c_im, d_skip, w_glu, b_glu):
    f32 = jnp.float32
    bsz, seq, _ = u.shape
    G, GC, N, L = S5_GROUPS, S5_GROUP_CH, S5_STATE, S5_CHUNK
    nc = seq // L
    uf = u.astype(f32).reshape(bsz, seq, G, GC)
    dt = jnp.exp(log_dt.astype(f32))[:, None]
    lr = jnp.minimum(a_re.astype(f32), -1e-4)
    li = a_im.astype(f32)
    mag = jnp.exp(dt * lr)
    ab_r = mag * jnp.cos(dt * li)
    ab_i = mag * jnp.sin(dt * li)
    am1_r = jnp.expm1(dt * lr) * jnp.cos(dt * li) - 2.0 * jnp.square(jnp.sin(0.5 * dt * li))
    den = lr * lr + li * li
    f_r = (am1_r * lr + ab_i * li) / den
    f_i = (ab_i * lr - am1_r * li) / den
    br, bi = b_re.astype(f32), b_im.astype(f32)
    bb_r = f_r[..., None] * br - f_i[..., None] * bi
    bb_i = f_r[..., None] * bi + f_i[..., None] * br
    bu_r = jnp.einsum('bsgc,gnc->bsgn', uf, bb_r).reshape(bsz, nc, L, G, N)
    bu_i = jnp.einsum('bsgc,gnc->bsgn', uf, bb_i).reshape(bsz, nc, L, G, N)
    a_r_t = jnp.broadcast_to(ab_r, (1, 1, L, G, N))
    a_i_t = jnp.broadcast_to(ab_i, (1, 1, L, G, N))
    _, _, loc_r, loc_i = lax.associative_scan(_complex_combine, (a_r_t, a_i_t, bu_r, bu_i), axis=2)
    powers = jnp.arange(1, L + 1, dtype=f32)[:, None, None] * dt[None]
    pw_mag = jnp.exp(powers * lr)
    pw_r = pw_mag * jnp.cos(powers * li)
    pw_i = pw_mag * jnp.sin(powers * li)

    def carry_state(h, end):
        hr, hi = h
        er, ei = end
        nr = pw_r[-1] * hr - pw_i[-1] * hi + er
        ni = pw_r[-1] * hi + pw_i[-1] * hr + ei
        return (nr, ni), (hr, hi)

    h0 = jnp.zeros((bsz, G, N), f32)
    _, (p_r, p_i) = lax.scan(carry_state, (h0, h0),
                             (jnp.moveaxis(loc_r[:, :, -1], 1, 0), jnp.moveaxis(loc_i[:, :, -1], 1, 0)))
    p_r = jnp.moveaxis(p_r, 0, 1)[:, :, None]
    p_i = jnp.moveaxis(p_i, 0, 1)[:, :, None]
    s_r = (loc_r + pw_r * p_r - pw_i * p_i).reshape(bsz, seq, G, N)
    s_i = (loc_i + pw_r * p_i + pw_i * p_r).reshape(bsz, seq, G, N)
    y = (jnp.einsum('bsgn,gcn->bsgc', s_r, c_re.astype(f32))
         - jnp.einsum('bsgn,gcn->bsgc', s_i, c_im.astype(f32))
         + d_skip.astype(f32).reshape(G, GC) * uf)
    y = jax.nn.gelu(y.reshape(bsz, seq, S5_WIDTH))
    return y * jax.nn.sigmoid(y @ w_glu.astype(f32) + b_glu.astype(f32))

def attn_ssd_layer(y, w_in, conv_w, conv_b, dt_bias, a_log, d_skip, ssd_norm, w_out):
    bsz, seq, _ = y.shape
    q, k, v, z, xbc, dt_raw = jnp.split(y @ w_in, AB_SPLITS, axis=-1)

    def heads(t):
        return t.reshape(bsz, seq, SB_HEADS, SB_HEAD_DIM).transpose(0, 2, 1, 3)

    o_a = stick_breaking_attention(heads(q), heads(k), heads(v))
    o_b = ssd_mixer(z, xbc, dt_raw, conv_w, conv_b, dt_bias, a_log, d_skip, ssd_norm)
    return jnp.concatenate([o_a, o_b], axis=-1).astype(y.dtype) @ w_out

def lru_s5_layer(y, w_in, conv_w, conv_b, w_a, b_a, w_i, b_i, lam, log_dt, a_re, a_im,
                 b_re, b_im, c_re, c_im, d_skip, w_glu, b_glu, w_out):
    gate_in, x_in, u = jnp.split(y @ w_in, [LRU_WIDTH, 2 * LRU_WIDTH], axis=-1)
    o_c = rglru_mixer(gate_in, x_in, conv_w, conv_b, w_a, b_a, w_i, b_i, lam)
    o_d = s5_mixer(u, log_dt, a_re, a_im, b_re, b_im, c_re, c_im, d_skip, w_glu, b_glu)
    return jnp.concatenate([o_c, o_d], axis=-1).astype(y.dtype) @ w_out

def conv_ffn(y, w_up, conv_w, conv_b, w_down):
    val, gate = jnp.split(y @ w_up, 2, axis=-1)
    gate = causal_dwconv(gate, conv_w, conv_b)
    return (jax.nn.silu(gate) * val) @ w_down

def setup_inputs(seed: int = 0) -> dict:
    key = jax.random.key(seed)
    keys = iter(jax.random.split(key, 64))

    def nrm(shape, scale):
        return jax.random.normal(next(keys), shape, jnp.float32) * scale

    def uni(shape, lo, hi):
        return jax.random.uniform(next(keys), shape, jnp.float32, lo, hi)

    E, O, D = N_EVEN, N_ODD, D_MODEL
    ssd_dt = jnp.exp(uni((E, SSD_HEADS), math.log(1e-3), math.log(1e-1)))
    lru_a = uni((O, LRU_WIDTH), 0.9, 0.999)
    s5_freq = math.pi * jnp.arange(S5_STATE, dtype=jnp.float32)
    return {
        'x': nrm((BATCH, SEQ, D), 1.0),
        'norm_mix': 1.0 + nrm((DEPTH, D), 0.02),
        'norm_ffn': 1.0 + nrm((DEPTH, D), 0.02),
        'norm_final': 1.0 + nrm((D,), 0.02),
        'ab_w_in': nrm((E, D, AB_IN), D ** -0.5),
        'ab_conv_w': nrm((E, SSD_CONV, SSD_CONV_CH), SSD_CONV ** -0.5),
        'ab_conv_b': nrm((E, SSD_CONV_CH), 0.02),
        'ab_dt_bias': ssd_dt + jnp.log(-jnp.expm1(-ssd_dt)),
        'ab_a_log': jnp.log(uni((E, SSD_HEADS), 1.0, 16.0)),
        'ab_d_skip': 1.0 + nrm((E, SSD_HEADS), 0.1),
        'ab_ssd_norm': 1.0 + nrm((E, SSD_WIDTH), 0.02),
        'ab_w_out': nrm((E, AB_OUT, D), AB_OUT ** -0.5),
        'cd_w_in': nrm((O, D, CD_IN), D ** -0.5),
        'cd_conv_w': nrm((O, LRU_CONV, LRU_WIDTH), LRU_CONV ** -0.5),
        'cd_conv_b': nrm((O, LRU_WIDTH), 0.02),
        'cd_w_a': nrm((O, LRU_BLOCKS, LRU_BLOCK, LRU_BLOCK), LRU_BLOCK ** -0.5),
        'cd_b_a': nrm((O, LRU_WIDTH), 0.1),
        'cd_w_i': nrm((O, LRU_BLOCKS, LRU_BLOCK, LRU_BLOCK), LRU_BLOCK ** -0.5),
        'cd_b_i': nrm((O, LRU_WIDTH), 0.1),
        'cd_lambda': jnp.log(lru_a) - jnp.log1p(-lru_a),
        'cd_log_dt': uni((O, S5_GROUPS), math.log(1e-3), math.log(1e-1)),
        'cd_a_re': -0.5 + nrm((O, S5_GROUPS, S5_STATE), 0.01),
        'cd_a_im': s5_freq + nrm((O, S5_GROUPS, S5_STATE), 0.01),
        'cd_b_re': nrm((O, S5_GROUPS, S5_STATE, S5_GROUP_CH), (2 * S5_GROUP_CH) ** -0.5),
        'cd_b_im': nrm((O, S5_GROUPS, S5_STATE, S5_GROUP_CH), (2 * S5_GROUP_CH) ** -0.5),
        'cd_c_re': nrm((O, S5_GROUPS, S5_GROUP_CH, S5_STATE), S5_STATE ** -0.5),
        'cd_c_im': nrm((O, S5_GROUPS, S5_GROUP_CH, S5_STATE), S5_STATE ** -0.5),
        'cd_d_skip': nrm((O, S5_WIDTH), 1.0),
        'cd_w_glu': nrm((O, S5_WIDTH, S5_WIDTH), S5_WIDTH ** -0.5),
        'cd_b_glu': nrm((O, S5_WIDTH), 0.02),
        'cd_w_out': nrm((O, CD_OUT, D), CD_OUT ** -0.5),
        'ffn_w_up': nrm((DEPTH, D, 2 * D_FF), D ** -0.5),
        'ffn_conv_w': nrm((DEPTH, FFN_CONV, D_FF), FFN_CONV ** -0.5),
        'ffn_conv_b': nrm((DEPTH, D_FF), 0.02),
        'ffn_w_down': nrm((DEPTH, D_FF, D), D_FF ** -0.5),
    }

def reference(x, norm_mix, norm_ffn, norm_final, ab_w_in, ab_conv_w, ab_conv_b, ab_dt_bias, ab_a_log,
              ab_d_skip, ab_ssd_norm, ab_w_out, cd_w_in, cd_conv_w, cd_conv_b, cd_w_a, cd_b_a, cd_w_i,
              cd_b_i, cd_lambda, cd_log_dt, cd_a_re, cd_a_im, cd_b_re, cd_b_im, cd_c_re, cd_c_im,
              cd_d_skip, cd_w_glu, cd_b_glu, cd_w_out, ffn_w_up, ffn_conv_w, ffn_conv_b, ffn_w_down):
    h = x
    for layer in range(DEPTH):
        y = rmsnorm(h, norm_mix[layer])
        j = layer // 2
        if layer % 2 == 0:
            mix = attn_ssd_layer(y, ab_w_in[j], ab_conv_w[j], ab_conv_b[j], ab_dt_bias[j], ab_a_log[j],
                                 ab_d_skip[j], ab_ssd_norm[j], ab_w_out[j])
        else:
            mix = lru_s5_layer(y, cd_w_in[j], cd_conv_w[j], cd_conv_b[j], cd_w_a[j], cd_b_a[j], cd_w_i[j],
                               cd_b_i[j], cd_lambda[j], cd_log_dt[j], cd_a_re[j], cd_a_im[j], cd_b_re[j],
                               cd_b_im[j], cd_c_re[j], cd_c_im[j], cd_d_skip[j], cd_w_glu[j], cd_b_glu[j],
                               cd_w_out[j])
        h = h + mix
        h = h + conv_ffn(rmsnorm(h, norm_ffn[layer]), ffn_w_up[layer], ffn_conv_w[layer],
                         ffn_conv_b[layer], ffn_w_down[layer])
    return rmsnorm(h, norm_final)


_drawn_inputs = setup_inputs


def setup_inputs(seed=0):
    import zlib

    import numpy as np

    out = dict(_drawn_inputs(seed))
    spreads = {}
    factors = {'norm_ffn': 3.386,
     'norm_final': 7.57,
     'ab_ssd_norm': 3.594,
     'cd_conv_b': 15.779,
     'cd_b_a': 55.246,
     'cd_b_i': 32.689,
     'cd_log_dt': 43.336,
     'cd_a_re': 64.0,
     'cd_a_im': 41.536,
     'cd_b_re': 59.12,
     'cd_b_im': 59.104,
     'cd_c_re': 58.16,
     'cd_c_im': 58.104,
     'cd_b_glu': 64.0,
     'ffn_conv_b': 4.957,
     'cd_w_a': 5.05,
     'cd_w_i': 3.3,
     'cd_lambda': 2.995,
     'cd_d_skip': 2.801,
     'cd_w_glu': 8.0}
    for name, (base, spread) in spreads.items():
        noise = np.random.default_rng([zlib.crc32(name.encode()), seed]).standard_normal(out[name].shape)
        drawn = base * np.exp(spread * noise) if base else spread * noise
        out[name] = __import__('jax').numpy.asarray(drawn.astype(out[name].dtype))
    for name, factor in factors.items():
        out[name] = (out[name] * factor).astype(out[name].dtype)
    return out
```

```python
from contextlib import ExitStack

import concourse.bass as bass
from concourse import mybir

ALU = mybir.AluOpType
ACT = mybir.ActivationFunctionType
F32 = mybir.dt.float32
F32R = mybir.dt.float32r

P = 128
TOK = 256
TT = TOK // P
D = 2048
KT = D // P
COLS = 512
FT = COLS // P
HK = 2
RING = 4
EPS = 1e-6

SB_HEADS, SB_DH = 4, 128
SSD_HEADS, SSD_P, SSD_GROUPS, SSD_N, SSD_CONV = 24, 64, 4, 128, 4
SSD_W = SSD_HEADS * SSD_P
XT = SSD_W // P
RH = SSD_HEADS // SSD_GROUPS
LRU_W, LRU_CONV, LRU_C = 1536, 4, 8.0
LT = LRU_W // P
S5_G, S5_CH, S5_N = 32, 16, 64
S5_W = S5_G * S5_CH
ST = S5_G * S5_N // P
UT = S5_W // P
DFF, FFN_CONV = 4096, 3
HT = DFF // P

PARAM_ROWS = [
    ("norm_mix", 2 * KT), ("norm_ffn", 2 * KT), ("ab_ssd_norm", XT),
    ("ab_conv_b", 20), ("ab_conv_w", SSD_CONV * 20),
    ("cd_conv_w", LRU_CONV * LT), ("cd_conv_b", LT), ("cd_b_a", LT), ("cd_b_i", LT),
    ("cd_lambda", LT), ("cd_d_skip", UT), ("cd_b_glu", UT),
    ("ffn_conv_w", 2 * FFN_CONV * HT), ("ffn_conv_b", 2 * HT),
    ("cd_a_re", ST), ("cd_a_im", ST),
]
COL = {}
_at = 0
for _name, _n in PARAM_ROWS:
    COL[_name] = _at
    _at += _n
NPARAM = _at
PT = -(-NPARAM // P)


def param_pieces():
    for name, n in PARAM_ROWS:
        done = 0
        while done < n:
            at = COL[name] + done
            m = min(n - done, P - at % P)
            yield name, done, at // P, at % P, m
            done += m


AB_GROUPS = [("x", 3072), ("x", 3584), ("x", 4096), ("x", 4608), ("x", 5120), ("dt", 5632),
             ("q", 0), ("k", 512), ("v", 1024), ("z", 1536), ("z", 2048), ("z", 2560)]
CD_GROUPS = [("u", 3072), ("x", 1536), ("x", 2048), ("x", 2560), ("g", 0), ("g", 512), ("g", 1024)]
PER_GROUP = KT // HK
DT_UNITS = 2
CHUNKS = D // COLS

AB_UNITS = sum(DT_UNITS if k == "dt" else PER_GROUP for k, _ in AB_GROUPS)
CD_UNITS = PER_GROUP * len(CD_GROUPS)
OUT_UNITS = CHUNKS * PER_GROUP
UP_ITERS = DFF // COLS
UP_UNITS = UP_ITERS * 2 * PER_GROUP
DOWN_PER = HT // HK
DOWN_UNITS = CHUNKS * DOWN_PER

U_AB = 0
U_OUT0 = U_AB + AB_UNITS
U_UP0 = U_OUT0 + OUT_UNITS
U_DOWN0 = U_UP0 + UP_UNITS
U_CD = U_DOWN0 + DOWN_UNITS
U_OUT1 = U_CD + CD_UNITS
U_UP1 = U_OUT1 + OUT_UNITS
U_DOWN1 = U_UP1 + UP_UNITS
U_END = U_DOWN1 + DOWN_UNITS

AB_ACCS = sum({"dt": 1, "v": TT}.get(k, FT) for k, _ in AB_GROUPS)
CD_ACCS = FT * len(CD_GROUPS)
OUT_ACCS = CHUNKS * TT
UP_ACCS = UP_ITERS * 2 * FT
A_AB = 0
A_OUT0 = A_AB + AB_ACCS
A_UP0 = A_OUT0 + OUT_ACCS
A_DOWN0 = A_UP0 + UP_ACCS
A_CD = A_DOWN0 + OUT_ACCS
A_OUT1 = A_CD + CD_ACCS
A_UP1 = A_OUT1 + OUT_ACCS
A_DOWN1 = A_UP1 + UP_ACCS
A_END = A_DOWN1 + OUT_ACCS
D_OF = {"dt": 0, "v": TT - 1}
D_AB = 0
D_OUT0 = D_AB + sum(D_OF.get(k, FT - 1) for k, _ in AB_GROUPS)
D_DOWN0 = D_OUT0 + CHUNKS
D_CD = D_DOWN0 + CHUNKS
D_OUT1 = D_CD + (FT - 1) * len(CD_GROUPS)
D_DOWN1 = D_OUT1 + CHUNKS
A_NORM = [0, A_UP0, A_CD, A_UP1, A_END]
H_AB = 0
H_UP0 = H_AB + AB_ACCS - TT
H_CD = H_UP0 + 2 * UP_ITERS
H_UP1 = H_CD + CD_ACCS
GELU_C = 0.7978845608028654
GELU_K = 0.044715
TWO_PI = (6.28125, 0.0019350051879882812, 3.01991598196e-07)
ROUND = 12582912.0


def trunk(nc, t, out):
    def at(name, shape, dtype, offset):
        return nc.alloc_sbuf_tensor_at(name, shape, dtype, offset=offset)

    KB = 1024
    base = 16512
    raw = at("raw", [P, RING, HK * COLS], F32, base)
    w_hi = at("w_hi", [P, RING, HK * COLS], F32R, base + 16 * KB)
    w_lo = at("w_lo", [P, RING, HK * COLS], F32R, base + 32 * KB)
    res = at("res", [P, TT, D], F32, base + 48 * KB)
    y = at("y", [P, KT, 2, TOK], F32R, base + 64 * KB)
    hff = at("hff", [P, HT, 2, TOK], F32R, base + 96 * KB)
    cat = hff
    mix2 = base + 128 * KB
    xn = at("xn", [P, TT, D], F32, mix2)
    c0 = base + 160 * KB
    params = at("params", [P, NPARAM], F32, c0)
    ident = at("ident", [P, P], F32, c0 + 2304)
    ones = at("ones", [P, P], F32, c0 + 2304 + 512)
    neg_ones = at("neg_ones", [P, P], F32, c0 + 2304 + 1024)
    neg_tri = at("neg_tri", [P, P], F32, c0 + 2304 + 1536)
    s5p = at("s5p", [P, 26, ST], F32, c0 + 4352)
    tiny = at("tiny", [P, 64], F32, c0 + 6016)
    c1 = c0 + 6272
    dt_t = at("dt_t", [P, TT, SSD_HEADS], F32, c1)
    cs_t = at("cs_t", [P, TT, SSD_HEADS], F32, c1 + 192)
    neg = at("neg", [P, 52], F32, c1 + 384)
    neg_ba, neg_bi, c8 = neg[:, 0:12], neg[:, 12:24], neg[:, 24:36]
    parity, strips = neg[:, 40:42], neg[:, 42:50]
    mix1 = c1 + 608

    prow = at("prow", [P, PT, P], F32, mix1)
    xbc = at("xbc", [P, 20, TOK], F32, mix1)
    qk = at("qk", [P, 2 * SB_HEADS, TOK], F32, mix1 + 20 * KB)
    v_t = at("v_t", [P, TT, SB_HEADS * SB_DH], F32, mix1 + 28 * KB)
    tmp = at("tmp", [P, FT, TOK], F32, mix1 + 32 * KB)
    cv = at("cv", [P, FT, TOK], F32, mix1 + 36 * KB)
    zg = at("zg", [P, XT, TOK], F32, mix2)
    xdt = at("xdt", [P, TT, SSD_W], F32, mix2 + 12 * KB)
    blk = [at(f"blk{n}", [P, 3, P], F32, mix2 + 24 * KB + 1536 * n) for n in range(4)]
    dts = at("dts", [SSD_HEADS, TOK], F32, mix2 + 30 * KB)
    cs = at("cs", [SSD_HEADS, TOK], F32, mix2 + 31 * KB)
    ffn_g = at("ffn_g", [P, FT, TOK], F32, mix1)
    ffn_tv = at("ffn_tv", [P, FT, TOK], F32, mix1 + 4 * KB)
    ffn_v = at("ffn_v", [P, FT, TOK], F32, mix1 + 8 * KB)
    hs = at("hs", [P, LT, TOK], F32, mix1)
    ut = at("ut", [P, UT, TOK], F32, mix1 + 12 * KB)
    wai = at("wai", [P, 2, FT, P], F32, mix1 + 16 * KB)
    xin = at("xin", [P, FT, TOK], F32, mix1 + 20 * KB)
    lru_r = at("lru_r", [P, FT, TOK], F32, mix1 + 24 * KB)
    lru_i = at("lru_i", [P, FT, TOK], F32, mix1 + 28 * KB)
    w_glu = at("w_glu", [P, UT, S5_W], F32, mix1 + 24 * KB)
    ph = at("ph", [P, FT, 2, TOK], F32, mix2)
    pt = at("pt", [P, 2, FT, 2, P], F32, mix2 + 8 * KB)
    rot = at("rot", [P, 2, 2, TOK], F32, mix2 + 8 * KB)
    bq = at("bq", [P, 2, 2, TOK], F32, mix2 + 16 * KB)
    gs = at("gs", [P, 2, TOK], F32, mix2 + 20 * KB)
    st = at("st", [P, 2, TOK], F32, mix2 + 22 * KB)
    bb = at("bb", [P, 2, UT, P], F32, mix2 + 24 * KB)
    cc = at("cc", [P, 2, UT, P], F32, mix2 + 28 * KB)
    b_raw = at("b_raw", [P, 2, ST, S5_CH], F32, mix1 + 20 * KB)
    b_pad = at("b_pad", [P, 2, ST, 2, S5_CH], F32, mix1 + 22 * KB)
    c_pad = at("c_pad", [P, 2, UT, 2, S5_N], F32, mix1 + 26 * KB)
    b_tmp = at("b_tmp", [P, 2, ST, S5_CH], F32, mix1 + 30 * KB)
    g_fin = at("g_fin", [P, D], F32, mix1)

    with ExitStack() as ctx:
        ps = ctx.enter_context(nc.psum_tensor("ps", [P, 8, COLS], F32))

        def sem(name):
            return ctx.enter_context(nc.semaphore(name))

        raw_loaded = [sem(f"raw_loaded{n}") for n in range(RING)]
        hi_ready, lo_ready, unit_used = sem("hi_ready"), sem("lo_ready"), sem("unit_used")
        acc_done, acc_free, half_copied = sem("acc_done"), sem("acc_free"), sem("half_copied")
        x_loaded, rows_loaded, small_loaded = sem("x_loaded"), sem("rows_loaded"), sem("small_loaded")
        consts_ready, rows_turned, params_ready = sem("consts_ready"), sem("rows_turned"), sem("params_ready")
        v_chain, a_chain, g_chain = sem("v_chain"), sem("a_chain"), sem("g_chain")
        ssq_ready, ms_ready, sd_ready = sem("ssq_ready"), sem("ms_ready"), sem("sd_ready")
        rstd_ready, xn_ready, turned = sem("rstd_ready"), sem("xn_ready"), sem("turned")
        y_hi_ready, y_lo_ready = sem("y_hi_ready"), sem("y_lo_ready")
        ffn_conv, ffn_act, ffn_h, ffn_hi, ffn_lo = (
            sem("ffn_conv"), sem("ffn_act"), sem("ffn_h"), sem("ffn_hi"), sem("ffn_lo"))
        xconv, xact, z_act = sem("xconv"), sem("xact"), sem("z_act")
        dt_abs, dt_exp, dt_w, dt_ln, dt_a, cs_ready = (
            sem("dt_abs"), sem("dt_exp"), sem("dt_w"), sem("dt_ln"), sem("dt_a"), sem("cs_ready"))
        cs_turned, cs_t_ready, x_turned, xdt_ready = (
            sem("cs_turned"), sem("cs_t_ready"), sem("x_turned"), sem("xdt_ready"))
        cb_done, cb_free, cs_spread, decay_ready, decay_cut, m_ready, yh_done, ys_ready = (
            sem("cb_done"), sem("cb_free"), sem("cs_spread"), sem("decay_ready"), sem("decay_cut"),
            sem("m_ready"), sem("yh_done"), sem("ys_ready"))
        gated, sq_ready, sq_summed, gn_ms, gn_sd, gn_rstd = (
            sem("gated"), sem("sq_ready"), sem("sq_summed"), sem("gn_ms"), sem("gn_sd"), sem("gn_rstd"))
        o_ready, o_hi, o_lo = sem("o_ready"), sem("o_hi"), sem("o_lo")
        zs_done, z_ln, sp_ready, sp_cut, zs_full, w_exp, w_cut, att_done = (
            sem("zs_done"), sem("z_ln"), sem("sp_ready"), sem("sp_cut"),
            sem("zs_full"), sem("w_exp"), sem("w_cut"), sem("att_done"))
        att_hi, att_lo = sem("att_hi"), sem("att_lo")
        wai_loaded, bc_loaded, glu_loaded = sem("wai_loaded"), sem("bc_loaded"), sem("glu_loaded")
        s5v, s5a, s5g, s5_pads, s5_turned, s5_mats = (
            sem("s5v"), sem("s5a"), sem("s5g"), sem("s5_pads"), sem("s5_turned"), sem("s5_mats"))
        phases_ready, bu_done, bu_free, scanned, st_ready, y5_done, y5_ready = (
            sem("phases_ready"), sem("bu_done"), sem("bu_free"), sem("scanned"), sem("st_ready"),
            sem("y5_done"), sem("y5_ready"))
        gelu_e, gelu_u, glu_in, glu_done, glu_act, glu_out = (
            sem("gelu_e"), sem("gelu_u"), sem("glu_in"), sem("glu_done"), sem("glu_act"), sem("glu_out"))
        xc_ready, gates_done, gates_exp, r_ready, lru_th, lru_q, lru_sd, hs_ready = (
            sem("xc_ready"), sem("gates_done"), sem("gates_exp"), sem("r_ready"),
            sem("lru_th"), sem("lru_q"), sem("lru_sd"), sem("hs_ready"))
        gfin_loaded, out_ready, stored = sem("gfin_loaded"), sem("out_ready"), sem("stored")

        def s5(n):
            return s5p[:, n, :]
        (LOGDT, DTV, LR, XDT, TH, MAG, THETA, TURN, SINH, SIN2, SIN, COS, E1, AM1, ABI, DEN, FR, FI,
         T0, T1, T2, T3) = range(22)

        def by_rows(w):
            return w.rearrange("(kt p) n -> p kt n", p=P)

        w_ab, w_cd = by_rows(t["ab_w_in"][0]), by_rows(t["cd_w_in"][0])
        w_out = [by_rows(t["ab_w_out"][0]), by_rows(t["cd_w_out"][0])]
        w_up = [by_rows(t["ffn_w_up"][n]) for n in range(2)]
        w_down = [by_rows(t["ffn_w_down"][n]) for n in range(2)]

        def plus(n, it, per):
            return n if it is None else it * per + n

        def flat(b):
            return b[:, :, :].rearrange("p a b -> p (a b)")

        def pcol(name, n):
            return params[:, COL[name] + n:COL[name] + n + 1]

        block = ctx.enter_context(nc.Block())

        @block.sync
        def _(sp):
            def load(u, src, it=None, per=0):
                if u >= RING:
                    sp.wait_ge(lo_ready, plus(u - RING + 1, it, per))
                    if it is not None:
                        sp.nop(nofuse=True)
                sp.dma_start(raw[:, u % RING, :].rearrange("p (k n) -> p k n", k=HK),
                             src).then_inc(raw_loaded[u % RING], 16)

            def in_proj(u, w, groups):
                for kind, col in groups:
                    if kind == "dt":
                        for k in range(DT_UNITS):
                            sp.wait_ge(lo_ready, u - RING + 1)
                            sp.dma_start(raw[:, u % RING, :].rearrange("p (k n) -> p k n", n=P)[:, :, 0:SSD_HEADS],
                                         w[:, k * KT // 2:(k + 1) * KT // 2, col:col + SSD_HEADS]
                                         ).then_inc(raw_loaded[u % RING], 16)
                            u += 1
                        continue
                    for k in range(PER_GROUP):
                        load(u, w[:, HK * k:HK * k + HK, col:col + COLS])
                        u += 1

            def out_proj(u, w, per):
                with sp.Fori(0, CHUNKS) as i:
                    for k in range(per):
                        load(u + k, w[:, HK * k:HK * k + HK, bass.ds(i * COLS, COLS)], i, per)

            def up_proj(u, w):
                with sp.Fori(0, UP_ITERS) as i:
                    for part in range(2):
                        for k in range(PER_GROUP):
                            load(u + part * PER_GROUP + k,
                                 w[:, HK * k:HK * k + HK, bass.ds(i * COLS + (1 - part) * DFF, COLS)],
                                 i, 2 * PER_GROUP)

            x_rows = t["x"][0].rearrange("(tt p) d -> p tt d", p=P)
            for tt in range(TT):
                sp.dma_start(res[:, tt, :], x_rows[:, tt, :]).then_inc(x_loaded, 16)
            in_proj(U_AB, w_ab, AB_GROUPS)
            out_proj(U_OUT0, w_out[0], PER_GROUP)
            up_proj(U_UP0, w_up[0])
            out_proj(U_DOWN0, w_down[0], DOWN_PER)
            in_proj(U_CD, w_cd, CD_GROUPS)
            out_proj(U_OUT1, w_out[1], PER_GROUP)
            up_proj(U_UP1, w_up[1])
            out_proj(U_DOWN1, w_down[1], DOWN_PER)

        @block.tensor
        def _(pe):
            def unit(u, it=None, per=0):
                pe.wait_ge(lo_ready, plus(u + 1, it, per))

            def half(parts, u):
                return parts[:, u % RING, :].rearrange("p (k n) -> p k n", k=HK)

            def fm_unit(u, k, a, bank0, free_lag, it=None, per=0, aper=0):
                unit(u, it, per)
                for f in range(FT):
                    if k == 0:
                        pe.wait_ge(acc_free, plus(a + f + 1 - free_lag, it, aper)) if a + f + 1 > free_lag else None
                    for kk in range(HK):
                        kt = HK * k + kk
                        cols = slice(f * P, f * P + P)
                        pe.matmul(ps[:, bank0 + f, :], half(w_hi, u)[:, kk, cols],
                                  y[:, kt, :, :].rearrange("p a b -> p (a b)"),
                                  start=kt == 0, stop=False)
                        mm = pe.matmul(ps[:, bank0 + f, 0:TOK], half(w_lo, u)[:, kk, cols], y[:, kt, 0, :],
                                       start=False, stop=kt == KT - 1)
                mm.then_inc(unit_used, 1)

            def tm_unit(u, k, per_acc, lhs, banks, it=None, per=0):
                unit(u, it, per)
                for tt in range(TT):
                    for kk in range(HK):
                        kt = HK * k + kk
                        hi = lhs[:, kt, 0, tt * P:tt * P + P]
                        lo = lhs[:, kt, 1, tt * P:tt * P + P]
                        pe.matmul(banks(tt), hi, half(w_hi, u)[:, kk, :], start=kt == 0, stop=False)
                        pe.matmul(banks(tt), hi, half(w_lo, u)[:, kk, :], start=False, stop=False)
                        mm = pe.matmul(banks(tt), lo, half(w_hi, u)[:, kk, :], start=False,
                                       stop=kt == HK * per_acc - 1)
                    if k == per_acc - 1 and tt < TT - 1:
                        mm.then_inc(acc_done, 1)
                mm.then_inc(unit_used, 1)

            def dt_units(u, a):
                for k in range(DT_UNITS):
                    unit(u + k)
                    if k == 0:
                        pe.wait_ge(acc_free, a - FT + 1)
                    for kk in range(KT // 2):
                        kt = k * KT // 2 + kk
                        w = [parts[:, (u + k) % RING, kk * P:kk * P + P] for parts in (w_hi, w_lo)]
                        pe.matmul(ps[:, a % FT, :], w[0], y[:, kt, :, :].rearrange("p a b -> p (a b)"),
                                  start=kt == 0, stop=False)
                        mm = pe.matmul(ps[:, a % FT, 0:TOK], w[1], y[:, kt, 0, :], start=False, stop=kt == KT - 1)
                    mm.then_inc(unit_used, 1)

            def out_proj(u, a, per, lhs):
                pe.wait_ge(acc_free, a)
                with pe.Fori(0, CHUNKS) as i:
                    def banks(tt):
                        return ps[:, bass.ds(i * TT + tt, 1), :]
                    for k in range(per):
                        tm_unit(u + k, k, per, lhs, banks, i, per)

            def up_proj(u, a):
                pe.wait_ge(acc_free, a)
                with pe.Fori(0, UP_ITERS) as i:
                    for part in range(2):
                        for k in range(PER_GROUP):
                            fm_unit(u + part * PER_GROUP + k, k, a + part * FT, part * FT, 2 * FT,
                                    i, 2 * PER_GROUP, 2 * FT)

            def norm(n):
                pe.wait_ge(xn_ready, TT * (n + 1))
                for kt in range(KT):
                    if kt >= 4:
                        pe.wait_ge(y_lo_ready, KT * n + kt - 3)
                    for tt in range(TT):
                        mm = pe.transpose(ps[:, 4 + kt % 4, tt * P:tt * P + P], xn[:, tt, kt * P:kt * P + P], ident[:, :])
                    mm.then_inc(turned, 1)
                pe.wait_ge(y_lo_ready, KT * (n + 1))

            def turn_params():
                pe.wait_ge(consts_ready, 4)
                pe.wait_ge(rows_loaded, 16 * len(list(param_pieces())))
                for n in range(PT):
                    rows = min(P, NPARAM - n * P)
                    mm = pe.transpose(ps[:, n // 4, (n % 4) * P:(n % 4) * P + rows], prow[0:rows, n, :],
                                      ident[0:rows, 0:rows])
                mm.then_inc(rows_turned, 1)
                pe.wait_ge(params_ready, 1)

            def ssd_setup():
                pe.wait_ge(cs_ready, 1)
                for tt in range(TT):
                    pe.transpose(ps[:, 4, tt * 32:tt * 32 + SSD_HEADS], dts[:, tt * P:tt * P + P],
                                 ident[0:SSD_HEADS, 0:SSD_HEADS])
                    mm = pe.transpose(ps[:, 4, 64 + tt * 32:64 + tt * 32 + SSD_HEADS], cs[:, tt * P:tt * P + P],
                                      ident[0:SSD_HEADS, 0:SSD_HEADS])
                mm.then_inc(cs_turned, 1)
                pe.wait_ge(xact, 5)
                for n in range(TT * XT // 4):
                    tt, q = n % TT, n // TT
                    if n >= 2:
                        pe.wait_ge(xdt_ready, n - 1)
                    for j in range(4):
                        mm = pe.transpose(ps[:, 5 + n % 2, j * P:j * P + P],
                                          xbc[:, 4 * q + j, tt * P:tt * P + P], ident[:, :])
                    mm.then_inc(x_turned, 1)

            def ssd_group(g):
                if g == 0:
                    pe.wait_ge(cs_t_ready, 1)
                    pe.wait_ge(xdt_ready, 6)
                else:
                    pe.wait_ge(m_ready, RH * g)
                b, c = xbc[:, XT + g, :], xbc[:, XT + SSD_GROUPS + g, :]
                pe.matmul(ps[:, 4, 0:TOK], b[:, 0:P], c, start=True, stop=True, skip_group_check=True)
                pe.matmul(ps[:, 4, TOK:TOK + P], b[:, P:TOK], c[:, P:TOK], start=False, stop=True,
                          skip_group_check=True).then_inc(cb_done, 1)
                for pair in range(RH // 2):
                    n = g * RH // 2 + pair
                    if n >= 1:
                        pe.wait_ge(decay_ready, 2 * n)
                    for j in range(2):
                        h = 2 * n + j
                        mm = pe.matmul(ps[:, 5, j * TOK:j * TOK + TOK],
                                       ident[0:SSD_HEADS, h:h + 1].broadcast_to([SSD_HEADS, P]), cs[:, :],
                                       start=j == 0, stop=True, skip_group_check=True)
                    mm.then_inc(cs_spread, 1)
                    if n >= 2:
                        pe.wait_ge(ys_ready, n - 1)
                    for j in range(2):
                        h = 2 * n + j
                        pe.wait_ge(m_ready, h + 1)
                        o = ps[j * SSD_P:(j + 1) * SSD_P, 6 + n % 2, 0:TOK]
                        pe.matmul(o, xdt[:, 0, h * SSD_P:(h + 1) * SSD_P], blk[h % 2][:, 0:2, :].rearrange("p a b -> p (a b)"),
                                  start=True, stop=False)
                        mm = pe.matmul(o[:, P:TOK], xdt[:, 1, h * SSD_P:(h + 1) * SSD_P], blk[h % 2][:, 2, :],
                                       start=False, stop=True)
                    mm.then_inc(yh_done, 1)

            def ssd_norm():
                for n in range(XT):
                    pe.wait_ge(sq_ready, n + 1)
                    mm = pe.matmul(ps[:, 4, 0:TOK], ones[:, :], tmp[:, n % FT, :], start=n == 0, stop=n == XT - 1)
                    mm.then_inc(sq_summed, 1)

            def attention():
                pe.wait_ge(acc_free, A_OUT0)
                pe.wait_ge(gn_ms, 1)
                for h in range(SB_HEADS):
                    q, k = qk[:, h, :], qk[:, SB_HEADS + h, :]
                    zb = 4 + h % 2
                    if h >= 2:
                        pe.wait_ge(w_exp, h - 1)
                    pe.matmul(ps[:, zb, 0:TOK], k[:, 0:P], q, start=True, stop=False, skip_group_check=True)
                    pe.matmul(ps[:, zb, TOK:TOK + P], k[:, P:TOK], q[:, P:TOK], start=False, stop=False,
                              skip_group_check=True).then_inc(zs_done, 1)
                    pe.wait_ge(sp_cut, h + 1)
                    pe.matmul(ps[:, zb, 0:TOK], neg_tri[:, :], blk[2][:, 0:2, :].rearrange("p a b -> p (a b)"),
                              start=False, stop=False, skip_group_check=True)
                    pe.matmul(ps[:, zb, P:TOK], neg_ones[:, :], blk[2][:, 2, :], start=False, stop=False,
                              skip_group_check=True)
                    pe.matmul(ps[:, zb, TOK:TOK + P], neg_tri[:, :], blk[2][:, 2, :], start=False, stop=True,
                              skip_group_check=True).then_inc(zs_full, 1)
                    pe.wait_ge(w_cut, h + 1)
                    if h >= 2:
                        pe.wait_ge(att_lo, h - 1)
                    o = ps[:, 6 + h % 2, 0:TOK]
                    pe.matmul(o, v_t[:, 0, h * SB_DH:(h + 1) * SB_DH], blk[3][:, 0:2, :].rearrange("p a b -> p (a b)"),
                              start=True, stop=False)
                    pe.matmul(o[:, P:TOK], v_t[:, 1, h * SB_DH:(h + 1) * SB_DH], blk[3][:, 2, :],
                              start=False, stop=True).then_inc(att_done, 1)

            def mix0():
                u, a = U_AB, A_AB
                for kind, _ in AB_GROUPS:
                    if kind == "dt":
                        dt_units(u, a)
                        u, a = u + DT_UNITS, a + 1
                    elif kind == "v":
                        pe.wait_ge(acc_free, a - 2)
                        for k in range(PER_GROUP):
                            tm_unit(u + k, k, PER_GROUP, y, lambda tt: ps[:, (a + tt) % FT, :])
                        u, a = u + PER_GROUP, a + TT
                    else:
                        bank = [(a + f) % FT for f in range(FT)]
                        for k in range(PER_GROUP):
                            fm_rot(u + k, k, a, bank)
                        u, a = u + PER_GROUP, a + FT
                ssd_setup()
                for g in range(SSD_GROUPS):
                    ssd_group(g)
                ssd_norm()
                attention()

            def fm_rot(u, k, a, bank):
                unit(u)
                for f in range(FT):
                    if k == 0 and a + f + 1 > FT:
                        pe.wait_ge(acc_free, a + f + 1 - FT)
                    for kk in range(HK):
                        kt = HK * k + kk
                        cols = slice(f * P, f * P + P)
                        pe.matmul(ps[:, bank[f], :], half(w_hi, u)[:, kk, cols],
                                  y[:, kt, :, :].rearrange("p a b -> p (a b)"), start=kt == 0, stop=False)
                        mm = pe.matmul(ps[:, bank[f], 0:TOK], half(w_lo, u)[:, kk, cols], y[:, kt, 0, :],
                                       start=False, stop=kt == KT - 1)
                    if k == PER_GROUP - 1 and f < FT - 1:
                        mm.then_inc(acc_done, 1)
                mm.then_inc(unit_used, 1)

            def s5_turn():
                pe.wait_ge(s5_pads, 2)
                for ri in range(2):
                    for q in range(UT):
                        mm = pe.transpose(ps[:, 4 + ri, q * P:q * P + P],
                                          b_pad[:, ri, 4 * q:4 * q + 4, :, :].rearrange("p a b c -> p (a b c)"),
                                          ident[:, :])
                for ri in range(2):
                    for q in range(UT):
                        mm = pe.transpose(ps[:, 6 + ri, q * P:q * P + P],
                                          c_pad[:, ri, q, :, :].rearrange("p a b -> p (a b)"), ident[:, :])
                mm.then_inc(s5_turned, 1)

            def gates(g):
                pe.wait_ge(wai_loaded, 32 * (g + 1))
                pe.wait_ge(xc_ready, g + 1)
                for f in range(FT):
                    pe.matmul(ps[:, 4 + f, 0:TOK], wai[:, 0, f, :], cv[:, f, :], start=True, stop=True,
                              skip_group_check=True)
                    pe.matmul(ps[:, 4 + f, TOK:2 * TOK], wai[:, 1, f, :], cv[:, f, :], start=False, stop=True,
                              skip_group_check=True).then_inc(gates_done, 1)

            def s5_states():
                pe.wait_ge(s5_mats, 2)
                pe.wait_ge(acc_free, A_CD + FT)
                for j in range(ST):
                    q, jj = j // 4, j % 4
                    rows = slice(32 * jj, 32 * jj + 32)
                    if j >= 2:
                        pe.wait_ge(bu_free, j - 1)
                    for ri in range(2):
                        mm = pe.matmul(ps[:, 4 + j % 2, ri * TOK:ri * TOK + TOK], bb[rows, ri, q, :], ut[rows, q, :],
                                       start=ri == 0, stop=True, skip_group_check=True)
                    mm.then_inc(bu_done, 1)
                    if j >= 1:
                        s5_out(j - 1)
                s5_out(ST - 1)

            def s5_out(j):
                q, jj = j // 4, j % 4
                rows = slice(32 * jj, 32 * jj + 32)
                pe.wait_ge(st_ready, j + 1)
                if q >= 2 and jj == 0:
                    pe.wait_ge(y5_ready, q - 1)
                for ri in range(2):
                    mm = pe.matmul(ps[rows, 6 + q % 2, 0:TOK], cc[:, ri, q, rows], st[:, ri, :],
                                   start=ri == 0, stop=ri == 1)
                mm.then_inc(y5_done, 1)

            def glu():
                pe.wait_ge(glu_in, 1)
                pe.wait_ge(glu_loaded, 16)
                for f in range(UT):
                    for k in range(UT):
                        mm = pe.matmul(ps[:, 4 + f, 0:TOK], w_glu[:, k, f * P:f * P + P], ut[:, k, :],
                                       start=k == 0, stop=k == UT - 1)
                    mm.then_inc(glu_done, 1)

            def mix1_():
                u, a = U_CD, A_CD
                pe.wait_ge(acc_free, a)
                s5_turn()
                x_groups = 0
                for kind, _ in CD_GROUPS:
                    bank = [(a + f) % FT for f in range(FT)]
                    for k in range(PER_GROUP):
                        fm_rot(u + k, k, a, bank)
                    u, a = u + PER_GROUP, a + FT
                    if kind == "x":
                        gates(x_groups)
                        x_groups += 1
                s5_states()
                glu()

            turn_params()
            norm(0)
            mix0()
            pe.wait_ge(o_lo, XT)
            pe.wait_ge(att_lo, SB_HEADS)
            out_proj(U_OUT0, A_OUT0, PER_GROUP, cat)
            norm(1)
            up_proj(U_UP0, A_UP0)
            pe.wait_ge(ffn_lo, UP_ITERS)
            out_proj(U_DOWN0, A_DOWN0, DOWN_PER, hff)
            norm(2)
            mix1_()
            pe.wait_ge(o_lo, 2 * XT + UT)
            out_proj(U_OUT1, A_OUT1, PER_GROUP, cat)
            norm(3)
            up_proj(U_UP1, A_UP1)
            pe.wait_ge(ffn_lo, 2 * UP_ITERS)
            out_proj(U_DOWN1, A_DOWN1, DOWN_PER, hff)

        @block.scalar
        def _(act):
            chain = [0]

            def link(ins):
                chain[0] += 1
                ins.then_inc(a_chain, 1)
                act.wait_ge(a_chain, chain[0])

            def split(u, it=None, per=0):
                if u >= U_END and it is None:
                    return
                act.wait_ge(raw_loaded[u % RING], plus(16 * (u // RING + 1), it, 16 * per // RING))
                if u >= RING:
                    act.wait_ge(unit_used, plus(u - RING + 1, it, per))
                act.activation(w_hi[:, u % RING, :], raw[:, u % RING, :], ACT.Copy).then_inc(hi_ready, 1)

            def out_proj(u, per, last=False):
                n = CHUNKS - 1 if last else CHUNKS
                with act.Fori(0, n) as i:
                    for k in range(per):
                        split(u + k + RING, i, per)
                if last:
                    for k in range(per - RING):
                        split(u + n * per + k + RING)

            def up_proj(u, a, layer):
                done = UP_ITERS * layer
                with act.Fori(0, UP_ITERS) as i:
                    for k in range(PER_GROUP - 1):
                        split(u + k + RING, i, 2 * PER_GROUP)
                    act.wait_ge(unit_used, i * 2 * PER_GROUP + (u + PER_GROUP))
                    act.activation(tmp[:, :, :], ps[:, 0:FT, TOK:2 * TOK], ACT.Copy).then_inc(half_copied, 1)
                    split(u + PER_GROUP - 1 + RING, i, 2 * PER_GROUP)
                    act.wait_ge(ffn_conv, i + (done + 1))
                    act.activation(cv[:, :, :], cv[:, :, :], ACT.Silu).then_inc(ffn_act, 1)
                    for k in range(PER_GROUP, 2 * PER_GROUP - 1):
                        split(u + k + RING, i, 2 * PER_GROUP)
                    act.wait_ge(unit_used, i * 2 * PER_GROUP + (u + 2 * PER_GROUP))
                    act.activation(ffn_tv[:, :, :], ps[:, FT:2 * FT, TOK:2 * TOK], ACT.Copy).then_inc(half_copied, 1)
                    split(u + 2 * PER_GROUP - 1 + RING, i, 2 * PER_GROUP)
                    act.wait_ge(ffn_h, i + (done + 1))
                    act.activation(hff[:, bass.ds(i * FT, FT), 0, :], ffn_v[:, :, :], ACT.Copy).then_inc(ffn_hi, 1)

            def norm(n):
                if n == 0:
                    act.wait_ge(x_loaded, 32)
                else:
                    act.wait_ge(acc_free, A_NORM[n])
                act.activation(xn[:, 0, :], res[:, 0, :], ACT.Square, accum_out=tiny[:, 0:1]).then_inc(ssq_ready, 1)
                act.wait_ge(ms_ready, n + 1)
                act.activation(tiny[:, 4:6], tiny[:, 2:4], ACT.Sqrt).then_inc(sd_ready, 1)
                act.wait_ge(rstd_ready, n + 1)
                act.activation(xn[:, 0, :], res[:, 0, :], ACT.Copy, scale=tiny[:, 6:7]).then_inc(xn_ready, 1)
                if n == 4:
                    return
                if n == 0:
                    act.wait_ge(params_ready, 1)
                name = ("norm_mix", "norm_ffn")[n % 2]
                for kt in range(KT):
                    act.wait_ge(turned, KT * n + kt + 1)
                    act.activation(y[:, kt, 0, :], ps[:, 4 + kt % 4, 0:TOK], ACT.Copy,
                                   scale=pcol(name, KT * (n // 2) + kt)).then_inc(y_hi_ready, 1)

            def param_loads():
                for name, r, tile, p, m in param_pieces():
                    src = t[name]
                    dims = " ".join("abc"[:len(src.shape)])
                    flat = src.rearrange(f"{dims} -> ({dims})").rearrange("(r p) -> r p", p=P)
                    act.dma_start(prow[p:p + m, tile, :], flat[r:r + m, :]).then_inc(rows_loaded, 16)
                act.dma_start(tiny[0:SSD_HEADS, 16:17], t["ab_dt_bias"].rearrange("a h -> h a")).then_inc(small_loaded, 16)
                act.dma_start(tiny[0:SSD_HEADS, 17:18], t["ab_a_log"].rearrange("a h -> h a")).then_inc(small_loaded, 16)
                heads = t["ab_d_skip"].rearrange("a (t j) -> a j t", j=2)
                steps = t["cd_log_dt"].rearrange("a (t j) -> a j t", j=2)
                with nc.allow_non_contiguous_dma(reason="two small vectors, once"):
                    for j in range(2):
                        act.dma_start(tiny[j * 64:j * 64 + 64, 20:20 + XT],
                                      heads[0, j:j + 1, :].broadcast_to([64, XT])).then_inc(small_loaded, 16)
                        act.dma_start(s5p[j * 64:j * 64 + 64, LOGDT, :],
                                      steps[0, j:j + 1, :].broadcast_to([64, ST])).then_inc(small_loaded, 16)

            def conv_silu(g):
                act.wait_ge(xconv, g + 1)
                act.activation(xbc[:, FT * g:FT * g + FT, :], cv[:, :, :], ACT.Silu).then_inc(xact, 1)

            def dt_path():
                act.wait_ge(small_loaded, 96)
                act.activation(tiny[0:SSD_HEADS, 18:19], tiny[0:SSD_HEADS, 17:18], ACT.Exp).then_inc(dt_a, 1)
                act.wait_ge(dt_abs, 1)
                act.activation(cv[0:SSD_HEADS, 1, :], cv[0:SSD_HEADS, 1, :], ACT.Exp, scale=-1.0).then_inc(dt_exp, 1)
                act.wait_ge(dt_w, 1)
                act.activation(cv[0:SSD_HEADS, 3, :], cv[0:SSD_HEADS, 2, :], ACT.Ln).then_inc(dt_ln, 1)

            def decays():
                act.wait_ge(cs_t_ready, 1)
                for h in range(SSD_HEADS):
                    act.wait_ge(cs_spread, h // 2 + 1)
                    if h >= 2:
                        act.wait_ge(m_ready, h - 1)
                    j = h % 2
                    b = flat(blk[2 + j])
                    act.activation(b[:, 0:TOK], ps[:, 5, j * TOK:j * TOK + TOK], ACT.Relu, scale=-1.0,
                                   bias=cs_t[:, 0, h:h + 1])
                    link(act.activation(b[:, TOK:3 * P], ps[:, 5, j * TOK + P:j * TOK + TOK], ACT.Relu, scale=-1.0,
                                        bias=cs_t[:, 1, h:h + 1]))
                    act.activation(b, b, ACT.Exp, scale=-1.0).then_inc(decay_ready, 1)

            def gated_norm():
                act.wait_ge(gn_ms, 1)
                act.activation(cv[:, 0, :], cv[:, 0, :], ACT.Sqrt).then_inc(gn_sd, 1)
                for n in range(XT):
                    act.wait_ge(o_ready, n + 1)
                    act.activation(cat[:, SB_HEADS + n, 0, :], tmp[:, n % FT, :], ACT.Copy).then_inc(o_hi, 1)

            def attention():
                for h in range(SB_HEADS):
                    zb = 4 + h % 2
                    act.wait_ge(zs_done, h + 1)
                    if h >= 1:
                        act.wait_ge(sp_ready, h)
                    z = ps[:, zb, 0:3 * P]
                    b = flat(blk[0])
                    link(act.activation(b, z, ACT.Abs))
                    link(act.activation(b, b, ACT.Exp, scale=-1.0))
                    act.activation(b, b, ACT.Ln, bias=1.0).then_inc(z_ln, 1)
                    act.wait_ge(zs_full, h + 1)
                    if h >= 1:
                        act.wait_ge(w_cut, h)
                    act.activation(flat(blk[1]), z, ACT.Exp).then_inc(w_exp, 1)
                    act.wait_ge(att_done, h + 1)
                    act.activation(cat[:, h, 0, :], ps[:, 6 + h % 2, 0:TOK], ACT.Copy).then_inc(att_hi, 1)

            def group(kind, u, a, d):
                per = DT_UNITS if kind == "dt" else PER_GROUP
                for k in range(per):
                    if k == per - 1 and kind != "v":
                        for f in range(1 if kind == "dt" else FT):
                            if kind == "dt" or f == FT - 1:
                                act.wait_ge(unit_used, u + per)
                            else:
                                act.wait_ge(acc_done, d + f + 1)
                            act.activation(tmp[:, (a + f) % FT, :], ps[:, (a + f) % FT, TOK:2 * TOK], ACT.Copy,
                                           scale=SB_DH ** -0.5 if kind == "q" else 1.0).then_inc(half_copied, 1)
                    split(u + k + RING)
                return u + per, a + {"dt": 1, "v": TT}.get(kind, FT), d + D_OF.get(kind, FT - 1)

            def mix0():
                u, a, d = U_AB, A_AB, D_AB
                n_x = n_z = 0
                for kind, _ in AB_GROUPS:
                    u, a, d = group(kind, u, a, d)
                    if kind == "x":
                        conv_silu(n_x)
                        n_x += 1
                    elif kind == "dt":
                        dt_path()
                    elif kind == "z":
                        act.wait_ge(acc_free, a)
                        act.activation(zg[:, FT * n_z:FT * n_z + FT, :],
                                       zg[:, FT * n_z:FT * n_z + FT, :], ACT.Silu).then_inc(z_act, 1)
                        n_z += 1
                decays()
                gated_norm()
                attention()

            def s5_prep():
                act.wait_ge(small_loaded, 96)
                act.activation(s5(DTV), s5(LOGDT), ACT.Exp).then_inc(s5a, 1)
                act.wait_ge(s5v, 1)
                act.activation(s5(TH), s5(XDT), ACT.Tanh, scale=0.5)
                act.activation(s5(MAG), s5(XDT), ACT.Exp)
                act.activation(s5(SINH), s5(TURN), ACT.Sin, scale=0.5)
                act.activation(s5(SIN), s5(TURN), ACT.Sin).then_inc(s5a, 1)
                lam = params[:, COL["cd_lambda"]:COL["cd_lambda"] + LT]
                link(act.activation(tiny[:, 32:44], lam, ACT.Abs))
                act.activation(s5p[:, T0, 0:LT], tiny[:, 32:44], ACT.Exp, scale=-1.0).then_inc(s5a, 1)
                act.wait_ge(s5v, 2)
                act.activation(s5p[:, T1, 0:LT], s5p[:, T2, 0:LT], ACT.Ln).then_inc(s5a, 1)

            def bc_loads():
                for ri, name in enumerate(("cd_b_re", "cd_b_im")):
                    act.dma_start(b_raw[:, ri, :, :], t[name][0].rearrange("(j g) n c -> (g n) j c", g=2)
                                  ).then_inc(bc_loaded, 16)
                for ri, name in enumerate(("cd_c_re", "cd_c_im")):
                    for gl in range(2):
                        act.dma_start(c_pad[:, ri, :, gl, :], t[name][0].rearrange("g c n -> (g c) n").rearrange(
                            "(q p) n -> p q n", p=P)).then_inc(bc_loaded, 16)

            def load_gate_weights(g):
                for m, name in enumerate(("cd_w_a", "cd_w_i")):
                    act.dma_start(wai[:, m, :, :], t[name][0, FT * g:FT * g + FT].rearrange("b i j -> i b j")
                                  ).then_inc(wai_loaded, 16)

            def lru(g):
                for f in range(FT):
                    act.wait_ge(gates_done, FT * g + f + 1)
                    act.activation(lru_r[:, f, :], ps[:, 4 + f, 0:TOK], ACT.Exp, scale=-1.0,
                                   bias=neg_ba[:, FT * g + f:FT * g + f + 1])
                    act.activation(lru_i[:, f, :], ps[:, 4 + f, TOK:2 * TOK], ACT.Exp, scale=-1.0,
                                   bias=neg_bi[:, FT * g + f:FT * g + f + 1]).then_inc(gates_exp, 1)
                if g + 1 < LT // FT:
                    load_gate_weights(g + 1)
                act.wait_ge(r_ready, g + 1)
                for f in range(FT):
                    act.activation(xin[:, f, :], lru_r[:, f, :], ACT.Exp, scale=c8[:, FT * g + f:FT * g + f + 1])
                    ins = act.activation(lru_r[:, f, :], lru_r[:, f, :], ACT.Tanh, scale=c8[:, FT * g + f:FT * g + f + 1])
                ins.then_inc(lru_th, 1)
                act.wait_ge(lru_q, g + 1)
                act.activation(lru_r[:, :, :], lru_r[:, :, :], ACT.Sqrt, scale=-2.0).then_inc(lru_sd, 1)

            def gelu_tanh(n):
                act.wait_ge(gelu_u, n + 1)
                act.activation(cv[:, :, :], cv[:, :, :], ACT.Tanh, scale=GELU_C).then_inc(gelu_e, 1)

            def gate_out(g):
                for f in range(FT):
                    act.wait_ge(o_ready, XT + FT * g + f + 1)
                    act.activation(cat[:, FT * g + f, 0, :], xin[:, f, :], ACT.Copy).then_inc(o_hi, 1)

            def mix1_():
                s5_prep()
                load_gate_weights(0)
                u, a, d = U_CD, A_CD, D_CD
                x_groups = g_groups = 0
                for kind, _ in CD_GROUPS:
                    u, a, d = group(kind, u, a, d)
                    if kind == "x":
                        lru(x_groups)
                        x_groups += 1
                        if x_groups == LT // FT:
                            act.wait_ge(hs_ready, LT)
                            act.dma_start(w_glu[:, :, :], t["cd_w_glu"][0].rearrange("(k p) n -> p k n", p=P)
                                          ).then_inc(glu_loaded, 16)
                    elif kind == "g":
                        gelu_tanh(g_groups)
                        gate_out(g_groups)
                        g_groups += 1
                gelu_tanh(LT // FT)
                for f in range(UT):
                    act.wait_ge(glu_done, f + 1)
                    act.activation(tmp[:, f, :], ps[:, 4 + f, 0:TOK], ACT.Sigmoid,
                                   bias=pcol("cd_b_glu", f)).then_inc(glu_act, 1)
                for f in range(UT):
                    act.wait_ge(o_ready, XT + LT + f + 1)
                    act.activation(cat[:, LT + f, 0, :], xin[:, f, :], ACT.Copy).then_inc(o_hi, 1)

            param_loads()
            for n in range(RING):
                split(n)
            norm(0)
            mix0()
            out_proj(U_OUT0, PER_GROUP)
            norm(1)
            up_proj(U_UP0, A_UP0, 0)
            out_proj(U_DOWN0, DOWN_PER)
            norm(2)
            bc_loads()
            mix1_()
            out_proj(U_OUT1, PER_GROUP)
            norm(3)
            up_proj(U_UP1, A_UP1, 1)
            out_proj(U_DOWN1, DOWN_PER, last=True)
            act.wait_ge(acc_free, A_END)
            act.dma_start(g_fin[:, :], t["norm_final"].rearrange("(a d) -> a d", a=1).broadcast_to([P, D])
                          ).then_inc(gfin_loaded, 16)
            norm(4)
            for tt in range(TT):
                act.wait_ge(out_ready, tt + 1)
                act.dma_start(out[0, tt * P:tt * P + P, :], xn[:, tt, :]).then_inc(stored, 16)
            act.wait_ge(stored, 16 * TT)

        @block.vector
        def _(dve):
            made, base_at = [0], [None]

            def mark(ins):
                made[0] += 1
                return ins.then_inc(v_chain, 1)

            def join():
                dve.wait_ge(v_chain, made[0] if base_at[0] is None else base_at[0] + made[0])

            def link(ins):
                mark(ins)
                join()

            def split(u, it=None, per=0):
                if u >= U_END and it is None:
                    return
                dve.wait_ge(hi_ready, plus(u + 1, it, per))
                dve.tensor_tensor(w_lo[:, u % RING, :], raw[:, u % RING, :], w_hi[:, u % RING, :],
                                  ALU.subtract).then_inc(lo_ready, 1)

            def out_proj(u, d, per, last=False):
                n = CHUNKS - 1 if last else CHUNKS

                def add(i, cols, banks, done):
                    for tt in range(TT):
                        if tt < TT - 1:
                            dve.wait_ge(acc_done, plus(d + done + 1, i, 1))
                        else:
                            dve.wait_ge(unit_used, plus(u + (done + 1) * per, i, per))
                        r = res[:, tt, cols]
                        dve.tensor_tensor(r, banks(tt), r, ALU.add).then_inc(acc_free, 1)

                with dve.Fori(0, n) as i:
                    for k in range(per - 1):
                        split(u + k + RING, i, per)
                    add(i, bass.ds(i * COLS, COLS), lambda tt: ps[:, bass.ds(i * TT + tt, 1), :], 0)
                    split(u + per - 1 + RING, i, per)
                if last:
                    for k in range(per - RING):
                        split(u + n * per + k + RING)
                    add(None, slice(n * COLS, D), lambda tt: ps[:, n * TT + tt, :], n)

            def up_proj(u, a, h, layer):
                done = UP_ITERS * layer
                per = 2 * PER_GROUP
                chain0 = made[0]
                with dve.Fori(0, UP_ITERS) as i:
                    base_at[0] = i * 2

                    def weight(tap, f):
                        c = COL["ffn_conv_w"] + (layer * FFN_CONV + tap) * HT + f
                        return params[:, bass.ds(i * FT + c, 1)]

                    for k in range(PER_GROUP - 1):
                        split(u + k + RING, i, per)
                    dve.wait_ge(half_copied, i * 2 + (h + 1))
                    for f in range(FT):
                        dve.tensor_tensor(ffn_g[:, f, :], ps[:, f, 0:TOK], tmp[:, f, :], ALU.add).then_inc(acc_free, 1)
                    dve.wait_ge(acc_free, i * 2 * FT + (a + FT))
                    for f in range(FT):
                        bias = params[:, bass.ds(i * FT + (COL["ffn_conv_b"] + layer * HT + f), 1)]
                        ins = dve.tensor_scalar(cv[:, f, :], ffn_g[:, f, :], weight(2, f), bias, ALU.mult, ALU.add)
                    link(ins)
                    for lag in (1, 2):
                        for f in range(FT):
                            c = cv[:, f, lag:TOK]
                            ins = dve.scalar_tensor_tensor(out=c, in0=ffn_g[:, f, 0:TOK - lag], scalar=weight(2 - lag, f),
                                                           in1=c, op0=ALU.mult, op1=ALU.add)
                        if lag == 1:
                            link(ins)
                    ins.then_inc(ffn_conv, 1)
                    for k in range(PER_GROUP - 1, per - 1):
                        split(u + k + RING, i, per)
                    dve.wait_ge(half_copied, i * 2 + (h + 2))
                    for f in range(FT):
                        dve.tensor_tensor(ffn_v[:, f, :], ps[:, FT + f, 0:TOK], ffn_tv[:, f, :], ALU.add
                                          ).then_inc(acc_free, 1)
                    dve.wait_ge(ffn_act, i + (done + 1))
                    dve.wait_ge(acc_free, i * 2 * FT + (a + 2 * FT))
                    dve.tensor_tensor(ffn_v[:, :, :], ffn_v[:, :, :], cv[:, :, :], ALU.mult).then_inc(ffn_h, 1)
                    split(u + per - 1 + RING, i, per)
                    dve.wait_ge(ffn_hi, i + (done + 1))
                    dve.tensor_tensor(hff[:, bass.ds(i * FT, FT), 1, :], ffn_v[:, :, :],
                                      hff[:, bass.ds(i * FT, FT), 0, :], ALU.subtract).then_inc(ffn_lo, 1)
                assert made[0] - chain0 == 2
                made[0] = chain0 + 2 * UP_ITERS
                base_at[0] = None

            def norm(n):
                if n == 0:
                    dve.wait_ge(x_loaded, 32)
                else:
                    dve.wait_ge(acc_free, A_NORM[n])
                link(dve.tensor_tensor_reduce(xn[:, 1, :], res[:, 1, :], res[:, 1, :], 1.0, 0.0, ALU.mult, ALU.add,
                                              accum_out=tiny[:, 1:2]))
                dve.wait_ge(ssq_ready, n + 1)
                dve.tensor_scalar(tiny[:, 2:4], tiny[:, 0:2], 1.0 / D, EPS, ALU.mult, ALU.add).then_inc(ms_ready, 1)
                dve.wait_ge(sd_ready, n + 1)
                dve.reciprocal(tiny[:, 6:8], tiny[:, 4:6]).then_inc(rstd_ready, 1)
                dve.wait_ge(rstd_ready, n + 1)
                dve.tensor_scalar(xn[:, 1, :], res[:, 1, :], tiny[:, 7:8], None, ALU.mult).then_inc(xn_ready, 1)
                if n == 4:
                    dve.wait_ge(xn_ready, TT * 5)
                    dve.wait_ge(gfin_loaded, 16)
                    for tt in range(TT):
                        dve.tensor_tensor(xn[:, tt, :], xn[:, tt, :], g_fin[:, :], ALU.mult).then_inc(out_ready, 1)
                    return
                name = ("norm_mix", "norm_ffn")[n % 2]
                for kt in range(KT):
                    dve.wait_ge(y_hi_ready, KT * n + kt + 1)
                    dve.scalar_tensor_tensor(out=y[:, kt, 1, :], in0=ps[:, 4 + kt % 4, 0:TOK],
                                             scalar=pcol(name, KT * (n // 2) + kt), in1=y[:, kt, 0, :],
                                             op0=ALU.mult, op1=ALU.subtract).then_inc(y_lo_ready, 1)

            def param_columns():
                dve.wait_ge(rows_turned, 1)
                dve.tensor_copy(params[:, 0:COLS], ps[:, 0, :])
                dve.tensor_copy(params[:, COLS:NPARAM], ps[:, 1, 0:NPARAM - COLS]).then_inc(params_ready, 1)
                dve.wait_ge(params_ready, 1)
                for dst, name, n in ((neg_ba, "cd_b_a", LT), (neg_bi, "cd_b_i", LT)):
                    dve.tensor_scalar(dst, params[:, COL[name]:COL[name] + n], -1.0, None, ALU.mult)
                dve.wait_ge(consts_ready, 5)
                link(dve.reduce_sum(parity, strips.rearrange("p (k g) -> p g k", g=2), axis=mybir.AxisListType.X))

            def group(kind, u, a, d, h, dst):
                per = DT_UNITS if kind == "dt" else PER_GROUP
                for k in range(per):
                    if k == per - 1:
                        if kind == "v":
                            for tt in range(TT):
                                if tt < TT - 1:
                                    dve.wait_ge(acc_done, d + tt + 1)
                                else:
                                    dve.wait_ge(unit_used, u + per)
                                dve.tensor_copy(dst(tt), ps[:, (a + tt) % FT, :]).then_inc(acc_free, 1)
                        else:
                            for f in range(1 if kind == "dt" else FT):
                                dve.wait_ge(half_copied, h + f + 1)
                                rows = slice(0, SSD_HEADS) if kind == "dt" else slice(0, P)
                                dve.scalar_tensor_tensor(
                                    out=dst(f), in0=ps[rows, (a + f) % FT, 0:TOK],
                                    scalar=SB_DH ** -0.5 if kind == "q" else 1.0, in1=tmp[rows, (a + f) % FT, :],
                                    op0=ALU.mult, op1=ALU.add).then_inc(acc_free, 1)
                    split(u + k + RING)
                a += {"dt": 1, "v": TT}.get(kind, FT)
                d += D_OF.get(kind, FT - 1)
                h += {"dt": 1, "v": 0}.get(kind, FT)
                dve.wait_ge(acc_free, a)
                return u + per, a, d, h

            def conv(dst, src, name_w, name_b, tile0, tiles, taps, last_sem):
                for lag in range(taps):
                    for f in range(FT):
                        w = pcol(name_w, (taps - 1 - lag) * tiles + tile0 + f)
                        if lag == 0:
                            ins = dve.tensor_scalar(dst[:, f, :], src(f), w, pcol(name_b, tile0 + f),
                                                    ALU.mult, ALU.add)
                        else:
                            c = dst[:, f, lag:TOK]
                            ins = dve.scalar_tensor_tensor(out=c, in0=src(f)[:, 0:TOK - lag], scalar=w, in1=c,
                                                           op0=ALU.mult, op1=ALU.add)
                    if lag < taps - 1:
                        link(ins)
                ins.then_inc(last_sem, 1)

            def dt_path():
                c = [cv[0:SSD_HEADS, n, :] for n in range(4)]
                d, eq = dts[:, :], cs[:, :]
                dve.wait_ge(small_loaded, 96)
                link(dve.tensor_scalar(c[0], c[0], tiny[0:SSD_HEADS, 16:17], None, ALU.add))
                dve.scalar_tensor_tensor(out=c[1], in0=c[0], scalar=-1.0, in1=c[0], op0=ALU.mult, op1=ALU.max
                                         ).then_inc(dt_abs, 1)
                dve.wait_ge(dt_exp, 1)
                dve.tensor_scalar(c[2], c[1], 1.0, None, ALU.add).then_inc(dt_w, 1)
                dve.wait_ge(dt_w, 1)
                link(dve.tensor_scalar(d, c[2], -1.0, None, ALU.add))
                link(dve.tensor_scalar(eq, d, 0.0, None, ALU.is_equal))
                link(dve.tensor_tensor(d, d, eq, ALU.add))
                dve.wait_ge(dt_ln, 1)
                link(dve.reciprocal(d, d))
                link(dve.tensor_tensor(c[2], c[1], d, ALU.mult))
                link(dve.tensor_tensor(c[3], c[3], c[2], ALU.mult))
                link(dve.tensor_tensor(c[2], c[1], eq, ALU.mult))
                link(dve.tensor_tensor(c[3], c[3], c[2], ALU.add))
                link(dve.scalar_tensor_tensor(out=d, in0=c[0], scalar=0.0, in1=c[3], op0=ALU.max, op1=ALU.add))
                dve.wait_ge(dt_a, 1)
                link(dve.tensor_scalar(c[1], d, tiny[0:SSD_HEADS, 18:19], -1.0, ALU.mult, ALU.mult))
                dve.tensor_tensor_scan(eq, ones[0:SSD_HEADS, 0:1].broadcast_to([SSD_HEADS, TOK]), c[1], 0.0,
                                       ALU.mult, ALU.add).then_inc(cs_ready, 1)

            def ssd():
                dve.wait_ge(cs_turned, 1)
                dve.tensor_copy(dt_t[:, :, :], ps[:, 4, 0:64].rearrange("p (a b) -> p a b", a=TT)[:, :, 0:SSD_HEADS])
                dve.tensor_copy(cs_t[:, :, :], ps[:, 4, 64:128].rearrange("p (a b) -> p a b", a=TT)[:, :, 0:SSD_HEADS]).then_inc(cs_t_ready, 1)
                dve.wait_ge(cs_t_ready, 1)
                for n in range(TT * XT // 4):
                    tt, q = n % TT, n // TT
                    dve.wait_ge(x_turned, n + 1)
                    dve.tensor_tensor(
                        xdt[:, tt, q * COLS:(q + 1) * COLS].rearrange("p (h c) -> p h c", c=SSD_P),
                        ps[:, 5 + n % 2, :].rearrange("p (h c) -> p h c", c=SSD_P),
                        dt_t[:, tt, 8 * q:8 * q + 8].unsqueeze(2).broadcast_to([P, 8, SSD_P]),
                        ALU.mult).then_inc(xdt_ready, 1)
                for n in range(XT):
                    for h in (2 * n, 2 * n + 1):
                        dve.wait_ge(cb_done, h // RH + 1)
                        dve.wait_ge(decay_cut, h + 1)
                        if n >= 1:
                            dve.wait_ge(yh_done, n)
                        dve.tensor_tensor(flat(blk[h % 2]), ps[:, 4, 0:3 * P], flat(blk[2 + h % 2]),
                                          ALU.mult).then_inc(m_ready, 1)
                    if n >= 1:
                        skip_and_gate(n - 1)
                skip_and_gate(XT - 1)
                join()
                for n in range(XT):
                    if n >= FT:
                        dve.wait_ge(sq_summed, n - FT + 1)
                    dve.tensor_tensor(tmp[:, n % FT, :], xbc[:, n, :], xbc[:, n, :], ALU.mult).then_inc(sq_ready, 1)
                dve.wait_ge(sq_summed, XT)
                dve.tensor_scalar(cv[:, 0, :], ps[:, 4, 0:TOK], 1.0 / SSD_W, EPS, ALU.mult, ALU.add).then_inc(gn_ms, 1)
                dve.wait_ge(gn_sd, 1)
                link(dve.reciprocal(cv[:, 1, :], cv[:, 0, :]))
                for n in range(XT + 1):
                    if n < XT:
                        dve.scalar_tensor_tensor(out=tmp[:, n % FT, :], in0=xbc[:, n, :], scalar=pcol("ab_ssd_norm", n),
                                                 in1=cv[:, 1, :], op0=ALU.mult, op1=ALU.mult).then_inc(o_ready, 1)
                    if n >= 1:
                        dve.wait_ge(o_hi, n)
                        dve.tensor_tensor(cat[:, SB_HEADS + n - 1, 1, :], tmp[:, (n - 1) % FT, :],
                                          cat[:, SB_HEADS + n - 1, 0, :], ALU.subtract).then_inc(o_lo, 1)

            def skip_and_gate(n):
                dve.wait_ge(yh_done, n + 1)
                dve.scalar_tensor_tensor(out=xbc[:, n, :], in0=xbc[:, n, :], scalar=tiny[:, 20 + n:21 + n],
                                         in1=ps[:, 6 + n % 2, 0:TOK], op0=ALU.mult, op1=ALU.add).then_inc(ys_ready, 1)
                dve.wait_ge(ys_ready, n + 1)
                if n == 0:
                    dve.wait_ge(z_act, 3)
                mark(dve.tensor_tensor(xbc[:, n, :], xbc[:, n, :], zg[:, n, :], ALU.mult))

            def attention():
                for h in range(SB_HEADS):
                    dve.wait_ge(z_ln, h + 1)
                    if h >= 1:
                        dve.wait_ge(zs_full, h)
                    dve.scalar_tensor_tensor(out=flat(blk[2]), in0=ps[:, 4 + h % 2, 0:3 * P], scalar=0.0,
                                             in1=flat(blk[0]), op0=ALU.max, op1=ALU.add).then_inc(sp_ready, 1)
                    dve.wait_ge(att_hi, h + 1)
                    dve.tensor_tensor(cat[:, h, 1, :], ps[:, 6 + h % 2, 0:TOK], cat[:, h, 0, :],
                                      ALU.subtract).then_inc(att_lo, 1)

            def mix0():
                u, a, d, h = U_AB, A_AB, D_AB, H_AB
                n_x = n_z = 0
                for kind, _ in AB_GROUPS:
                    dst = {
                        "x": lambda f: xbc[:, FT * n_x + f, :],
                        "dt": lambda f: cv[0:SSD_HEADS, 0, :],
                        "q": lambda f: qk[:, f, :],
                        "k": lambda f: qk[:, SB_HEADS + f, :],
                        "v": lambda tt: v_t[:, tt, :],
                        "z": lambda f: zg[:, FT * n_z + f, :],
                    }[kind]
                    if kind == "dt":
                        dve.wait_ge(xact, 5)
                    u, a, d, h = group(kind, u, a, d, h, dst)
                    if kind == "x":
                        if n_x:
                            dve.wait_ge(xact, n_x)
                        conv(cv, lambda f: xbc[:, FT * n_x + f, :], "ab_conv_w", "ab_conv_b", FT * n_x, 20,
                             SSD_CONV, xconv)
                        n_x += 1
                    elif kind == "dt":
                        dt_path()
                    elif kind == "z":
                        n_z += 1
                ssd()
                attention()

            def s5_prep():
                li = params[:, COL["cd_a_im"]:COL["cd_a_im"] + ST]
                lam = params[:, COL["cd_lambda"]:COL["cd_lambda"] + LT]

                def tt_(o, a, b, op):
                    link(dve.tensor_tensor(o, a, b, op))

                def ts_(o, a, x, op, x2=None, op2=None):
                    if op2 is None:
                        link(dve.tensor_scalar(o, a, x, None, op))
                    else:
                        link(dve.tensor_scalar(o, a, x, x2, op, op2))

                dve.wait_ge(s5a, 1)
                ts_(s5(LR), params[:, COL["cd_a_re"]:COL["cd_a_re"] + ST], -1e-4, ALU.min)
                tt_(s5(XDT), s5(LR), s5(DTV), ALU.mult)
                tt_(s5(THETA), li, s5(DTV), ALU.mult)
                ts_(s5(T0), s5(THETA), 0.15915494309189535, ALU.mult)
                ts_(s5(T0), s5(T0), ROUND, ALU.add)
                ts_(s5(T0), s5(T0), -ROUND, ALU.add)
                src = s5(THETA)
                for part in TWO_PI:
                    link(dve.scalar_tensor_tensor(out=s5(TURN), in0=s5(T0), scalar=-part, in1=src,
                                                  op0=ALU.mult, op1=ALU.add))
                    src = s5(TURN)
                dve.tensor_scalar(s5(TURN), s5(TURN), 3.1415925, -3.1415925, ALU.min, ALU.max).then_inc(s5v, 1)
                dve.wait_ge(s5a, 3)
                e, w, ln, t3, eq = (s5p[:, n, 0:LT] for n in (T0, T2, T1, T3, FR))
                dve.tensor_scalar(w, e, 1.0, None, ALU.add).then_inc(s5v, 1)
                dve.wait_ge(s5v, 2)
                ts_(t3, w, -1.0, ALU.add)
                ts_(eq, t3, 0.0, ALU.is_equal)
                tt_(t3, t3, eq, ALU.add)
                link(dve.reciprocal(t3, t3))
                tt_(t3, e, t3, ALU.mult)
                dve.wait_ge(s5a, 4)
                tt_(ln, ln, t3, ALU.mult)
                tt_(t3, e, eq, ALU.mult)
                tt_(ln, ln, t3, ALU.add)
                ts_(t3, lam, -1.0, ALU.mult, 0.0, ALU.max)
                tt_(ln, ln, t3, ALU.add)
                ts_(c8, ln, -LRU_C, ALU.mult)
                tt_(s5(SIN2), s5(SINH), s5(SINH), ALU.mult)
                dve.tensor_scalar(s5(COS), s5(SIN2), -2.0, 1.0, ALU.mult, ALU.add).then_inc(s5v, 1)
                dve.wait_ge(s5v, 3)
                ts_(s5(T2), s5(TH), -1.0, ALU.mult, 1.0, ALU.add)
                link(dve.reciprocal(s5(T2), s5(T2)))
                tt_(s5(E1), s5(TH), s5(T2), ALU.mult)
                ts_(s5(E1), s5(E1), 2.0, ALU.mult)
                tt_(s5(AM1), s5(E1), s5(COS), ALU.mult)
                link(dve.scalar_tensor_tensor(out=s5(AM1), in0=s5(SIN2), scalar=-2.0, in1=s5(AM1),
                                              op0=ALU.mult, op1=ALU.add))
                tt_(s5(ABI), s5(MAG), s5(SIN), ALU.mult)
                tt_(s5(DEN), s5(LR), s5(LR), ALU.mult)
                tt_(s5(T2), li, li, ALU.mult)
                tt_(s5(DEN), s5(DEN), s5(T2), ALU.add)
                tt_(s5(T2), s5(AM1), s5(LR), ALU.mult)
                tt_(s5(T3), s5(ABI), li, ALU.mult)
                tt_(s5(T2), s5(T2), s5(T3), ALU.add)
                link(dve.reciprocal(s5(DEN), s5(DEN)))
                tt_(s5(FR), s5(T2), s5(DEN), ALU.mult)
                tt_(s5(T2), s5(ABI), s5(LR), ALU.mult)
                tt_(s5(T3), s5(AM1), li, ALU.mult)
                tt_(s5(T2), s5(T2), s5(T3), ALU.subtract)
                tt_(s5(FI), s5(T2), s5(DEN), ALU.mult)
                dve.wait_ge(bc_loaded, 96)
                dve.wait_ge(s5g, 1)
                fr = s5(FR).unsqueeze(2).broadcast_to([P, ST, S5_CH])
                fi = s5(FI).unsqueeze(2).broadcast_to([P, ST, S5_CH])
                for ri, op in enumerate((ALU.subtract, ALU.add)):
                    mark(dve.tensor_tensor(b_tmp[:, 0, :, :], b_raw[:, ri, :, :], fr, ALU.mult))
                    tt_(b_tmp[:, 1, :, :], b_raw[:, 1 - ri, :, :], fi, ALU.mult)
                    for gl in range(2):
                        rows = slice(64 * gl, 64 * gl + 64)
                        ins = dve.tensor_tensor(b_pad[rows, ri, :, gl, :], b_tmp[rows, 0, :, :], b_tmp[rows, 1, :, :], op)
                    if ri:
                        ins.then_inc(s5_pads, 1)
                    else:
                        link(ins)
                for gl in range(2):
                    dve.tensor_scalar(c_pad[:, 0, :, gl, :], c_pad[:, 0, :, gl, :], parity[:, gl:gl + 1], None, ALU.mult)
                    ins = dve.tensor_scalar(c_pad[:, 1, :, gl, :], c_pad[:, 1, :, gl, :], parity[:, gl:gl + 1], -1.0,
                                            ALU.mult, ALU.mult)
                ins.then_inc(s5_pads, 1)
                dve.wait_ge(s5_turned, 1)
                for ri in range(2):
                    dve.tensor_copy(bb[:, ri, :, :], ps[:, 4 + ri, :].rearrange("p (q n) -> p q n", n=P))
                    dve.tensor_copy(cc[:, ri, :, :], ps[:, 6 + ri, :].rearrange("p (q n) -> p q n", n=P)
                                    ).then_inc(s5_mats, 1)

            def lru(g):
                conv(cv, lambda f: xin[:, f, :], "cd_conv_w", "cd_conv_b", FT * g, LT, LRU_CONV, xc_ready)
                dve.wait_ge(gates_exp, FT * (g + 1))
                mark(dve.tensor_scalar(lru_i[:, :, :], lru_i[:, :, :], 1.0, None, ALU.add))
                link(dve.tensor_scalar(lru_r[:, :, :], lru_r[:, :, :], 1.0, None, ALU.add))
                dve.reciprocal(lru_r[:, :, :], lru_r[:, :, :]).then_inc(r_ready, 1)
                link(dve.reciprocal(lru_i[:, :, :], lru_i[:, :, :]))
                link(dve.tensor_tensor(cv[:, :, :], cv[:, :, :], lru_i[:, :, :], ALU.mult))
                dve.wait_ge(lru_th, g + 1)
                link(dve.tensor_scalar(lru_i[:, :, :], lru_r[:, :, :], -1.0, 1.0, ALU.mult, ALU.add))
                link(dve.reciprocal(lru_i[:, :, :], lru_i[:, :, :]))
                dve.tensor_tensor(lru_r[:, :, :], lru_r[:, :, :], lru_i[:, :, :], ALU.mult).then_inc(lru_q, 1)
                dve.wait_ge(lru_sd, g + 1)
                link(dve.tensor_tensor(cv[:, :, :], cv[:, :, :], lru_r[:, :, :], ALU.mult))
                for f in range(FT):
                    dve.tensor_tensor_scan(hs[:, FT * g + f, :], xin[:, f, :], cv[:, f, :], 0.0, ALU.mult, ALU.add
                                           ).then_inc(hs_ready, 1)

            def gelu(x, n):
                link(dve.tensor_tensor(cv[:, :, :], x[:, :, :], x[:, :, :], ALU.mult))
                link(dve.tensor_scalar(cv[:, :, :], cv[:, :, :], GELU_K, 1.0, ALU.mult, ALU.add))
                dve.tensor_tensor(cv[:, :, :], cv[:, :, :], x[:, :, :], ALU.mult).then_inc(gelu_u, 1)
                dve.wait_ge(gelu_e, n + 1)
                link(dve.scalar_tensor_tensor(out=x[:, :, :], in0=cv[:, :, :], scalar=1.0, in1=x[:, :, :],
                                              op0=ALU.add, op1=ALU.mult))

            def lows(first, tile0):
                for f in range(FT):
                    dve.wait_ge(o_hi, first + f + 1)
                    dve.tensor_tensor(cat[:, tile0 + f, 1, :], xin[:, f, :], cat[:, tile0 + f, 0, :],
                                      ALU.subtract).then_inc(o_lo, 1)

            def gate_out(g):
                gelu(xin, g)
                dve.wait_ge(hs_ready, LT)
                for f in range(FT):
                    dve.scalar_tensor_tensor(out=xin[:, f, :], in0=xin[:, f, :], scalar=0.5, in1=hs[:, FT * g + f, :],
                                             op0=ALU.mult, op1=ALU.mult).then_inc(o_ready, 1)
                lows(XT + FT * g, FT * g)

            def s5_states():
                for j in range(ST):
                    q, jj = j // 4, j % 4
                    pr, pi = (ph[:, jj:jj + 1, ri, :].broadcast_to([P, 2, TOK]) for ri in range(2))
                    x = ps[:, 4 + j % 2, :].rearrange("p (r n) -> p r n", r=2)
                    dve.wait_ge(bu_done, j + 1)
                    dve.wait_ge(phases_ready, q + 1)
                    dve.tensor_tensor(bq[:, 0, :, :], x, pr, ALU.mult)
                    dve.tensor_tensor(bq[:, 1, :, :], x, pi, ALU.mult).then_inc(bu_free, 1)
                    dve.wait_ge(bu_free, j + 1)
                    if j >= 1:
                        dve.wait_ge(st_ready, j)
                    mark(dve.tensor_tensor(gs[:, 0, :], bq[:, 0, 0, :], bq[:, 1, 1, :], ALU.add))
                    link(dve.tensor_tensor(gs[:, 1, :], bq[:, 0, 1, :], bq[:, 1, 0, :], ALU.subtract))
                    mag = s5p[:, MAG, j:j + 1].broadcast_to([P, TOK])
                    for ri in range(2):
                        ins = dve.tensor_tensor_scan(gs[:, ri, :], mag, gs[:, ri, :], 0.0, ALU.mult, ALU.add)
                    ins.then_inc(scanned, 1)
                    if j % 4 == 0 and j:
                        s5_skip(q - 1)
                s5_skip(UT - 1)

            def s5_skip(q):
                dve.wait_ge(y5_done, 4 * (q + 1))
                dve.scalar_tensor_tensor(out=ut[:, q, :], in0=ut[:, q, :], scalar=pcol("cd_d_skip", q),
                                         in1=ps[:, 6 + q % 2, 0:TOK], op0=ALU.mult, op1=ALU.add).then_inc(y5_ready, 1)

            def glu():
                dve.wait_ge(y5_ready, UT)
                gelu(ut, LT // FT)
                dve.tensor_scalar(ut[:, :, :], ut[:, :, :], 0.5, None, ALU.mult).then_inc(glu_in, 1)
                dve.wait_ge(glu_in, 1)
                dve.wait_ge(glu_act, UT)
                for f in range(UT):
                    dve.tensor_tensor(xin[:, f, :], ut[:, f, :], tmp[:, f, :], ALU.mult).then_inc(o_ready, 1)
                lows(XT + LT, LT)

            def mix1_():
                s5_prep()
                u, a, d, h = U_CD, A_CD, D_CD, H_CD
                n_x = n_g = 0
                for kind, _ in CD_GROUPS:
                    dst = ut if kind == "u" else xin
                    u, a, d, h = group(kind, u, a, d, h, lambda f: dst[:, f, :])
                    if kind == "x":
                        lru(n_x)
                        n_x += 1
                    elif kind == "g":
                        gate_out(n_g)
                        n_g += 1
                s5_states()
                glu()

            param_columns()
            for n in range(RING):
                split(n)
            norm(0)
            mix0()
            out_proj(U_OUT0, D_OUT0, PER_GROUP)
            norm(1)
            up_proj(U_UP0, A_UP0, H_UP0, 0)
            out_proj(U_DOWN0, D_DOWN0, DOWN_PER)
            norm(2)
            mix1_()
            out_proj(U_OUT1, D_OUT1, PER_GROUP)
            norm(3)
            up_proj(U_UP1, A_UP1, H_UP1, 1)
            out_proj(U_DOWN1, D_DOWN1, DOWN_PER, last=True)
            norm(4)

        @block.gpsimd
        def _(pool):
            chain = [0]

            def mark(ins):
                chain[0] += 1
                ins.then_inc(g_chain, 1)

            def link(ins):
                mark(ins)
                pool.wait_ge(g_chain, chain[0])

            def constants():
                mark(pool.memset(ident[:, :], 0.0))
                mark(pool.memset(neg_tri[:, :], -1.0))
                mark(pool.memset(strips, 1.0))
                pool.memset(ones[:, :], 1.0).then_inc(consts_ready, 1)
                pool.memset(neg_ones[:, :], -1.0).then_inc(consts_ready, 1)
                pool.wait_ge(g_chain, chain[0])
                pool.affine_select(out=ident[:, :], in_=ident[:, :], compare_op=ALU.not_equal, fill=1.0, base=0,
                                   pattern=[[-1, P]], channel_multiplier=1).then_inc(consts_ready, 1)
                pool.affine_select(out=neg_tri[:, :], in_=neg_tri[:, :], compare_op=ALU.is_ge, fill=0.0, base=0,
                                   pattern=[[-1, P]], channel_multiplier=1).then_inc(consts_ready, 1)
                link(pool.affine_select(out=strips, in_=strips, compare_op=ALU.is_ge, fill=0.0, base=0,
                                        pattern=[[-S5_CH, 8]], channel_multiplier=1))
                pool.affine_select(out=strips, in_=strips, compare_op=ALU.is_ge, fill=0.0, base=S5_CH - 1,
                                   pattern=[[S5_CH, 8]], channel_multiplier=-1).then_inc(consts_ready, 1)

            def cut(dst, src, least, done):
                pool.affine_select(out=dst[:, 0:3:2, :], in_=src[:, 0:3:2, :], compare_op=ALU.is_ge, fill=0.0,
                                   base=-least, pattern=[[0, 2], [1, P]], channel_multiplier=-1).then_inc(done, 1)

            def phases(q):
                if q:
                    pool.wait_ge(scanned, 4 * q)
                    pool.wait_ge(st_ready, 4 * q)
                for ri, src in enumerate((COS, SIN)):
                    mark(pool.tensor_copy(ph[:, :, ri, 0:1], s5p[:, src, 4 * q:4 * q + 4].unsqueeze(2)))
                pool.wait_ge(g_chain, chain[0])
                n = 1
                while n < TOK:
                    x = ph[:, :, :, 0:n]
                    for f in range(FT):
                        for ri in range(2):
                            mark(pool.tensor_tensor(pt[:, ri, f, :, 0:n], ph[:, f, :, 0:n],
                                                    ph[:, f, ri:ri + 1, n - 1:n].broadcast_to([P, 2, n]), ALU.mult))
                    pool.wait_ge(g_chain, chain[0])
                    mark(pool.tensor_tensor(ph[:, :, 0, n:2 * n], pt[:, 0, :, 0, 0:n], pt[:, 1, :, 1, 0:n], ALU.subtract))
                    ins = pool.tensor_tensor(ph[:, :, 1, n:2 * n], pt[:, 0, :, 1, 0:n], pt[:, 1, :, 0, 0:n], ALU.add)
                    n *= 2
                    if n < TOK:
                        link(ins)
                    else:
                        ins.then_inc(phases_ready, 1)
                        pool.wait_ge(phases_ready, q + 1)

            def turn_states(j):
                jj = j % 4
                pr, pi = (ph[:, jj:jj + 1, ri, :].broadcast_to([P, 2, TOK]) for ri in range(2))
                pool.wait_ge(scanned, j + 1)
                mark(pool.tensor_tensor(rot[:, 0, :, :], gs[:, :, :], pr, ALU.mult))
                link(pool.tensor_tensor(rot[:, 1, :, :], gs[:, :, :], pi, ALU.mult))
                if j >= 1:
                    pool.wait_ge(y5_done, j)
                pool.tensor_tensor(st[:, 0, :], rot[:, 0, 0, :], rot[:, 1, 1, :], ALU.subtract)
                pool.tensor_tensor(st[:, 1, :], rot[:, 0, 1, :], rot[:, 1, 0, :], ALU.add).then_inc(st_ready, 1)

            constants()
            for h in range(SSD_HEADS):
                pool.wait_ge(decay_ready, h + 1)
                cut(blk[2 + h % 2], blk[2 + h % 2], 0, decay_cut)
            for h in range(SB_HEADS):
                pool.wait_ge(sp_ready, h + 1)
                cut(blk[2], blk[2], 1, sp_cut)
                pool.wait_ge(w_exp, h + 1)
                if h >= 1:
                    pool.wait_ge(att_done, h)
                link(pool.tensor_copy(blk[3][:, 1, :], blk[1][:, 1, :]))
                cut(blk[3], blk[1], 1, w_cut)
            pool.wait_ge(acc_free, A_CD)
            pool.memset(b_pad[:, :, :, :, :], 0.0).then_inc(s5g, 1)
            pool.wait_ge(y_lo_ready, 3 * KT)
            pool.wait_ge(s5v, 3)
            for j in range(ST):
                if j % 4 == 0:
                    phases(j // 4)
                turn_states(j)


_INS = ["x", "norm_mix", "norm_ffn", "norm_final", "ab_w_in", "ab_conv_w", "ab_conv_b", "ab_dt_bias", "ab_a_log",
        "ab_d_skip", "ab_ssd_norm", "ab_w_out", "cd_w_in", "cd_conv_w", "cd_conv_b", "cd_w_a", "cd_b_a", "cd_w_i",
        "cd_b_i", "cd_lambda", "cd_log_dt", "cd_a_re", "cd_a_im", "cd_b_re", "cd_b_im", "cd_c_re", "cd_c_im",
        "cd_d_skip", "cd_w_glu", "cd_b_glu", "cd_w_out", "ffn_w_up", "ffn_conv_w", "ffn_conv_b", "ffn_w_down"]


def kernel(**inputs):
    import numpy as np
    import concourse.bacc as bacc
    from concourse.bass_utils import run_bass_kernel_spmd

    nc = bacc.Bacc("TRN2", target_bir_lowering=False, num_devices=1)
    arrays, tensors = {}, {}
    for name in _INS:
        a = np.ascontiguousarray(inputs[name])
        arrays[f"in_{name}"] = a
        tensors[name] = nc.dram_tensor(f"in_{name}", a.shape, mybir.dt.from_np(a.dtype), kind="ExternalInput").ap()
    out = nc.dram_tensor("out_0", (1, TOK, D), F32, kind="ExternalOutput").ap()
    trunk(nc, tensors, out)
    r = run_bass_kernel_spmd(nc, [arrays], core_ids=[0])
    return r.results[0]["out_0"]
```

```python
from contextlib import ExitStack

import concourse.bass as bass
from concourse import mybir

ALU = mybir.AluOpType
ACT = mybir.ActivationFunctionType
F32 = mybir.dt.float32
F32R = mybir.dt.float32r

P = 128
TOK = 256
TT = TOK // P
D = 2048
KT = D // P
COLS = 512
FT = COLS // P
HK = 2
RING = 4
EPS = 1e-6

SB_HEADS, SB_DH = 4, 128
SSD_HEADS, SSD_P, SSD_GROUPS, SSD_N, SSD_CONV = 24, 64, 4, 128, 4
SSD_W = SSD_HEADS * SSD_P
XT = SSD_W // P
RH = SSD_HEADS // SSD_GROUPS
LRU_W, LRU_CONV, LRU_C = 1536, 4, 8.0
LT = LRU_W // P
S5_G, S5_CH, S5_N = 32, 16, 64
S5_W = S5_G * S5_CH
ST = S5_G * S5_N // P
UT = S5_W // P
DFF, FFN_CONV = 4096, 3
HT = DFF // P

PARAM_ROWS = [
    ("norm_mix", 2 * KT), ("norm_ffn", 2 * KT), ("ab_ssd_norm", XT),
    ("ab_conv_b", 20), ("ab_conv_w", SSD_CONV * 20),
    ("cd_conv_w", LRU_CONV * LT), ("cd_conv_b", LT), ("cd_b_a", LT), ("cd_b_i", LT),
    ("cd_lambda", LT), ("cd_d_skip", UT), ("cd_b_glu", UT),
    ("ffn_conv_w", 2 * FFN_CONV * HT), ("ffn_conv_b", 2 * HT),
    ("cd_a_re", ST), ("cd_a_im", ST),
]
COL = {}
_at = 0
for _name, _n in PARAM_ROWS:
    COL[_name] = _at
    _at += _n
NPARAM = _at
PT = -(-NPARAM // P)


def param_pieces():
    for name, n in PARAM_ROWS:
        done = 0
        while done < n:
            at = COL[name] + done
            m = min(n - done, P - at % P)
            yield name, done, at // P, at % P, m
            done += m


AB_GROUPS = [("x", 3072), ("x", 3584), ("x", 4096), ("x", 4608), ("x", 5120), ("dt", 5632),
             ("q", 0), ("k", 512), ("v", 1024), ("z", 1536), ("z", 2048), ("z", 2560)]
CD_GROUPS = [("u", 3072), ("x", 1536), ("x", 2048), ("x", 2560), ("g", 0), ("g", 512), ("g", 1024)]
LRU_AT = [15 + 8 * g for g in range(3)]
GATE_AT = [39 + 8 * g for g in range(3)]
S5_AT = [8, 10, 12, 14, 21, 23, 25, 27, 35, 37, 39, 41, 43, 45, 47, 49]
S5_OUT = 4
PER_GROUP = KT // HK
DT_UNITS = 2
CHUNKS = D // COLS

AB_UNITS = sum(DT_UNITS if k == "dt" else PER_GROUP for k, _ in AB_GROUPS)
CD_UNITS = PER_GROUP * len(CD_GROUPS)
CD_STEPS = GATE_AT[-1] + 7
OUT_UNITS = CHUNKS * PER_GROUP
UP_ITERS = DFF // COLS
UP_UNITS = UP_ITERS * 2 * PER_GROUP
DOWN_PER = HT // HK
DOWN_UNITS = CHUNKS * DOWN_PER

U_AB = 0
U_OUT0 = U_AB + AB_UNITS
U_UP0 = U_OUT0 + OUT_UNITS
U_DOWN0 = U_UP0 + UP_UNITS
U_CD = U_DOWN0 + DOWN_UNITS
U_OUT1 = U_CD + CD_UNITS
U_UP1 = U_OUT1 + OUT_UNITS
U_DOWN1 = U_UP1 + UP_UNITS
U_END = U_DOWN1 + DOWN_UNITS

AB_ACCS = sum({"dt": 1, "v": TT}.get(k, FT) for k, _ in AB_GROUPS)
CD_ACCS = FT * len(CD_GROUPS)
OUT_ACCS = CHUNKS * TT
UP_ACCS = UP_ITERS * 2 * FT
A_AB = 0
A_OUT0 = A_AB + AB_ACCS
A_UP0 = A_OUT0 + OUT_ACCS
A_DOWN0 = A_UP0 + UP_ACCS
A_CD = A_DOWN0 + OUT_ACCS
A_OUT1 = A_CD + CD_ACCS
A_UP1 = A_OUT1 + OUT_ACCS
A_DOWN1 = A_UP1 + UP_ACCS
A_END = A_DOWN1 + OUT_ACCS
D_OF = {"dt": 0, "v": TT - 1}
D_AB = 0
D_OUT0 = D_AB + sum(D_OF.get(k, FT - 1) for k, _ in AB_GROUPS)
D_DOWN0 = D_OUT0 + CHUNKS
D_CD = D_DOWN0 + CHUNKS
D_OUT1 = D_CD + (FT - 1) * len(CD_GROUPS)
D_DOWN1 = D_OUT1 + CHUNKS
A_NORM = [0, A_UP0, A_CD, A_UP1, A_END]
H_AB = 0
H_UP0 = H_AB + AB_ACCS - TT
H_CD = H_UP0 + 2 * UP_ITERS
H_UP1 = H_CD + CD_ACCS
GELU_C = 0.7978845608028654
GELU_K = 0.044715
TWO_PI = (6.28125, 0.0019350051879882812, 3.01991598196e-07)
ROUND = 12582912.0


def trunk(nc, t, out):
    def at(name, shape, dtype, offset):
        return nc.alloc_sbuf_tensor_at(name, shape, dtype, offset=offset)

    KB = 1024
    base = 16512
    raw = at("raw", [P, RING, HK * COLS], F32, base)
    w_hi = at("w_hi", [P, RING, HK * COLS], F32R, base + 16 * KB)
    w_lo = at("w_lo", [P, RING, HK * COLS], F32R, base + 32 * KB)
    res = at("res", [P, TT, D], F32, base + 48 * KB)
    y = at("y", [P, KT, 2, TOK], F32R, base + 64 * KB)
    hff = at("hff", [P, HT, 2, TOK], F32R, base + 96 * KB)
    cat = hff
    mix2 = base + 128 * KB
    xn = at("xn", [P, TT, D], F32, mix2)
    c0 = base + 160 * KB
    params = at("params", [P, NPARAM], F32, c0)
    ident = at("ident", [P, P], F32, c0 + 2304)
    ones = at("ones", [P, P], F32, c0 + 2304 + 512)
    neg_ones = at("neg_ones", [P, P], F32, c0 + 2304 + 1024)
    neg_tri = at("neg_tri", [P, P], F32, c0 + 2304 + 1536)
    s5p = at("s5p", [P, 26, ST], F32, c0 + 4352)
    tiny = at("tiny", [P, 64], F32, c0 + 6016)
    c1 = c0 + 6272
    dt_t = at("dt_t", [P, TT, SSD_HEADS], F32, c1)
    cs_t = at("cs_t", [P, TT, SSD_HEADS], F32, c1 + 192)
    c8 = at("c8", [P, LT], F32, c1 + 384)
    parity = at("parity", [P, 2], F32, c1 + 448)[:, :]
    strips = at("strips", [P, 8], F32, c1 + 480)[:, :]
    mix1 = c1 + 608

    prow = at("prow", [P, PT, P], F32, mix1)
    xbc = at("xbc", [P, 20, TOK], F32, mix1)
    qk = at("qk", [P, 2 * SB_HEADS, TOK], F32, mix1 + 20 * KB)
    v_t = at("v_t", [P, TT, SB_HEADS * SB_DH], F32, mix1 + 28 * KB)
    tmp = at("tmp", [P, FT, TOK], F32, mix1 + 32 * KB)
    cv = at("cv", [P, FT, TOK], F32, mix1 + 36 * KB)
    zg = at("zg", [P, XT, TOK], F32, mix2)
    xdt = at("xdt", [P, TT, SSD_W], F32, mix2 + 12 * KB)
    blk = [at(f"blk{n}", [P, 3, P], F32, mix2 + 24 * KB + 1536 * n) for n in range(4)]
    dts = at("dts", [SSD_HEADS, TOK], F32, mix2 + 30 * KB)
    cs = at("cs", [SSD_HEADS, TOK], F32, mix2 + 31 * KB)
    ffn_g = at("ffn_g", [P, FT, TOK], F32, mix1)
    ffn_tv = at("ffn_tv", [P, FT, TOK], F32, mix1 + 4 * KB)
    ffn_v = at("ffn_v", [P, FT, TOK], F32, mix1 + 8 * KB)
    hs = at("hs", [P, LT, TOK], F32, mix1)
    ut = at("ut", [P, UT, TOK], F32, mix1 + 12 * KB)
    wai = at("wai", [P, 2, FT, P], F32, mix1 + 16 * KB)
    xin = at("xin", [P, FT, TOK], F32, mix1 + 20 * KB)
    lru_r = at("lru_r", [P, FT, TOK], F32, mix1 + 24 * KB)
    lru_i = at("lru_i", [P, FT, TOK], F32, mix1 + 28 * KB)
    w_glu = at("w_glu", [P, UT, S5_W], F32, mix1 + 24 * KB)
    ph = [at(f"ph{n}", [P, FT, 2, TOK], F32, mix2 + 16 * KB * n) for n in range(2)]
    bq = at("bq", [P, 2, 2, TOK], F32, mix2 + 8 * KB)
    gs = at("gs", [P, 2, 2, TOK], F32, mix2 + 12 * KB)
    s5_gelu = at("s5_gelu", [P, UT, TOK], F32, mix2 + 16 * KB)
    s5_gate = at("s5_gate", [P, UT, TOK], F32, mix2 + 20 * KB)
    pt = at("pt", [P, 2, FT, 2, P // 2], F32, mix2 + 24 * KB)
    rot = at("rot", [P, 2, 2, TOK], F32, mix2 + 24 * KB)
    st = at("st", [P, 2, 2, TOK], F32, mix2 + 28 * KB)
    bb = at("bb", [P, 2, UT, P], F32, base + 120 * KB)
    cc = at("cc", [P, 2, UT, P], F32, base + 124 * KB)
    b_raw = at("b_raw", [P, 2, ST, S5_CH], F32, mix1 + 20 * KB)
    b_pad = at("b_pad", [P, 2, ST, 2, S5_CH], F32, mix1 + 22 * KB)
    c_pad = at("c_pad", [P, 2, UT, 2, S5_N], F32, mix1 + 26 * KB)
    b_tmp = at("b_tmp", [P, 2, ST, S5_CH], F32, mix1 + 30 * KB)
    g_fin = at("g_fin", [P, D], F32, mix1)

    with ExitStack() as ctx:
        ps = ctx.enter_context(nc.psum_tensor("ps", [P, 8, COLS], F32))

        def sem(name):
            return ctx.enter_context(nc.semaphore(name))

        raw_loaded = [sem(f"raw_loaded{n}") for n in range(RING)]
        hi_ready, lo_ready, unit_used = sem("hi_ready"), sem("lo_ready"), sem("unit_used")
        acc_done, acc_free, half_copied = sem("acc_done"), sem("acc_free"), sem("half_copied")
        x_loaded, rows_loaded, small_loaded = sem("x_loaded"), sem("rows_loaded"), sem("small_loaded")
        consts_ready, rows_turned, params_ready = sem("consts_ready"), sem("rows_turned"), sem("params_ready")
        v_chain, a_chain, g_chain = sem("v_chain"), sem("a_chain"), sem("g_chain")
        ssq_ready, ms_ready, sd_ready = sem("ssq_ready"), sem("ms_ready"), sem("sd_ready")
        rstd_ready, xn_ready, turned = sem("rstd_ready"), sem("xn_ready"), sem("turned")
        y_hi_ready, y_lo_ready = sem("y_hi_ready"), sem("y_lo_ready")
        ffn_conv, ffn_act, ffn_h, ffn_hi, ffn_lo = (
            sem("ffn_conv"), sem("ffn_act"), sem("ffn_h"), sem("ffn_hi"), sem("ffn_lo"))
        xconv, xact, z_act = sem("xconv"), sem("xact"), sem("z_act")
        dt_abs, dt_exp, dt_w, dt_ln, dt_a, cs_ready = (
            sem("dt_abs"), sem("dt_exp"), sem("dt_w"), sem("dt_ln"), sem("dt_a"), sem("cs_ready"))
        cs_turned, cs_t_ready, x_turned, xdt_ready = (
            sem("cs_turned"), sem("cs_t_ready"), sem("x_turned"), sem("xdt_ready"))
        cb_done, cb_free, cs_spread, decay_ready, decay_cut, m_ready, yh_done, ys_ready = (
            sem("cb_done"), sem("cb_free"), sem("cs_spread"), sem("decay_ready"), sem("decay_cut"),
            sem("m_ready"), sem("yh_done"), sem("ys_ready"))
        gated, sq_ready, sq_summed, gn_ms, gn_sd, gn_rstd = (
            sem("gated"), sem("sq_ready"), sem("sq_summed"), sem("gn_ms"), sem("gn_sd"), sem("gn_rstd"))
        o_ready, o_hi, o_lo = sem("o_ready"), sem("o_hi"), sem("o_lo")
        zs_done, z_ln, sp_ready, sp_cut, zs_full, w_exp, w_cut, att_done = (
            sem("zs_done"), sem("z_ln"), sem("sp_ready"), sem("sp_cut"),
            sem("zs_full"), sem("w_exp"), sem("w_cut"), sem("att_done"))
        att_hi, att_lo = sem("att_hi"), sem("att_lo")
        wai_loaded, bc_loaded, glu_loaded = sem("wai_loaded"), sem("bc_loaded"), sem("glu_loaded")
        s5v, s5a, s5g, s5_pads, s5_turned, s5_mats = (
            sem("s5v"), sem("s5a"), sem("s5g"), sem("s5_pads"), sem("s5_turned"), sem("s5_mats"))
        phases_ready, bu_done, bu_free, scanned, st_ready, y5_done, y5_ready = (
            sem("phases_ready"), sem("bu_done"), sem("bu_free"), sem("scanned"), sem("st_ready"),
            sem("y5_done"), sem("y5_ready"))
        gelu_sq, gelu_u, gelu_th, glu_in, glu_done, glu_act = (
            sem("gelu_sq"), sem("gelu_u"), sem("gelu_th"), sem("glu_in"), sem("glu_done"), sem("glu_act"))
        g5_ready, g5_hi, g5_lo = sem("g5_ready"), sem("g5_hi"), sem("g5_lo")
        s5_sq, s5_u, s5_th = sem("s5_sq"), sem("s5_u"), sem("s5_th")
        tap0_ready, xc_ready, gates_done, gates_read, gx_ready, decayed, lru_q, lru_sd, hs_ready = (
            sem("tap0_ready"), sem("xc_ready"), sem("gates_done"), sem("gates_read"), sem("gx_ready"),
            sem("decayed"), sem("lru_q"), sem("lru_sd"), sem("hs_ready"))
        gfin_loaded, out_ready, stored = sem("gfin_loaded"), sem("out_ready"), sem("stored")

        def s5(n):
            return s5p[:, n, :]
        (LOGDT, DTV, LR, XDT, TH, MAG, THETA, TURN, SINH, SIN2, SIN, COS, E1, AM1, ABI, DEN, FR, FI,
         T0, T1, T2, T3) = range(22)

        def by_rows(w):
            return w.rearrange("(kt p) n -> p kt n", p=P)

        w_ab, w_cd = by_rows(t["ab_w_in"][0]), by_rows(t["cd_w_in"][0])
        w_out = [by_rows(t["ab_w_out"][0]), by_rows(t["cd_w_out"][0])]
        w_up = [by_rows(t["ffn_w_up"][n]) for n in range(2)]
        w_down = [by_rows(t["ffn_w_down"][n]) for n in range(2)]

        def plus(n, it, per):
            return n if it is None else it * per + n

        def flat(b):
            return b[:, :, :].rearrange("p a b -> p (a b)")

        def pcol(name, n):
            return params[:, COL[name] + n:COL[name] + n + 1]

        block = ctx.enter_context(nc.Block())

        @block.sync
        def _(sp):
            def load(u, src, it=None, per=0):
                if u >= RING:
                    sp.wait_ge(lo_ready, plus(u - RING + 1, it, per))
                    if it is not None:
                        sp.nop(nofuse=True)
                sp.dma_start(raw[:, u % RING, :].rearrange("p (k n) -> p k n", k=HK),
                             src).then_inc(raw_loaded[u % RING], 16)

            def in_proj(u, w, groups):
                for kind, col in groups:
                    if kind == "dt":
                        for k in range(DT_UNITS):
                            sp.wait_ge(lo_ready, u - RING + 1)
                            sp.dma_start(raw[:, u % RING, :].rearrange("p (k n) -> p k n", n=P)[:, :, 0:SSD_HEADS],
                                         w[:, k * KT // 2:(k + 1) * KT // 2, col:col + SSD_HEADS]
                                         ).then_inc(raw_loaded[u % RING], 16)
                            u += 1
                        continue
                    for k in range(PER_GROUP):
                        load(u, w[:, HK * k:HK * k + HK, col:col + COLS])
                        u += 1

            def out_proj(u, w, per):
                with sp.Fori(0, CHUNKS) as i:
                    for k in range(per):
                        load(u + k, w[:, HK * k:HK * k + HK, bass.ds(i * COLS, COLS)], i, per)

            def up_proj(u, w):
                with sp.Fori(0, UP_ITERS) as i:
                    for part in range(2):
                        for k in range(PER_GROUP):
                            load(u + part * PER_GROUP + k,
                                 w[:, HK * k:HK * k + HK, bass.ds(i * COLS + (1 - part) * DFF, COLS)],
                                 i, 2 * PER_GROUP)

            x_rows = t["x"][0].rearrange("(tt p) d -> p tt d", p=P)
            for tt in range(TT):
                sp.dma_start(res[:, tt, :], x_rows[:, tt, :]).then_inc(x_loaded, 16)
            in_proj(U_AB, w_ab, AB_GROUPS)
            out_proj(U_OUT0, w_out[0], PER_GROUP)
            up_proj(U_UP0, w_up[0])
            out_proj(U_DOWN0, w_down[0], DOWN_PER)
            in_proj(U_CD, w_cd, CD_GROUPS)
            out_proj(U_OUT1, w_out[1], PER_GROUP)
            up_proj(U_UP1, w_up[1])
            out_proj(U_DOWN1, w_down[1], DOWN_PER)

        @block.tensor
        def _(pe):
            def unit(u, it=None, per=0):
                pe.wait_ge(lo_ready, plus(u + 1, it, per))

            def half(parts, u):
                return parts[:, u % RING, :].rearrange("p (k n) -> p k n", k=HK)

            def fm_unit(u, k, a, bank0, free_lag, it=None, per=0, aper=0):
                unit(u, it, per)
                for f in range(FT):
                    if k == 0:
                        pe.wait_ge(acc_free, plus(a + f + 1 - free_lag, it, aper)) if a + f + 1 > free_lag else None
                    for kk in range(HK):
                        kt = HK * k + kk
                        cols = slice(f * P, f * P + P)
                        pe.matmul(ps[:, bank0 + f, :], half(w_hi, u)[:, kk, cols],
                                  y[:, kt, :, :].rearrange("p a b -> p (a b)"),
                                  start=kt == 0, stop=False)
                        mm = pe.matmul(ps[:, bank0 + f, 0:TOK], half(w_lo, u)[:, kk, cols], y[:, kt, 0, :],
                                       start=False, stop=kt == KT - 1)
                mm.then_inc(unit_used, 1)

            def tm_unit(u, k, per_acc, lhs, banks, it=None, per=0):
                unit(u, it, per)
                for tt in range(TT):
                    for kk in range(HK):
                        kt = HK * k + kk
                        hi = lhs[:, kt, 0, tt * P:tt * P + P]
                        lo = lhs[:, kt, 1, tt * P:tt * P + P]
                        pe.matmul(banks(tt), hi, half(w_hi, u)[:, kk, :], start=kt == 0, stop=False)
                        pe.matmul(banks(tt), hi, half(w_lo, u)[:, kk, :], start=False, stop=False)
                        mm = pe.matmul(banks(tt), lo, half(w_hi, u)[:, kk, :], start=False,
                                       stop=kt == HK * per_acc - 1)
                    if k == per_acc - 1 and tt < TT - 1:
                        mm.then_inc(acc_done, 1)
                mm.then_inc(unit_used, 1)

            def dt_units(u, a):
                for k in range(DT_UNITS):
                    unit(u + k)
                    if k == 0:
                        pe.wait_ge(acc_free, a - FT + 1)
                    for kk in range(KT // 2):
                        kt = k * KT // 2 + kk
                        w = [parts[:, (u + k) % RING, kk * P:kk * P + P] for parts in (w_hi, w_lo)]
                        pe.matmul(ps[:, a % FT, :], w[0], y[:, kt, :, :].rearrange("p a b -> p (a b)"),
                                  start=kt == 0, stop=False)
                        mm = pe.matmul(ps[:, a % FT, 0:TOK], w[1], y[:, kt, 0, :], start=False, stop=kt == KT - 1)
                    mm.then_inc(unit_used, 1)

            def out_proj(u, a, per, lhs, ready=None):
                pe.wait_ge(acc_free, a)
                with pe.Fori(0, CHUNKS) as i:
                    def banks(tt):
                        return ps[:, bass.ds(i * TT + tt, 1), :]
                    for k in range(per):
                        if ready is not None:
                            ready(k)
                        tm_unit(u + k, k, per, lhs, banks, i, per)

            def up_proj(u, a):
                pe.wait_ge(acc_free, a)
                with pe.Fori(0, UP_ITERS) as i:
                    for part in range(2):
                        for k in range(PER_GROUP):
                            fm_unit(u + part * PER_GROUP + k, k, a + part * FT, part * FT, 2 * FT,
                                    i, 2 * PER_GROUP, 2 * FT)

            def norm(n):
                pe.wait_ge(xn_ready, TT * (n + 1))
                for kt in range(KT):
                    if kt >= 4:
                        pe.wait_ge(y_lo_ready, KT * n + kt - 3)
                    for tt in range(TT):
                        mm = pe.transpose(ps[:, 4 + kt % 4, tt * P:tt * P + P], xn[:, tt, kt * P:kt * P + P], ident[:, :])
                    mm.then_inc(turned, 1)
                pe.wait_ge(y_lo_ready, KT * (n + 1))

            def turn_params():
                pe.wait_ge(consts_ready, 4)
                pe.wait_ge(rows_loaded, 16 * len(list(param_pieces())))
                for n in range(PT):
                    rows = min(P, NPARAM - n * P)
                    mm = pe.transpose(ps[:, n // 4, (n % 4) * P:(n % 4) * P + rows], prow[0:rows, n, :],
                                      ident[0:rows, 0:rows])
                mm.then_inc(rows_turned, 1)
                pe.wait_ge(params_ready, 1)

            def ssd_setup():
                pe.wait_ge(cs_ready, 1)
                for tt in range(TT):
                    pe.transpose(ps[:, 4, tt * 32:tt * 32 + SSD_HEADS], dts[:, tt * P:tt * P + P],
                                 ident[0:SSD_HEADS, 0:SSD_HEADS])
                    mm = pe.transpose(ps[:, 4, 64 + tt * 32:64 + tt * 32 + SSD_HEADS], cs[:, tt * P:tt * P + P],
                                      ident[0:SSD_HEADS, 0:SSD_HEADS])
                mm.then_inc(cs_turned, 1)
                pe.wait_ge(xact, 5)
                for n in range(TT * XT // 4):
                    tt, q = n % TT, n // TT
                    if n >= 2:
                        pe.wait_ge(xdt_ready, n - 1)
                    for j in range(4):
                        mm = pe.transpose(ps[:, 5 + n % 2, j * P:j * P + P],
                                          xbc[:, 4 * q + j, tt * P:tt * P + P], ident[:, :])
                    mm.then_inc(x_turned, 1)

            def ssd_group(g):
                if g == 0:
                    pe.wait_ge(cs_t_ready, 1)
                    pe.wait_ge(xdt_ready, 6)
                else:
                    pe.wait_ge(m_ready, RH * g)
                b, c = xbc[:, XT + g, :], xbc[:, XT + SSD_GROUPS + g, :]
                pe.matmul(ps[:, 4, 0:TOK], b[:, 0:P], c, start=True, stop=True, skip_group_check=True)
                pe.matmul(ps[:, 4, TOK:TOK + P], b[:, P:TOK], c[:, P:TOK], start=False, stop=True,
                          skip_group_check=True).then_inc(cb_done, 1)
                for pair in range(RH // 2):
                    n = g * RH // 2 + pair
                    if n >= 1:
                        pe.wait_ge(decay_ready, 2 * n)
                    for j in range(2):
                        h = 2 * n + j
                        mm = pe.matmul(ps[:, 5, j * TOK:j * TOK + TOK],
                                       ident[0:SSD_HEADS, h:h + 1].broadcast_to([SSD_HEADS, P]), cs[:, :],
                                       start=j == 0, stop=True, skip_group_check=True)
                    mm.then_inc(cs_spread, 1)
                    if n >= 2:
                        pe.wait_ge(ys_ready, n - 1)
                    for j in range(2):
                        h = 2 * n + j
                        pe.wait_ge(m_ready, h + 1)
                        o = ps[j * SSD_P:(j + 1) * SSD_P, 6 + n % 2, 0:TOK]
                        pe.matmul(o, xdt[:, 0, h * SSD_P:(h + 1) * SSD_P], blk[h % 2][:, 0:2, :].rearrange("p a b -> p (a b)"),
                                  start=True, stop=False)
                        mm = pe.matmul(o[:, P:TOK], xdt[:, 1, h * SSD_P:(h + 1) * SSD_P], blk[h % 2][:, 2, :],
                                       start=False, stop=True)
                    mm.then_inc(yh_done, 1)

            def ssd_norm():
                for n in range(XT):
                    pe.wait_ge(sq_ready, n + 1)
                    mm = pe.matmul(ps[:, 4, 0:TOK], ones[:, :], tmp[:, n % FT, :], start=n == 0, stop=n == XT - 1)
                    mm.then_inc(sq_summed, 1)

            def attention():
                pe.wait_ge(acc_free, A_OUT0)
                pe.wait_ge(gn_ms, 1)
                for h in range(SB_HEADS):
                    q, k = qk[:, h, :], qk[:, SB_HEADS + h, :]
                    zb = 4 + h % 2
                    if h >= 2:
                        pe.wait_ge(w_exp, h - 1)
                    pe.matmul(ps[:, zb, 0:TOK], k[:, 0:P], q, start=True, stop=False, skip_group_check=True)
                    pe.matmul(ps[:, zb, TOK:TOK + P], k[:, P:TOK], q[:, P:TOK], start=False, stop=False,
                              skip_group_check=True).then_inc(zs_done, 1)
                    pe.wait_ge(sp_cut, h + 1)
                    pe.matmul(ps[:, zb, 0:TOK], neg_tri[:, :], blk[2][:, 0:2, :].rearrange("p a b -> p (a b)"),
                              start=False, stop=False, skip_group_check=True)
                    pe.matmul(ps[:, zb, P:TOK], neg_ones[:, :], blk[2][:, 2, :], start=False, stop=False,
                              skip_group_check=True)
                    pe.matmul(ps[:, zb, TOK:TOK + P], neg_tri[:, :], blk[2][:, 2, :], start=False, stop=True,
                              skip_group_check=True).then_inc(zs_full, 1)
                    pe.wait_ge(w_cut, h + 1)
                    if h >= 2:
                        pe.wait_ge(att_lo, h - 1)
                    o = ps[:, 6 + h % 2, 0:TOK]
                    pe.matmul(o, v_t[:, 0, h * SB_DH:(h + 1) * SB_DH], blk[3][:, 0:2, :].rearrange("p a b -> p (a b)"),
                              start=True, stop=False)
                    pe.matmul(o[:, P:TOK], v_t[:, 1, h * SB_DH:(h + 1) * SB_DH], blk[3][:, 2, :],
                              start=False, stop=True).then_inc(att_done, 1)

            def mix0():
                u, a = U_AB, A_AB
                for kind, _ in AB_GROUPS:
                    if kind == "dt":
                        dt_units(u, a)
                        u, a = u + DT_UNITS, a + 1
                    elif kind == "v":
                        pe.wait_ge(acc_free, a - 2)
                        for k in range(PER_GROUP):
                            tm_unit(u + k, k, PER_GROUP, y, lambda tt: ps[:, (a + tt) % FT, :])
                        u, a = u + PER_GROUP, a + TT
                    else:
                        bank = [(a + f) % FT for f in range(FT)]
                        for k in range(PER_GROUP):
                            fm_rot(u + k, k, a, bank)
                        u, a = u + PER_GROUP, a + FT
                ssd_setup()
                for g in range(SSD_GROUPS):
                    ssd_group(g)
                ssd_norm()
                attention()

            def fm_rot(u, k, a, bank):
                unit(u)
                for f in range(FT):
                    if k == 0 and a + f + 1 > FT:
                        pe.wait_ge(acc_free, a + f + 1 - FT)
                    for kk in range(HK):
                        kt = HK * k + kk
                        cols = slice(f * P, f * P + P)
                        pe.matmul(ps[:, bank[f], :], half(w_hi, u)[:, kk, cols],
                                  y[:, kt, :, :].rearrange("p a b -> p (a b)"), start=kt == 0, stop=False)
                        mm = pe.matmul(ps[:, bank[f], 0:TOK], half(w_lo, u)[:, kk, cols], y[:, kt, 0, :],
                                       start=False, stop=kt == KT - 1)
                    if k == PER_GROUP - 1 and f < FT - 1:
                        mm.then_inc(acc_done, 1)
                mm.then_inc(unit_used, 1)

            def s5_turn():
                pe.wait_ge(s5_pads, 2)
                for ri in range(2):
                    for q in range(UT):
                        mm = pe.transpose(ps[:, 4 + ri, q * P:q * P + P],
                                          b_pad[:, ri, 4 * q:4 * q + 4, :, :].rearrange("p a b c -> p (a b c)"),
                                          ident[:, :])
                for ri in range(2):
                    for q in range(UT):
                        mm = pe.transpose(ps[:, 6 + ri, q * P:q * P + P],
                                          c_pad[:, ri, q, :, :].rearrange("p a b -> p (a b)"), ident[:, :])
                mm.then_inc(s5_turned, 1)

            def gates(g, tiles):
                if tiles[0] == 0:
                    pe.wait_ge(wai_loaded, 32 * (g + 1))
                    pe.wait_ge(xc_ready, g + 1)
                for f in tiles:
                    if FT * g + f >= 2:
                        pe.wait_ge(gates_read, FT * g + f - 1)
                    pe.matmul(ps[:, 4 + f % 2, 0:TOK], wai[:, 0, f, :], cv[:, f, :], start=True, stop=True,
                              skip_group_check=True)
                    pe.matmul(ps[:, 4 + f % 2, TOK:2 * TOK], wai[:, 1, f, :], cv[:, f, :], start=False, stop=True,
                              skip_group_check=True).then_inc(gates_done, 1)

            def s5_in(j):
                q, jj = j // 4, j % 4
                rows = slice(32 * jj, 32 * jj + 32)
                if j == 0:
                    pe.wait_ge(s5_mats, 2)
                    pe.wait_ge(acc_free, A_CD + FT)
                else:
                    pe.wait_ge(bu_free, j)
                for ri in range(2):
                    mm = pe.matmul(ps[:, 6, ri * TOK:ri * TOK + TOK], bb[rows, ri, q, :], ut[rows, q, :],
                                   start=ri == 0, stop=True, skip_group_check=True)
                mm.then_inc(bu_done, 1)

            def s5_out(j):
                q, jj = j // 4, j % 4
                rows = slice(32 * jj, 32 * jj + 32)
                pe.wait_ge(st_ready, j + 1)
                if q and jj == 0:
                    pe.wait_ge(y5_ready, q)
                for ri in range(2):
                    mm = pe.matmul(ps[rows, 7, 0:TOK], cc[:, ri, q, rows], st[:, j % 2, ri, :],
                                   start=ri == 0, stop=ri == 1)
                mm.then_inc(y5_done, 1)

            def glu():
                pe.wait_ge(glu_in, 1)
                pe.wait_ge(glu_loaded, 16)
                for f in range(UT):
                    for k in range(UT):
                        mm = pe.matmul(ps[:, 4 + f, 0:TOK], w_glu[:, k, f * P:f * P + P], ut[:, k, :],
                                       start=k == 0, stop=k == UT - 1)
                    mm.then_inc(glu_done, 1)

            def cd_step(m):
                if m == 2:
                    s5_turn()
                for j, at_ in enumerate(S5_AT):
                    if m == at_ + S5_OUT:
                        s5_out(j)
                    if m == at_:
                        s5_in(j)
                for g, at_ in enumerate(LRU_AT):
                    if m == at_ + 5:
                        gates(g, (0, 1))
                    if m == at_ + 6:
                        gates(g, (2, 3))

            def mix_cd():
                pe.wait_ge(acc_free, A_CD)
                for n in range(len(CD_GROUPS)):
                    a = A_CD + FT * n
                    for k in range(PER_GROUP):
                        m = PER_GROUP * n + k
                        fm_rot(U_CD + m, k, a, [(a + f) % FT for f in range(FT)])
                        cd_step(m)
                glu()

            def ab_ready(k):
                kt = HK * k + HK
                if kt <= SB_HEADS:
                    pe.wait_ge(att_lo, kt)
                else:
                    pe.wait_ge(o_lo, kt - SB_HEADS)

            def cd_ready(k):
                kt = HK * k + HK
                if kt <= LT:
                    pe.wait_ge(o_lo, XT + kt)
                else:
                    pe.wait_ge(g5_lo, kt - LT)

            turn_params()
            norm(0)
            mix0()
            out_proj(U_OUT0, A_OUT0, PER_GROUP, cat, ab_ready)
            norm(1)
            up_proj(U_UP0, A_UP0)
            pe.wait_ge(ffn_lo, UP_ITERS)
            out_proj(U_DOWN0, A_DOWN0, DOWN_PER, hff)
            norm(2)
            mix_cd()
            out_proj(U_OUT1, A_OUT1, PER_GROUP, cat, cd_ready)
            norm(3)
            up_proj(U_UP1, A_UP1)
            pe.wait_ge(ffn_lo, 2 * UP_ITERS)
            out_proj(U_DOWN1, A_DOWN1, DOWN_PER, hff)

        @block.scalar
        def _(act):
            chain = [0]

            def link(ins):
                chain[0] += 1
                ins.then_inc(a_chain, 1)
                act.wait_ge(a_chain, chain[0])

            def split(u, it=None, per=0):
                if u >= U_END and it is None:
                    return
                act.wait_ge(raw_loaded[u % RING], plus(16 * (u // RING + 1), it, 16 * per // RING))
                if u >= RING:
                    act.wait_ge(unit_used, plus(u - RING + 1, it, per))
                act.activation(w_hi[:, u % RING, :], raw[:, u % RING, :], ACT.Copy).then_inc(hi_ready, 1)

            def out_proj(u, per, last=False):
                n = CHUNKS - 1 if last else CHUNKS
                with act.Fori(0, n) as i:
                    for k in range(per):
                        split(u + k + RING, i, per)
                if last:
                    for k in range(per - RING):
                        split(u + n * per + k + RING)

            def up_proj(u, a, layer):
                done = UP_ITERS * layer
                with act.Fori(0, UP_ITERS) as i:
                    for k in range(PER_GROUP - 1):
                        split(u + k + RING, i, 2 * PER_GROUP)
                    act.wait_ge(unit_used, i * 2 * PER_GROUP + (u + PER_GROUP))
                    act.activation(tmp[:, :, :], ps[:, 0:FT, TOK:2 * TOK], ACT.Copy).then_inc(half_copied, 1)
                    split(u + PER_GROUP - 1 + RING, i, 2 * PER_GROUP)
                    act.wait_ge(ffn_conv, i + (done + 1))
                    act.activation(cv[:, :, :], cv[:, :, :], ACT.Silu).then_inc(ffn_act, 1)
                    for k in range(PER_GROUP, 2 * PER_GROUP - 1):
                        split(u + k + RING, i, 2 * PER_GROUP)
                    act.wait_ge(unit_used, i * 2 * PER_GROUP + (u + 2 * PER_GROUP))
                    act.activation(ffn_tv[:, :, :], ps[:, FT:2 * FT, TOK:2 * TOK], ACT.Copy).then_inc(half_copied, 1)
                    split(u + 2 * PER_GROUP - 1 + RING, i, 2 * PER_GROUP)
                    act.wait_ge(ffn_h, i + (done + 1))
                    act.activation(hff[:, bass.ds(i * FT, FT), 0, :], ffn_v[:, :, :], ACT.Copy).then_inc(ffn_hi, 1)

            def norm(n):
                if n == 0:
                    act.wait_ge(x_loaded, 32)
                else:
                    act.wait_ge(acc_free, A_NORM[n])
                act.activation(xn[:, 0, :], res[:, 0, :], ACT.Square, accum_out=tiny[:, 0:1]).then_inc(ssq_ready, 1)
                act.wait_ge(ms_ready, n + 1)
                act.activation(tiny[:, 4:6], tiny[:, 2:4], ACT.Sqrt).then_inc(sd_ready, 1)
                act.wait_ge(rstd_ready, n + 1)
                act.activation(xn[:, 0, :], res[:, 0, :], ACT.Copy, scale=tiny[:, 6:7]).then_inc(xn_ready, 1)
                if n == 4:
                    return
                if n == 0:
                    act.wait_ge(params_ready, 1)
                name = ("norm_mix", "norm_ffn")[n % 2]
                for kt in range(KT):
                    act.wait_ge(turned, KT * n + kt + 1)
                    act.activation(y[:, kt, 0, :], ps[:, 4 + kt % 4, 0:TOK], ACT.Copy,
                                   scale=pcol(name, KT * (n // 2) + kt)).then_inc(y_hi_ready, 1)

            def param_loads():
                for name, r, tile, p, m in param_pieces():
                    src = t[name]
                    dims = " ".join("abc"[:len(src.shape)])
                    flat = src.rearrange(f"{dims} -> ({dims})").rearrange("(r p) -> r p", p=P)
                    act.dma_start(prow[p:p + m, tile, :], flat[r:r + m, :]).then_inc(rows_loaded, 16)
                act.dma_start(tiny[0:SSD_HEADS, 16:17], t["ab_dt_bias"].rearrange("a h -> h a")).then_inc(small_loaded, 16)
                act.dma_start(tiny[0:SSD_HEADS, 17:18], t["ab_a_log"].rearrange("a h -> h a")).then_inc(small_loaded, 16)
                heads = t["ab_d_skip"].rearrange("a (t j) -> a j t", j=2)
                steps = t["cd_log_dt"].rearrange("a (t j) -> a j t", j=2)
                with nc.allow_non_contiguous_dma(reason="two small vectors, once"):
                    for j in range(2):
                        act.dma_start(tiny[j * 64:j * 64 + 64, 20:20 + XT],
                                      heads[0, j:j + 1, :].broadcast_to([64, XT])).then_inc(small_loaded, 16)
                        act.dma_start(s5p[j * 64:j * 64 + 64, LOGDT, :],
                                      steps[0, j:j + 1, :].broadcast_to([64, ST])).then_inc(small_loaded, 16)

            def conv_silu(g):
                act.wait_ge(xconv, g + 1)
                act.activation(xbc[:, FT * g:FT * g + FT, :], cv[:, :, :], ACT.Silu).then_inc(xact, 1)

            def dt_path():
                act.wait_ge(small_loaded, 96)
                act.activation(tiny[0:SSD_HEADS, 18:19], tiny[0:SSD_HEADS, 17:18], ACT.Exp).then_inc(dt_a, 1)
                act.wait_ge(dt_abs, 1)
                act.activation(cv[0:SSD_HEADS, 1, :], cv[0:SSD_HEADS, 1, :], ACT.Exp, scale=-1.0).then_inc(dt_exp, 1)
                act.wait_ge(dt_w, 1)
                act.activation(cv[0:SSD_HEADS, 3, :], cv[0:SSD_HEADS, 2, :], ACT.Ln).then_inc(dt_ln, 1)

            def decays():
                act.wait_ge(cs_t_ready, 1)
                for h in range(SSD_HEADS):
                    act.wait_ge(cs_spread, h // 2 + 1)
                    if h >= 2:
                        act.wait_ge(m_ready, h - 1)
                    j = h % 2
                    b = flat(blk[2 + j])
                    act.activation(b[:, 0:TOK], ps[:, 5, j * TOK:j * TOK + TOK], ACT.Relu, scale=-1.0,
                                   bias=cs_t[:, 0, h:h + 1])
                    link(act.activation(b[:, TOK:3 * P], ps[:, 5, j * TOK + P:j * TOK + TOK], ACT.Relu, scale=-1.0,
                                        bias=cs_t[:, 1, h:h + 1]))
                    act.activation(b, b, ACT.Exp, scale=-1.0).then_inc(decay_ready, 1)

            def gated_norm():
                act.wait_ge(gn_ms, 1)
                act.activation(cv[:, 0, :], cv[:, 0, :], ACT.Sqrt).then_inc(gn_sd, 1)
                for n in range(XT):
                    act.wait_ge(o_ready, n + 1)
                    act.activation(cat[:, SB_HEADS + n, 0, :], tmp[:, n % FT, :], ACT.Copy).then_inc(o_hi, 1)

            def attention():
                for h in range(SB_HEADS):
                    zb = 4 + h % 2
                    act.wait_ge(zs_done, h + 1)
                    if h >= 1:
                        act.wait_ge(sp_ready, h)
                    z = ps[:, zb, 0:3 * P]
                    b = flat(blk[0])
                    link(act.activation(b, z, ACT.Abs))
                    link(act.activation(b, b, ACT.Exp, scale=-1.0))
                    act.activation(b, b, ACT.Ln, bias=1.0).then_inc(z_ln, 1)
                    act.wait_ge(zs_full, h + 1)
                    if h >= 1:
                        act.wait_ge(w_cut, h)
                    act.activation(flat(blk[1]), z, ACT.Exp).then_inc(w_exp, 1)
                    act.wait_ge(att_done, h + 1)
                    act.activation(cat[:, h, 0, :], ps[:, 6 + h % 2, 0:TOK], ACT.Copy).then_inc(att_hi, 1)

            def group(kind, u, a, d, step=None):
                per = DT_UNITS if kind == "dt" else PER_GROUP
                for k in range(per):
                    if k == per - 1 and kind != "v":
                        for f in range(1 if kind == "dt" else FT):
                            if kind == "dt" or f == FT - 1:
                                act.wait_ge(unit_used, u + per)
                            else:
                                act.wait_ge(acc_done, d + f + 1)
                            act.activation(tmp[:, (a + f) % FT, :], ps[:, (a + f) % FT, TOK:2 * TOK], ACT.Copy,
                                           scale=SB_DH ** -0.5 if kind == "q" else 1.0).then_inc(half_copied, 1)
                    split(u + k + RING)
                    if step is not None:
                        step(k)
                return u + per, a + {"dt": 1, "v": TT}.get(kind, FT), d + D_OF.get(kind, FT - 1)

            def mix0():
                u, a, d = U_AB, A_AB, D_AB
                n_x = n_z = 0
                for kind, _ in AB_GROUPS:
                    u, a, d = group(kind, u, a, d)
                    if kind == "x":
                        conv_silu(n_x)
                        n_x += 1
                    elif kind == "dt":
                        dt_path()
                    elif kind in "qkv":
                        s5_prep("qkv".index(kind))
                    elif kind == "z":
                        act.wait_ge(acc_free, a)
                        act.activation(zg[:, FT * n_z:FT * n_z + FT, :],
                                       zg[:, FT * n_z:FT * n_z + FT, :], ACT.Silu).then_inc(z_act, 1)
                        n_z += 1
                decays()
                gated_norm()
                attention()

            def s5_prep(stage):
                if stage == 0:
                    act.wait_ge(small_loaded, 96)
                    act.activation(s5(DTV), s5(LOGDT), ACT.Exp).then_inc(s5a, 1)
                elif stage == 1:
                    act.wait_ge(s5v, 1)
                    act.activation(s5(TH), s5(XDT), ACT.Tanh, scale=0.5)
                    act.activation(s5(MAG), s5(XDT), ACT.Exp)
                    act.activation(s5(SINH), s5(TURN), ACT.Sin, scale=0.5)
                    act.activation(s5(SIN), s5(TURN), ACT.Sin).then_inc(s5a, 1)
                    lam = params[:, COL["cd_lambda"]:COL["cd_lambda"] + LT]
                    link(act.activation(tiny[:, 32:44], lam, ACT.Abs))
                    act.activation(s5p[:, T0, 0:LT], tiny[:, 32:44], ACT.Exp, scale=-1.0).then_inc(s5a, 1)
                else:
                    act.wait_ge(s5v, 2)
                    act.activation(s5p[:, T1, 0:LT], s5p[:, T2, 0:LT], ACT.Ln).then_inc(s5a, 1)

            def bc_loads():
                for ri, name in enumerate(("cd_b_re", "cd_b_im")):
                    act.dma_start(b_raw[:, ri, :, :], t[name][0].rearrange("(j g) n c -> (g n) j c", g=2)
                                  ).then_inc(bc_loaded, 16)
                for ri, name in enumerate(("cd_c_re", "cd_c_im")):
                    for gl in range(2):
                        act.dma_start(c_pad[:, ri, :, gl, :], t[name][0].rearrange("g c n -> (g c) n").rearrange(
                            "(q p) n -> p q n", p=P)).then_inc(bc_loaded, 16)

            def load_gate_weights(g):
                for m, name in enumerate(("cd_w_a", "cd_w_i")):
                    act.dma_start(wai[:, m, :, :], t[name][0, FT * g:FT * g + FT].rearrange("b i j -> i b j")
                                  ).then_inc(wai_loaded, 16)

            def gate_sigmoids(g, tiles):
                for f in tiles:
                    n = FT * g + f
                    act.wait_ge(gates_done, n + 1)
                    act.activation(lru_r[:, f, :], ps[:, 4 + f % 2, 0:TOK], ACT.Sigmoid, bias=pcol("cd_b_a", n))
                    act.activation(lru_i[:, f, :], ps[:, 4 + f % 2, TOK:2 * TOK], ACT.Sigmoid,
                                   bias=pcol("cd_b_i", n)).then_inc(gates_read, 1)

            def lru_decay(g):
                act.wait_ge(gates_read, FT * (g + 1))
                for f in range(FT):
                    n = FT * g + f
                    ins = act.activation(hs[:, n, :], lru_r[:, f, :], ACT.Exp, scale=c8[:, n:n + 1])
                link(ins)
                for f in range(FT):
                    n = FT * g + f
                    act.activation(lru_r[:, f, :], lru_r[:, f, :], ACT.Tanh, scale=c8[:, n:n + 1])
                act.wait_ge(gx_ready, g + 1)
                act.activation(lru_i[:, :, :], hs[:, FT * g:FT * g + FT, :], ACT.Square).then_inc(decayed, 1)

            def cd_step(m):
                for g, at_ in enumerate(LRU_AT):
                    if m == at_ + 2:
                        if g:
                            act.wait_ge(hs_ready, FT * g)
                        act.wait_ge(acc_free, A_CD + FT * (g + 2))
                        for f in range(FT):
                            n = FT * g + f
                            ins = act.activation(cv[:, f, :], xin[:, f, :], ACT.Identity, bias=pcol("cd_conv_b", n),
                                                 scale=pcol("cd_conv_w", (LRU_CONV - 1) * LT + n))
                        ins.then_inc(tap0_ready, 1)
                    if m == at_ + 5:
                        gate_sigmoids(g, (0, 1))
                    if m == at_ + 6:
                        gate_sigmoids(g, (2, 3))
                        if g + 1 < LT // FT:
                            load_gate_weights(g + 1)
                    if m == at_ + 7:
                        lru_decay(g)
                    if m == at_ + 8:
                        act.wait_ge(lru_q, g + 1)
                        act.activation(lru_r[:, :, :], lru_r[:, :, :], ACT.Sqrt, scale=-1.0).then_inc(lru_sd, 1)
                for g, at_ in enumerate(GATE_AT):
                    if m == at_ + 2:
                        if g == 0:
                            act.wait_ge(hs_ready, LT)
                            act.dma_start(w_glu[:, :, :], t["cd_w_glu"][0].rearrange("(k p) n -> p k n", p=P)
                                          ).then_inc(glu_loaded, 16)
                        act.wait_ge(acc_free, A_CD + FT * (g + 5))
                        act.activation(cv[:, :, :], xin[:, :, :], ACT.Square).then_inc(gelu_sq, 1)
                    if m == at_ + 3:
                        act.wait_ge(gelu_u, g + 1)
                        act.activation(cv[:, :, :], cv[:, :, :], ACT.Tanh, scale=GELU_C).then_inc(gelu_th, 1)
                    if m == at_ + 5:
                        for f in range(FT):
                            act.wait_ge(o_ready, XT + FT * g + f + 1)
                            act.activation(cat[:, FT * g + f, 0, :], xin[:, f, :], ACT.Copy).then_inc(o_hi, 1)
                if m == S5_AT[-1] + S5_OUT + 2:
                    act.wait_ge(y5_ready, UT)
                    act.activation(s5_gelu[:, :, :], ut[:, :, :], ACT.Square).then_inc(s5_sq, 1)
                if m == S5_AT[-1] + S5_OUT + 3:
                    act.wait_ge(s5_u, 1)
                    act.activation(s5_gelu[:, :, :], s5_gelu[:, :, :], ACT.Tanh, scale=GELU_C).then_inc(s5_th, 1)

            def mix_cd():
                u, a, d = U_CD, A_CD, D_CD
                for n, (kind, _) in enumerate(CD_GROUPS):
                    u, a, d = group(kind, u, a, d, lambda k: cd_step(PER_GROUP * n + k))
                for m in range(CD_UNITS, CD_STEPS):
                    cd_step(m)
                for f in range(UT):
                    act.wait_ge(glu_done, f + 1)
                    act.activation(s5_gate[:, f, :], ps[:, 4 + f, 0:TOK], ACT.Sigmoid,
                                   bias=pcol("cd_b_glu", f)).then_inc(glu_act, 1)
                for f in range(UT):
                    act.wait_ge(g5_ready, f + 1)
                    act.activation(cat[:, LT + f, 0, :], ut[:, f, :], ACT.Copy).then_inc(g5_hi, 1)

            param_loads()
            for n in range(RING):
                split(n)
            norm(0)
            mix0()
            out_proj(U_OUT0, PER_GROUP)
            norm(1)
            bc_loads()
            load_gate_weights(0)
            up_proj(U_UP0, A_UP0, 0)
            out_proj(U_DOWN0, DOWN_PER)
            norm(2)
            mix_cd()
            out_proj(U_OUT1, PER_GROUP)
            norm(3)
            up_proj(U_UP1, A_UP1, 1)
            out_proj(U_DOWN1, DOWN_PER, last=True)
            act.wait_ge(acc_free, A_END)
            act.dma_start(g_fin[:, :], t["norm_final"].rearrange("(a d) -> a d", a=1).broadcast_to([P, D])
                          ).then_inc(gfin_loaded, 16)
            norm(4)
            for tt in range(TT):
                act.wait_ge(out_ready, tt + 1)
                act.dma_start(out[0, tt * P:tt * P + P, :], xn[:, tt, :]).then_inc(stored, 16)
            act.wait_ge(stored, 16 * TT)

        @block.vector
        def _(dve):
            made, base_at = [0], [None]

            def mark(ins):
                made[0] += 1
                return ins.then_inc(v_chain, 1)

            def join():
                dve.wait_ge(v_chain, made[0] if base_at[0] is None else base_at[0] + made[0])

            def link(ins):
                mark(ins)
                join()

            def split(u, it=None, per=0):
                if u >= U_END and it is None:
                    return
                dve.wait_ge(hi_ready, plus(u + 1, it, per))
                dve.tensor_tensor(w_lo[:, u % RING, :], raw[:, u % RING, :], w_hi[:, u % RING, :],
                                  ALU.subtract).then_inc(lo_ready, 1)

            def out_proj(u, d, per, last=False):
                n = CHUNKS - 1 if last else CHUNKS

                def add(i, cols, banks, done):
                    for tt in range(TT):
                        if tt < TT - 1:
                            dve.wait_ge(acc_done, plus(d + done + 1, i, 1))
                        else:
                            dve.wait_ge(unit_used, plus(u + (done + 1) * per, i, per))
                        r = res[:, tt, cols]
                        dve.tensor_tensor(r, banks(tt), r, ALU.add).then_inc(acc_free, 1)

                with dve.Fori(0, n) as i:
                    for k in range(per - 1):
                        split(u + k + RING, i, per)
                    add(i, bass.ds(i * COLS, COLS), lambda tt: ps[:, bass.ds(i * TT + tt, 1), :], 0)
                    split(u + per - 1 + RING, i, per)
                if last:
                    for k in range(per - RING):
                        split(u + n * per + k + RING)
                    add(None, slice(n * COLS, D), lambda tt: ps[:, n * TT + tt, :], n)

            def up_proj(u, a, h, layer):
                done = UP_ITERS * layer
                per = 2 * PER_GROUP
                chain0 = made[0]
                with dve.Fori(0, UP_ITERS) as i:
                    base_at[0] = i * 2

                    def weight(tap, f):
                        c = COL["ffn_conv_w"] + (layer * FFN_CONV + tap) * HT + f
                        return params[:, bass.ds(i * FT + c, 1)]

                    for k in range(PER_GROUP - 1):
                        split(u + k + RING, i, per)
                    dve.wait_ge(half_copied, i * 2 + (h + 1))
                    for f in range(FT):
                        dve.tensor_tensor(ffn_g[:, f, :], ps[:, f, 0:TOK], tmp[:, f, :], ALU.add).then_inc(acc_free, 1)
                    dve.wait_ge(acc_free, i * 2 * FT + (a + FT))
                    for f in range(FT):
                        bias = params[:, bass.ds(i * FT + (COL["ffn_conv_b"] + layer * HT + f), 1)]
                        ins = dve.tensor_scalar(cv[:, f, :], ffn_g[:, f, :], weight(2, f), bias, ALU.mult, ALU.add)
                    link(ins)
                    for lag in (1, 2):
                        for f in range(FT):
                            c = cv[:, f, lag:TOK]
                            ins = dve.scalar_tensor_tensor(out=c, in0=ffn_g[:, f, 0:TOK - lag], scalar=weight(2 - lag, f),
                                                           in1=c, op0=ALU.mult, op1=ALU.add)
                        if lag == 1:
                            link(ins)
                    ins.then_inc(ffn_conv, 1)
                    for k in range(PER_GROUP - 1, per - 1):
                        split(u + k + RING, i, per)
                    dve.wait_ge(half_copied, i * 2 + (h + 2))
                    for f in range(FT):
                        dve.tensor_tensor(ffn_v[:, f, :], ps[:, FT + f, 0:TOK], ffn_tv[:, f, :], ALU.add
                                          ).then_inc(acc_free, 1)
                    dve.wait_ge(ffn_act, i + (done + 1))
                    dve.wait_ge(acc_free, i * 2 * FT + (a + 2 * FT))
                    dve.tensor_tensor(ffn_v[:, :, :], ffn_v[:, :, :], cv[:, :, :], ALU.mult).then_inc(ffn_h, 1)
                    split(u + per - 1 + RING, i, per)
                    dve.wait_ge(ffn_hi, i + (done + 1))
                    dve.tensor_tensor(hff[:, bass.ds(i * FT, FT), 1, :], ffn_v[:, :, :],
                                      hff[:, bass.ds(i * FT, FT), 0, :], ALU.subtract).then_inc(ffn_lo, 1)
                assert made[0] - chain0 == 2
                made[0] = chain0 + 2 * UP_ITERS
                base_at[0] = None

            def norm(n):
                if n == 0:
                    dve.wait_ge(x_loaded, 32)
                else:
                    dve.wait_ge(acc_free, A_NORM[n])
                link(dve.tensor_tensor_reduce(xn[:, 1, :], res[:, 1, :], res[:, 1, :], 1.0, 0.0, ALU.mult, ALU.add,
                                              accum_out=tiny[:, 1:2]))
                dve.wait_ge(ssq_ready, n + 1)
                dve.tensor_scalar(tiny[:, 2:4], tiny[:, 0:2], 1.0 / D, EPS, ALU.mult, ALU.add).then_inc(ms_ready, 1)
                dve.wait_ge(sd_ready, n + 1)
                dve.reciprocal(tiny[:, 6:8], tiny[:, 4:6]).then_inc(rstd_ready, 1)
                dve.wait_ge(rstd_ready, n + 1)
                dve.tensor_scalar(xn[:, 1, :], res[:, 1, :], tiny[:, 7:8], None, ALU.mult).then_inc(xn_ready, 1)
                if n == 4:
                    dve.wait_ge(xn_ready, TT * 5)
                    dve.wait_ge(gfin_loaded, 16)
                    for tt in range(TT):
                        dve.tensor_tensor(xn[:, tt, :], xn[:, tt, :], g_fin[:, :], ALU.mult).then_inc(out_ready, 1)
                    return
                name = ("norm_mix", "norm_ffn")[n % 2]
                for kt in range(KT):
                    dve.wait_ge(y_hi_ready, KT * n + kt + 1)
                    dve.scalar_tensor_tensor(out=y[:, kt, 1, :], in0=ps[:, 4 + kt % 4, 0:TOK],
                                             scalar=pcol(name, KT * (n // 2) + kt), in1=y[:, kt, 0, :],
                                             op0=ALU.mult, op1=ALU.subtract).then_inc(y_lo_ready, 1)

            def param_columns():
                dve.wait_ge(rows_turned, 1)
                dve.tensor_copy(params[:, 0:COLS], ps[:, 0, :])
                dve.tensor_copy(params[:, COLS:NPARAM], ps[:, 1, 0:NPARAM - COLS]).then_inc(params_ready, 1)
                dve.wait_ge(params_ready, 1)
                dve.wait_ge(consts_ready, 5)
                link(dve.reduce_sum(parity, strips.rearrange("p (k g) -> p g k", g=2), axis=mybir.AxisListType.X))

            def group(kind, u, a, d, h, dst, step=None):
                per = DT_UNITS if kind == "dt" else PER_GROUP
                for k in range(per):
                    if k == per - 1:
                        if kind == "v":
                            for tt in range(TT):
                                if tt < TT - 1:
                                    dve.wait_ge(acc_done, d + tt + 1)
                                else:
                                    dve.wait_ge(unit_used, u + per)
                                dve.tensor_copy(dst(tt), ps[:, (a + tt) % FT, :]).then_inc(acc_free, 1)
                        else:
                            for f in range(1 if kind == "dt" else FT):
                                dve.wait_ge(half_copied, h + f + 1)
                                rows = slice(0, SSD_HEADS) if kind == "dt" else slice(0, P)
                                dve.scalar_tensor_tensor(
                                    out=dst(f), in0=ps[rows, (a + f) % FT, 0:TOK],
                                    scalar=SB_DH ** -0.5 if kind == "q" else 1.0, in1=tmp[rows, (a + f) % FT, :],
                                    op0=ALU.mult, op1=ALU.add).then_inc(acc_free, 1)
                    split(u + k + RING)
                    if step is not None:
                        step(k)
                a += {"dt": 1, "v": TT}.get(kind, FT)
                d += D_OF.get(kind, FT - 1)
                h += {"dt": 1, "v": 0}.get(kind, FT)
                dve.wait_ge(acc_free, a)
                return u + per, a, d, h

            def conv(dst, src, name_w, name_b, tile0, tiles, taps, last_sem):
                for lag in range(taps):
                    for f in range(FT):
                        w = pcol(name_w, (taps - 1 - lag) * tiles + tile0 + f)
                        if lag == 0:
                            ins = dve.tensor_scalar(dst[:, f, :], src(f), w, pcol(name_b, tile0 + f),
                                                    ALU.mult, ALU.add)
                        else:
                            c = dst[:, f, lag:TOK]
                            ins = dve.scalar_tensor_tensor(out=c, in0=src(f)[:, 0:TOK - lag], scalar=w, in1=c,
                                                           op0=ALU.mult, op1=ALU.add)
                    if lag < taps - 1:
                        link(ins)
                ins.then_inc(last_sem, 1)

            def dt_path():
                c = [cv[0:SSD_HEADS, n, :] for n in range(4)]
                d, eq = dts[:, :], cs[:, :]
                dve.wait_ge(small_loaded, 96)
                link(dve.tensor_scalar(c[0], c[0], tiny[0:SSD_HEADS, 16:17], None, ALU.add))
                dve.scalar_tensor_tensor(out=c[1], in0=c[0], scalar=-1.0, in1=c[0], op0=ALU.mult, op1=ALU.max
                                         ).then_inc(dt_abs, 1)
                dve.wait_ge(dt_exp, 1)
                dve.tensor_scalar(c[2], c[1], 1.0, None, ALU.add).then_inc(dt_w, 1)
                dve.wait_ge(dt_w, 1)
                link(dve.tensor_scalar(d, c[2], -1.0, None, ALU.add))
                link(dve.tensor_scalar(eq, d, 0.0, None, ALU.is_equal))
                link(dve.tensor_tensor(d, d, eq, ALU.add))
                dve.wait_ge(dt_ln, 1)
                link(dve.reciprocal(d, d))
                link(dve.tensor_tensor(c[2], c[1], d, ALU.mult))
                link(dve.tensor_tensor(c[3], c[3], c[2], ALU.mult))
                link(dve.tensor_tensor(c[2], c[1], eq, ALU.mult))
                link(dve.tensor_tensor(c[3], c[3], c[2], ALU.add))
                link(dve.scalar_tensor_tensor(out=d, in0=c[0], scalar=0.0, in1=c[3], op0=ALU.max, op1=ALU.add))
                dve.wait_ge(dt_a, 1)
                link(dve.tensor_scalar(c[1], d, tiny[0:SSD_HEADS, 18:19], -1.0, ALU.mult, ALU.mult))
                dve.tensor_tensor_scan(eq, ones[0:SSD_HEADS, 0:1].broadcast_to([SSD_HEADS, TOK]), c[1], 0.0,
                                       ALU.mult, ALU.add).then_inc(cs_ready, 1)

            def ssd():
                dve.wait_ge(cs_turned, 1)
                dve.tensor_copy(dt_t[:, :, :], ps[:, 4, 0:64].rearrange("p (a b) -> p a b", a=TT)[:, :, 0:SSD_HEADS])
                dve.tensor_copy(cs_t[:, :, :], ps[:, 4, 64:128].rearrange("p (a b) -> p a b", a=TT)[:, :, 0:SSD_HEADS]).then_inc(cs_t_ready, 1)
                dve.wait_ge(cs_t_ready, 1)
                for n in range(TT * XT // 4):
                    tt, q = n % TT, n // TT
                    dve.wait_ge(x_turned, n + 1)
                    dve.tensor_tensor(
                        xdt[:, tt, q * COLS:(q + 1) * COLS].rearrange("p (h c) -> p h c", c=SSD_P),
                        ps[:, 5 + n % 2, :].rearrange("p (h c) -> p h c", c=SSD_P),
                        dt_t[:, tt, 8 * q:8 * q + 8].unsqueeze(2).broadcast_to([P, 8, SSD_P]),
                        ALU.mult).then_inc(xdt_ready, 1)
                for n in range(XT):
                    for h in (2 * n, 2 * n + 1):
                        dve.wait_ge(cb_done, h // RH + 1)
                        dve.wait_ge(decay_cut, h + 1)
                        if n >= 1:
                            dve.wait_ge(yh_done, n)
                        dve.tensor_tensor(flat(blk[h % 2]), ps[:, 4, 0:3 * P], flat(blk[2 + h % 2]),
                                          ALU.mult).then_inc(m_ready, 1)
                    if n >= 1:
                        skip_and_gate(n - 1)
                skip_and_gate(XT - 1)
                join()
                for n in range(XT):
                    if n >= FT:
                        dve.wait_ge(sq_summed, n - FT + 1)
                    dve.tensor_tensor(tmp[:, n % FT, :], xbc[:, n, :], xbc[:, n, :], ALU.mult).then_inc(sq_ready, 1)
                dve.wait_ge(sq_summed, XT)
                dve.tensor_scalar(cv[:, 0, :], ps[:, 4, 0:TOK], 1.0 / SSD_W, EPS, ALU.mult, ALU.add).then_inc(gn_ms, 1)
                dve.wait_ge(gn_sd, 1)
                link(dve.reciprocal(cv[:, 1, :], cv[:, 0, :]))
                for n in range(XT + 1):
                    if n < XT:
                        dve.scalar_tensor_tensor(out=tmp[:, n % FT, :], in0=xbc[:, n, :], scalar=pcol("ab_ssd_norm", n),
                                                 in1=cv[:, 1, :], op0=ALU.mult, op1=ALU.mult).then_inc(o_ready, 1)
                    if n >= 1:
                        dve.wait_ge(o_hi, n)
                        dve.tensor_tensor(cat[:, SB_HEADS + n - 1, 1, :], tmp[:, (n - 1) % FT, :],
                                          cat[:, SB_HEADS + n - 1, 0, :], ALU.subtract).then_inc(o_lo, 1)

            def skip_and_gate(n):
                dve.wait_ge(yh_done, n + 1)
                dve.scalar_tensor_tensor(out=xbc[:, n, :], in0=xbc[:, n, :], scalar=tiny[:, 20 + n:21 + n],
                                         in1=ps[:, 6 + n % 2, 0:TOK], op0=ALU.mult, op1=ALU.add).then_inc(ys_ready, 1)
                dve.wait_ge(ys_ready, n + 1)
                if n == 0:
                    dve.wait_ge(z_act, 3)
                mark(dve.tensor_tensor(xbc[:, n, :], xbc[:, n, :], zg[:, n, :], ALU.mult))

            def attention():
                for h in range(SB_HEADS):
                    dve.wait_ge(z_ln, h + 1)
                    if h >= 1:
                        dve.wait_ge(zs_full, h)
                    dve.scalar_tensor_tensor(out=flat(blk[2]), in0=ps[:, 4 + h % 2, 0:3 * P], scalar=0.0,
                                             in1=flat(blk[0]), op0=ALU.max, op1=ALU.add).then_inc(sp_ready, 1)
                    dve.wait_ge(att_hi, h + 1)
                    dve.tensor_tensor(cat[:, h, 1, :], ps[:, 6 + h % 2, 0:TOK], cat[:, h, 0, :],
                                      ALU.subtract).then_inc(att_lo, 1)

            def mix0():
                u, a, d, h = U_AB, A_AB, D_AB, H_AB
                n_x = n_z = 0
                for kind, _ in AB_GROUPS:
                    dst = {
                        "x": lambda f: xbc[:, FT * n_x + f, :],
                        "dt": lambda f: cv[0:SSD_HEADS, 0, :],
                        "q": lambda f: qk[:, f, :],
                        "k": lambda f: qk[:, SB_HEADS + f, :],
                        "v": lambda tt: v_t[:, tt, :],
                        "z": lambda f: zg[:, FT * n_z + f, :],
                    }[kind]
                    if kind == "dt":
                        dve.wait_ge(xact, 5)
                    u, a, d, h = group(kind, u, a, d, h, dst)
                    if kind == "x":
                        if n_x:
                            dve.wait_ge(xact, n_x)
                        conv(cv, lambda f: xbc[:, FT * n_x + f, :], "ab_conv_w", "ab_conv_b", FT * n_x, 20,
                             SSD_CONV, xconv)
                        n_x += 1
                    elif kind == "dt":
                        dt_path()
                    elif kind in "qkv":
                        s5_prep("qkv".index(kind))
                    elif kind == "z":
                        n_z += 1
                ssd()
                attention()

            def tt_(o, a, b, op):
                link(dve.tensor_tensor(o, a, b, op))

            def ts_(o, a, x, op, x2=None, op2=None):
                if op2 is None:
                    link(dve.tensor_scalar(o, a, x, None, op))
                else:
                    link(dve.tensor_scalar(o, a, x, x2, op, op2))

            def s5_prep(stage):
                (s5_angles, lru_rates, s5_factors)[stage]()

            def s5_angles():
                li = params[:, COL["cd_a_im"]:COL["cd_a_im"] + ST]
                dve.wait_ge(s5a, 1)
                ts_(s5(LR), params[:, COL["cd_a_re"]:COL["cd_a_re"] + ST], -1e-4, ALU.min)
                tt_(s5(XDT), s5(LR), s5(DTV), ALU.mult)
                tt_(s5(THETA), li, s5(DTV), ALU.mult)
                ts_(s5(T0), s5(THETA), 0.15915494309189535, ALU.mult)
                ts_(s5(T0), s5(T0), ROUND, ALU.add)
                ts_(s5(T0), s5(T0), -ROUND, ALU.add)
                src = s5(THETA)
                for part in TWO_PI:
                    link(dve.scalar_tensor_tensor(out=s5(TURN), in0=s5(T0), scalar=-part, in1=src,
                                                  op0=ALU.mult, op1=ALU.add))
                    src = s5(TURN)
                dve.tensor_scalar(s5(TURN), s5(TURN), 3.1415925, -3.1415925, ALU.min, ALU.max).then_inc(s5v, 1)

            def lru_rates():
                lam = params[:, COL["cd_lambda"]:COL["cd_lambda"] + LT]
                dve.wait_ge(s5a, 3)
                e, w, t3, eq, low = (s5p[:, n, 0:LT] for n in (T0, T2, T3, FR, FI))
                dve.tensor_scalar(w, e, 1.0, None, ALU.add).then_inc(s5v, 1)
                dve.wait_ge(s5v, 2)
                ts_(t3, w, -1.0, ALU.add)
                ts_(eq, t3, 0.0, ALU.is_equal)
                tt_(t3, t3, eq, ALU.add)
                link(dve.reciprocal(t3, t3))
                tt_(t3, e, t3, ALU.mult)
                tt_(eq, e, eq, ALU.mult)
                ts_(low, lam, -1.0, ALU.mult, 0.0, ALU.max)

            def s5_factors():
                li = params[:, COL["cd_a_im"]:COL["cd_a_im"] + ST]
                ln, t3, eq, low = (s5p[:, n, 0:LT] for n in (T1, T3, FR, FI))
                dve.wait_ge(s5a, 4)
                tt_(ln, ln, t3, ALU.mult)
                tt_(ln, ln, eq, ALU.add)
                tt_(ln, ln, low, ALU.add)
                ts_(c8[:, :], ln, -LRU_C, ALU.mult)
                tt_(s5(SIN2), s5(SINH), s5(SINH), ALU.mult)
                dve.tensor_scalar(s5(COS), s5(SIN2), -2.0, 1.0, ALU.mult, ALU.add).then_inc(s5v, 1)
                dve.wait_ge(s5v, 3)
                ts_(s5(T2), s5(TH), -1.0, ALU.mult, 1.0, ALU.add)
                link(dve.reciprocal(s5(T2), s5(T2)))
                tt_(s5(E1), s5(TH), s5(T2), ALU.mult)
                ts_(s5(E1), s5(E1), 2.0, ALU.mult)
                tt_(s5(AM1), s5(E1), s5(COS), ALU.mult)
                link(dve.scalar_tensor_tensor(out=s5(AM1), in0=s5(SIN2), scalar=-2.0, in1=s5(AM1),
                                              op0=ALU.mult, op1=ALU.add))
                tt_(s5(ABI), s5(MAG), s5(SIN), ALU.mult)
                tt_(s5(DEN), s5(LR), s5(LR), ALU.mult)
                tt_(s5(T2), li, li, ALU.mult)
                tt_(s5(DEN), s5(DEN), s5(T2), ALU.add)
                tt_(s5(T2), s5(AM1), s5(LR), ALU.mult)
                tt_(s5(T3), s5(ABI), li, ALU.mult)
                tt_(s5(T2), s5(T2), s5(T3), ALU.add)
                link(dve.reciprocal(s5(DEN), s5(DEN)))
                tt_(s5(FR), s5(T2), s5(DEN), ALU.mult)
                tt_(s5(T2), s5(ABI), s5(LR), ALU.mult)
                tt_(s5(T3), s5(AM1), li, ALU.mult)
                tt_(s5(T2), s5(T2), s5(T3), ALU.subtract)
                tt_(s5(FI), s5(T2), s5(DEN), ALU.mult)

            def s5_inputs():
                dve.wait_ge(bc_loaded, 96)
                dve.wait_ge(s5g, 1)
                fr = s5(FR).unsqueeze(2).broadcast_to([P, ST, S5_CH])
                fi = s5(FI).unsqueeze(2).broadcast_to([P, ST, S5_CH])
                for ri, op in enumerate((ALU.subtract, ALU.add)):
                    mark(dve.tensor_tensor(b_tmp[:, 0, :, :], b_raw[:, ri, :, :], fr, ALU.mult))
                    tt_(b_tmp[:, 1, :, :], b_raw[:, 1 - ri, :, :], fi, ALU.mult)
                    for gl in range(2):
                        rows = slice(64 * gl, 64 * gl + 64)
                        ins = dve.tensor_tensor(b_pad[rows, ri, :, gl, :], b_tmp[rows, 0, :, :], b_tmp[rows, 1, :, :], op)
                    if ri:
                        ins.then_inc(s5_pads, 1)
                    else:
                        link(ins)
                for gl in range(2):
                    dve.tensor_scalar(c_pad[:, 0, :, gl, :], c_pad[:, 0, :, gl, :], parity[:, gl:gl + 1], None, ALU.mult)
                    ins = dve.tensor_scalar(c_pad[:, 1, :, gl, :], c_pad[:, 1, :, gl, :], parity[:, gl:gl + 1], -1.0,
                                            ALU.mult, ALU.mult)
                ins.then_inc(s5_pads, 1)

            def s5_matrices():
                dve.wait_ge(s5_turned, 1)
                for ri in range(2):
                    dve.tensor_copy(bb[:, ri, :, :], ps[:, 4 + ri, :].rearrange("p (q n) -> p q n", n=P))
                    dve.tensor_copy(cc[:, ri, :, :], ps[:, 6 + ri, :].rearrange("p (q n) -> p q n", n=P)
                                    ).then_inc(s5_mats, 1)

            def lru_tap(g, lag):
                for f in range(FT):
                    c = cv[:, f, lag:TOK]
                    ins = dve.scalar_tensor_tensor(
                        out=c, in0=xin[:, f, 0:TOK - lag], scalar=pcol("cd_conv_w", (LRU_CONV - 1 - lag) * LT + FT * g + f),
                        in1=c, op0=ALU.mult, op1=ALU.add)
                if lag < LRU_CONV - 1:
                    link(ins)
                else:
                    ins.then_inc(xc_ready, 1)

            def lru_step(g, k):
                if k == 3:
                    dve.wait_ge(tap0_ready, g + 1)
                    lru_tap(g, 1)
                    lru_tap(g, 2)
                if k == 4:
                    lru_tap(g, 3)
                if k == 7:
                    dve.wait_ge(gates_read, FT * (g + 1))
                    dve.wait_ge(xc_ready, g + 1)
                    dve.tensor_tensor(cv[:, :, :], cv[:, :, :], lru_i[:, :, :], ALU.mult).then_inc(gx_ready, 1)
                if k == 8:
                    dve.wait_ge(decayed, g + 1)
                    dve.scalar_tensor_tensor(out=lru_r[:, :, :], in0=lru_i[:, :, :], scalar=1.0, in1=lru_r[:, :, :],
                                             op0=ALU.add, op1=ALU.mult).then_inc(lru_q, 1)
                if k == 9:
                    dve.wait_ge(gx_ready, g + 1)
                    dve.wait_ge(lru_sd, g + 1)
                    link(dve.tensor_tensor(cv[:, :, :], cv[:, :, :], lru_r[:, :, :], ALU.mult))
                    for f in range(FT):
                        h = hs[:, FT * g + f, :]
                        dve.tensor_tensor_scan(h, h, cv[:, f, :], 0.0, ALU.mult, ALU.add).then_inc(hs_ready, 1)

            def gelu_argument(x, u, squared, count, ready):
                dve.wait_ge(squared, count)
                link(dve.tensor_scalar(u[:, :, :], u[:, :, :], GELU_K, 1.0, ALU.mult, ALU.add))
                dve.tensor_tensor(u[:, :, :], u[:, :, :], x[:, :, :], ALU.mult).then_inc(ready, 1)

            def gelu_product(x, u, tanh_ready, count):
                dve.wait_ge(tanh_ready, count)
                link(dve.scalar_tensor_tensor(out=x[:, :, :], in0=u[:, :, :], scalar=1.0, in1=x[:, :, :],
                                              op0=ALU.add, op1=ALU.mult))

            def gate_step(g, k):
                if k == 3:
                    gelu_argument(xin, cv, gelu_sq, g + 1, gelu_u)
                if k == 4:
                    gelu_product(xin, cv, gelu_th, g + 1)
                    dve.wait_ge(hs_ready, LT)
                    for f in range(FT):
                        dve.scalar_tensor_tensor(out=xin[:, f, :], in0=xin[:, f, :], scalar=0.5, in1=hs[:, FT * g + f, :],
                                                 op0=ALU.mult, op1=ALU.mult).then_inc(o_ready, 1)
                if k == 6:
                    dve.wait_ge(o_ready, XT + FT * (g + 1))
                    for f in range(FT):
                        n = FT * g + f
                        dve.wait_ge(o_hi, XT + n + 1)
                        dve.tensor_tensor(cat[:, n, 1, :], xin[:, f, :], cat[:, n, 0, :], ALU.subtract).then_inc(o_lo, 1)
                    dve.wait_ge(o_lo, XT + FT * (g + 1))

            def s5_states(j):
                q, jj, slot = j // 4, j % 4, j % 2
                pr, pi = (ph[1 - q % 2][:, jj:jj + 1, ri, :].broadcast_to([P, 2, TOK]) for ri in range(2))
                x = ps[:, 6, :].rearrange("p (r n) -> p r n", r=2)
                dve.wait_ge(bu_done, j + 1)
                dve.wait_ge(phases_ready, q + 1)
                dve.tensor_tensor(bq[:, 0, :, :], x, pr, ALU.mult)
                dve.tensor_tensor(bq[:, 1, :, :], x, pi, ALU.mult).then_inc(bu_free, 1)
                dve.wait_ge(bu_free, j + 1)
                if j >= 2:
                    dve.wait_ge(st_ready, j - 1)
                mark(dve.tensor_tensor(gs[:, slot, 0, :], bq[:, 0, 0, :], bq[:, 1, 1, :], ALU.add))
                link(dve.tensor_tensor(gs[:, slot, 1, :], bq[:, 0, 1, :], bq[:, 1, 0, :], ALU.subtract))
                mag = s5p[:, MAG, j:j + 1].broadcast_to([P, TOK])
                for ri in range(2):
                    ins = dve.tensor_tensor_scan(gs[:, slot, ri, :], mag, gs[:, slot, ri, :], 0.0, ALU.mult, ALU.add)
                ins.then_inc(scanned, 1)

            def s5_skip(q):
                dve.wait_ge(y5_done, 4 * (q + 1))
                dve.scalar_tensor_tensor(out=ut[:, q, :], in0=ut[:, q, :], scalar=pcol("cd_d_skip", q),
                                         in1=ps[:, 7, 0:TOK], op0=ALU.mult, op1=ALU.add).then_inc(y5_ready, 1)

            def cd_step(m):
                if m == 0:
                    s5_inputs()
                if m == 3:
                    s5_matrices()
                for j, at_ in enumerate(S5_AT):
                    if m == at_ + 1:
                        s5_states(j)
                    if m == at_ + S5_OUT + 1 and j % 4 == 3:
                        s5_skip(j // 4)
                for g, at_ in enumerate(LRU_AT):
                    lru_step(g, m - at_)
                s5_end = S5_AT[-1] + S5_OUT + 2
                if m == s5_end:
                    dve.wait_ge(y5_ready, UT)
                    gelu_argument(ut, s5_gelu, s5_sq, 1, s5_u)
                if m == s5_end + 1:
                    gelu_product(ut, s5_gelu, s5_th, 1)
                    dve.tensor_scalar(ut[:, :, :], ut[:, :, :], 0.5, None, ALU.mult).then_inc(glu_in, 1)
                for g, at_ in enumerate(GATE_AT):
                    gate_step(g, m - at_)

            def glu():
                dve.wait_ge(glu_in, 1)
                for f in range(UT):
                    dve.wait_ge(glu_act, UT)
                    dve.tensor_tensor(ut[:, f, :], ut[:, f, :], s5_gate[:, f, :], ALU.mult).then_inc(g5_ready, 1)
                for f in range(UT):
                    dve.wait_ge(g5_hi, f + 1)
                    dve.tensor_tensor(cat[:, LT + f, 1, :], ut[:, f, :], cat[:, LT + f, 0, :],
                                      ALU.subtract).then_inc(g5_lo, 1)

            def mix_cd():
                u, a, d, h = U_CD, A_CD, D_CD, H_CD
                for n, (kind, _) in enumerate(CD_GROUPS):
                    dst = ut if kind == "u" else xin
                    u, a, d, h = group(kind, u, a, d, h, lambda f: dst[:, f, :],
                                       lambda k: cd_step(PER_GROUP * n + k))
                for m in range(CD_UNITS, CD_STEPS):
                    cd_step(m)
                glu()

            param_columns()
            for n in range(RING):
                split(n)
            norm(0)
            mix0()
            out_proj(U_OUT0, D_OUT0, PER_GROUP)
            norm(1)
            up_proj(U_UP0, A_UP0, H_UP0, 0)
            out_proj(U_DOWN0, D_DOWN0, DOWN_PER)
            norm(2)
            mix_cd()
            out_proj(U_OUT1, D_OUT1, PER_GROUP)
            norm(3)
            up_proj(U_UP1, A_UP1, H_UP1, 1)
            out_proj(U_DOWN1, D_DOWN1, DOWN_PER, last=True)
            norm(4)

        @block.gpsimd
        def _(pool):
            chain = [0]

            def mark(ins):
                chain[0] += 1
                ins.then_inc(g_chain, 1)

            def link(ins):
                mark(ins)
                pool.wait_ge(g_chain, chain[0])

            def constants():
                mark(pool.memset(ident[:, :], 0.0))
                mark(pool.memset(neg_tri[:, :], -1.0))
                mark(pool.memset(strips, 1.0))
                pool.memset(ones[:, :], 1.0).then_inc(consts_ready, 1)
                pool.memset(neg_ones[:, :], -1.0).then_inc(consts_ready, 1)
                pool.wait_ge(g_chain, chain[0])
                pool.affine_select(out=ident[:, :], in_=ident[:, :], compare_op=ALU.not_equal, fill=1.0, base=0,
                                   pattern=[[-1, P]], channel_multiplier=1).then_inc(consts_ready, 1)
                pool.affine_select(out=neg_tri[:, :], in_=neg_tri[:, :], compare_op=ALU.is_ge, fill=0.0, base=0,
                                   pattern=[[-1, P]], channel_multiplier=1).then_inc(consts_ready, 1)
                link(pool.affine_select(out=strips, in_=strips, compare_op=ALU.is_ge, fill=0.0, base=0,
                                        pattern=[[-S5_CH, 8]], channel_multiplier=1))
                pool.affine_select(out=strips, in_=strips, compare_op=ALU.is_ge, fill=0.0, base=S5_CH - 1,
                                   pattern=[[S5_CH, 8]], channel_multiplier=-1).then_inc(consts_ready, 1)

            def cut(dst, src, least, done):
                pool.affine_select(out=dst[:, 0:3:2, :], in_=src[:, 0:3:2, :], compare_op=ALU.is_ge, fill=0.0,
                                   base=-least, pattern=[[0, 2], [1, P]], channel_multiplier=-1).then_inc(done, 1)

            def phases(q):
                ph_q = ph[1 - q % 2]
                if q >= 2:
                    pool.wait_ge(scanned, 4 * (q - 1))
                    pool.wait_ge(st_ready, 4 * (q - 1))
                for ri, src in enumerate((COS, SIN)):
                    mark(pool.tensor_copy(ph_q[:, :, ri, 0:1], s5p[:, src, 4 * q:4 * q + 4].unsqueeze(2)))
                pool.wait_ge(g_chain, chain[0])
                n = 1
                while n < TOK:
                    half = min(n, P // 2)
                    for at_ in range(0, n, half):
                        for ri in range(2):
                            mark(pool.tensor_tensor(pt[:, ri, :, :, 0:half], ph_q[:, :, :, at_:at_ + half],
                                                    ph_q[:, :, ri:ri + 1, n - 1:n].broadcast_to([P, FT, 2, half]),
                                                    ALU.mult))
                        pool.wait_ge(g_chain, chain[0])
                        to = slice(n + at_, n + at_ + half)
                        mark(pool.tensor_tensor(ph_q[:, :, 0, to], pt[:, 0, :, 0, 0:half], pt[:, 1, :, 1, 0:half],
                                                ALU.subtract))
                        ins = pool.tensor_tensor(ph_q[:, :, 1, to], pt[:, 0, :, 1, 0:half], pt[:, 1, :, 0, 0:half],
                                                 ALU.add)
                        if to.stop < TOK:
                            link(ins)
                        else:
                            ins.then_inc(phases_ready, 1)
                            pool.wait_ge(phases_ready, q + 1)
                    n *= 2

            def turn_states(j):
                q, jj, slot = j // 4, j % 4, j % 2
                pr, pi = (ph[1 - q % 2][:, jj:jj + 1, ri, :].broadcast_to([P, 2, TOK]) for ri in range(2))
                pool.wait_ge(scanned, j + 1)
                if j >= 1:
                    pool.wait_ge(st_ready, j)
                mark(pool.tensor_tensor(rot[:, 0, :, :], gs[:, slot, :, :], pr, ALU.mult))
                link(pool.tensor_tensor(rot[:, 1, :, :], gs[:, slot, :, :], pi, ALU.mult))
                if j >= 2:
                    pool.wait_ge(y5_done, j - 1)
                pool.tensor_tensor(st[:, slot, 0, :], rot[:, 0, 0, :], rot[:, 1, 1, :], ALU.subtract)
                pool.tensor_tensor(st[:, slot, 1, :], rot[:, 0, 1, :], rot[:, 1, 0, :], ALU.add).then_inc(st_ready, 1)

            constants()
            for h in range(SSD_HEADS):
                pool.wait_ge(decay_ready, h + 1)
                cut(blk[2 + h % 2], blk[2 + h % 2], 0, decay_cut)
            for h in range(SB_HEADS):
                pool.wait_ge(sp_ready, h + 1)
                cut(blk[2], blk[2], 1, sp_cut)
                pool.wait_ge(w_exp, h + 1)
                if h >= 1:
                    pool.wait_ge(att_done, h)
                link(pool.tensor_copy(blk[3][:, 1, :], blk[1][:, 1, :]))
                cut(blk[3], blk[1], 1, w_cut)
            pool.wait_ge(acc_free, A_UP0)
            pool.memset(b_pad[:, :, :, :, :], 0.0).then_inc(s5g, 1)
            pool.wait_ge(acc_free, A_CD)
            pool.wait_ge(s5v, 3)
            phases(0)
            pool.wait_ge(y_lo_ready, 3 * KT)
            phases(1)
            for q in range(ST // 4):
                for jj in range(4):
                    turn_states(4 * q + jj)
                if q + 2 < ST // 4:
                    phases(q + 2)


_INS = ["x", "norm_mix", "norm_ffn", "norm_final", "ab_w_in", "ab_conv_w", "ab_conv_b", "ab_dt_bias", "ab_a_log",
        "ab_d_skip", "ab_ssd_norm", "ab_w_out", "cd_w_in", "cd_conv_w", "cd_conv_b", "cd_w_a", "cd_b_a", "cd_w_i",
        "cd_b_i", "cd_lambda", "cd_log_dt", "cd_a_re", "cd_a_im", "cd_b_re", "cd_b_im", "cd_c_re", "cd_c_im",
        "cd_d_skip", "cd_w_glu", "cd_b_glu", "cd_w_out", "ffn_w_up", "ffn_conv_w", "ffn_conv_b", "ffn_w_down"]


def kernel(**inputs):
    import numpy as np
    import concourse.bacc as bacc
    from concourse.bass_utils import run_bass_kernel_spmd

    nc = bacc.Bacc("TRN2", target_bir_lowering=False, num_devices=1)
    arrays, tensors = {}, {}
    for name in _INS:
        a = np.ascontiguousarray(inputs[name])
        arrays[f"in_{name}"] = a
        tensors[name] = nc.dram_tensor(f"in_{name}", a.shape, mybir.dt.from_np(a.dtype), kind="ExternalInput").ap()
    out = nc.dram_tensor("out_0", (1, TOK, D), F32, kind="ExternalOutput").ap()
    trunk(nc, tensors, out)
    r = run_bass_kernel_spmd(nc, [arrays], core_ids=[0])
    return r.results[0]["out_0"]
```

```python
from contextlib import ExitStack

import concourse.bass as bass
from concourse import mybir

ALU = mybir.AluOpType
ACT = mybir.ActivationFunctionType
F32 = mybir.dt.float32
F32R = mybir.dt.float32r

P = 128
TOK = 256
TT = TOK // P
D = 2048
KT = D // P
COLS = 512
FT = COLS // P
HK = 2
RING = 4
EPS = 1e-6

SB_HEADS, SB_DH = 4, 128
SSD_HEADS, SSD_P, SSD_GROUPS, SSD_N, SSD_CONV = 24, 64, 4, 128, 4
SSD_W = SSD_HEADS * SSD_P
XT = SSD_W // P
RH = SSD_HEADS // SSD_GROUPS
LRU_W, LRU_CONV, LRU_C = 1536, 4, 8.0
LT = LRU_W // P
S5_G, S5_CH, S5_N = 32, 16, 64
S5_W = S5_G * S5_CH
ST = S5_G * S5_N // P
UT = S5_W // P
DFF, FFN_CONV = 4096, 3
HT = DFF // P

PARAM_ROWS = [
    ("norm_mix", 2 * KT), ("norm_ffn", 2 * KT), ("ab_ssd_norm", XT),
    ("ab_conv_b", 20), ("ab_conv_w", SSD_CONV * 20),
    ("cd_conv_w", LRU_CONV * LT), ("cd_conv_b", LT), ("cd_b_a", LT), ("cd_b_i", LT),
    ("cd_lambda", LT), ("cd_d_skip", UT), ("cd_b_glu", UT),
    ("ffn_conv_w", 2 * FFN_CONV * HT), ("ffn_conv_b", 2 * HT),
    ("cd_a_re", ST), ("cd_a_im", ST),
]
COL = {}
_at = 0
for _name, _n in PARAM_ROWS:
    COL[_name] = _at
    _at += _n
NPARAM = _at
PT = -(-NPARAM // P)


def pieces(first):
    found = []
    for name, n in PARAM_ROWS:
        done = 0
        while done < n:
            at = COL[name] + done
            m = min(n - done, P - at % P)
            if (at < P) == first:
                found.append((name, done, at // P, at % P, m))
            done += m
    return found


AB_GROUPS = [("x", 3072), ("x", 3584), ("x", 4096), ("x", 4608), ("x", 5120), ("dt", 5632),
             ("z", 1536), ("z", 2048), ("z", 2560), ("q", 0), ("k", 512), ("v", 1024)]
CD_GROUPS = [("u", 3072), ("x", 1536), ("x", 2048), ("x", 2560), ("g", 0), ("g", 512), ("g", 1024)]
CONV_AT = [7 + 8 * g for g in range(5)]
DT_AT = 41
XT_AT = (48, 50)
PAIR_AT = [52 + 2 * n for n in range(XT)]
Z_AT = [49 + 8 * g for g in range(3)]
GNORM_AT = 80
HEAD_AT = [83 + h for h in range(SB_HEADS)]
LRU_AT = [15 + 8 * g for g in range(3)]
GATE_AT = [39 + 8 * g for g in range(3)]
S5_AT = [7, 10, 12, 15, 20, 24, 29, 31, 32, 36, 40, 42, 43, 46, 47, 50]
S5_OUT = [12, 13, 16, 19, 27, 29, 32, 34, 36, 42, 44, 45, 48, 49, 52, 53]
S5_END = S5_OUT[-1] + 1
PER_GROUP = KT // HK
DT_UNITS = 2
CHUNKS = D // COLS

AB_UNITS = sum(DT_UNITS if k == "dt" else PER_GROUP for k, _ in AB_GROUPS)
CD_UNITS = PER_GROUP * len(CD_GROUPS)
CD_STEPS = GATE_AT[-1] + 8
OUT_UNITS = CHUNKS * PER_GROUP
UP_ITERS = DFF // COLS
UP_UNITS = UP_ITERS * 2 * PER_GROUP
DOWN_PER = HT // HK
DOWN_UNITS = CHUNKS * DOWN_PER

U_AB = 0
U_OUT0 = U_AB + AB_UNITS
U_UP0 = U_OUT0 + OUT_UNITS
U_DOWN0 = U_UP0 + UP_UNITS
U_CD = U_DOWN0 + DOWN_UNITS
U_OUT1 = U_CD + CD_UNITS
U_UP1 = U_OUT1 + OUT_UNITS
U_DOWN1 = U_UP1 + UP_UNITS
U_END = U_DOWN1 + DOWN_UNITS

AB_ACCS = sum({"dt": 1, "v": TT}.get(k, FT) for k, _ in AB_GROUPS)
CD_ACCS = FT * len(CD_GROUPS)
OUT_ACCS = CHUNKS * TT
UP_ACCS = UP_ITERS * 2 * FT
A_AB = 0
A_OUT0 = A_AB + AB_ACCS
A_UP0 = A_OUT0 + OUT_ACCS
A_DOWN0 = A_UP0 + UP_ACCS
A_CD = A_DOWN0 + OUT_ACCS
A_OUT1 = A_CD + CD_ACCS
A_UP1 = A_OUT1 + OUT_ACCS
A_DOWN1 = A_UP1 + UP_ACCS
D_OF = {"dt": 0, "v": TT - 1}
D_AB = 0
D_OUT0 = D_AB + sum(D_OF.get(k, FT - 1) for k, _ in AB_GROUPS)
D_DOWN0 = D_OUT0 + CHUNKS
D_CD = D_DOWN0 + CHUNKS
D_OUT1 = D_CD + (FT - 1) * len(CD_GROUPS)
D_DOWN1 = D_OUT1 + CHUNKS
NEXT = [U_AB, U_UP0, U_CD, U_UP1]
H_AB = 0
H_UP0 = H_AB + AB_ACCS - TT
H_CD = H_UP0 + 2 * UP_ITERS
H_UP1 = H_CD + CD_ACCS


def mix_bank(n):
    return (n - (A_AB if n < A_CD else A_CD)) % FT


GELU_C = 0.7978845608028654
GELU_K = 0.044715
TWO_PI = (6.28125, 0.0019350051879882812, 3.01991598196e-07)
ROUND = 12582912.0


def trunk(nc, t, out):
    def at(name, shape, dtype, offset):
        return nc.alloc_sbuf_tensor_at(name, shape, dtype, offset=offset)

    KB = 1024
    base = 16512
    raw = at("raw", [P, RING, HK * COLS], F32, base)
    w_hi = at("w_hi", [P, RING, HK * COLS], F32R, base + 16 * KB)
    w_lo = at("w_lo", [P, RING, HK * COLS], F32R, base + 32 * KB)
    res = at("res", [P, TT, D], F32, base + 48 * KB)
    y = at("y", [P, KT, 2, TOK], F32R, base + 64 * KB)
    hff = at("hff", [P, HT, 2, TOK], F32R, base + 96 * KB)
    cat = hff
    mix2 = base + 128 * KB
    xn = at("xn", [P, TT, D], F32, mix2)
    c0 = base + 160 * KB
    params = at("params", [P, NPARAM], F32, c0)
    ident = at("ident", [P, P], F32, c0 + 2304)
    ones = at("ones", [P, P], F32, c0 + 2304 + 512)
    neg_ones = at("neg_ones", [P, P], F32, c0 + 2304 + 1024)
    neg_tri = at("neg_tri", [P, P], F32, c0 + 2304 + 1536)
    s5p = at("s5p", [P, 26, ST], F32, c0 + 4352)
    tiny = at("tiny", [P, 56], F32, c0 + 6016)
    ssq = at("ssq", [P, TT, CHUNKS], F32, c0 + 6240)
    c1 = c0 + 6272
    dt_t = at("dt_t", [P, TT, SSD_HEADS], F32, c1)
    cs_t = at("cs_t", [P, TT, SSD_HEADS], F32, c1 + 192)
    c8 = at("c8", [P, LT], F32, c1 + 384)
    parity = at("parity", [P, 2], F32, c1 + 448)[:, :]
    strips = at("strips", [P, 8], F32, c1 + 480)[:, :]
    mix1 = c1 + 608

    prow = at("prow", [P, PT, P], F32, mix1 + 20 * KB)
    xbc = at("xbc", [P, 20, TOK], F32, mix1)
    qk = at("qk", [P, 2 * SB_HEADS, TOK], F32, mix1 + 20 * KB)
    v_t = at("v_t", [P, TT, SB_HEADS * SB_DH], F32, mix1 + 28 * KB)
    tmp = at("tmp", [P, FT, TOK], F32, mix1 + 32 * KB)
    cv = at("cv", [P, FT, TOK], F32, mix1 + 36 * KB)
    zg = at("zg", [P, XT, TOK], F32, mix2)
    xdt = at("xdt", [P, TT, SSD_W], F32, mix2 + 12 * KB)
    blk = [at(f"blk{n}", [P, 3, P], F32, mix2 + 24 * KB + 1536 * n) for n in range(4)]
    decayed_cb = [at(f"decayed_cb{n}", [P, 3, P], F32, base + 96 * KB + 1536 * n) for n in range(4)]
    z_ln = [at(f"z_ln{h}", [P, 3, P], F32, mix2 + 12 * KB + 1536 * h) for h in range(SB_HEADS)]
    probs = [at(f"probs{h}", [P, 3, P], F32, mix2 + 18 * KB + 1536 * h) for h in range(SB_HEADS)]
    dts = at("dts", [SSD_HEADS, TOK], F32, mix2 + 30 * KB)
    cs = at("cs", [SSD_HEADS, TOK], F32, mix2 + 31 * KB)
    dt_w0, dt_w1, dt_w2, dt_w3 = (qk[0:SSD_HEADS, n, :] for n in range(4))
    ffn_g = at("ffn_g", [P, FT, TOK], F32, mix1)
    ffn_tv = at("ffn_tv", [P, FT, TOK], F32, mix1 + 4 * KB)
    ffn_v = at("ffn_v", [P, FT, TOK], F32, mix1 + 8 * KB)
    hs = at("hs", [P, LT, TOK], F32, mix1)
    ut = at("ut", [P, UT, TOK], F32, mix1 + 12 * KB)
    wai = at("wai", [P, 2, FT, P], F32, mix1 + 16 * KB)
    xin = at("xin", [P, FT, TOK], F32, mix1 + 20 * KB)
    cd_tmp = at("cd_tmp", [P, FT, TOK], F32, base + 116 * KB)
    xc = [cv, cd_tmp, cv]
    lru_r = at("lru_r", [P, FT, TOK], F32, mix1 + 24 * KB)
    lru_i = at("lru_i", [P, FT, TOK], F32, mix1 + 28 * KB)
    w_glu = at("w_glu", [P, UT, S5_W], F32, mix1 + 24 * KB)
    ph = [at(f"ph{n}", [P, FT, 2, TOK], F32, mix2 + 16 * KB * n) for n in range(2)]
    bq = at("bq", [P, 2, 2, TOK], F32, mix2 + 8 * KB)
    gs = at("gs", [P, 2, 2, TOK], F32, mix2 + 12 * KB)
    s5_gelu = at("s5_gelu", [P, UT, TOK], F32, mix2 + 16 * KB)
    s5_gate = at("s5_gate", [P, UT, TOK], F32, mix2 + 20 * KB)
    pt = at("pt", [P, 2, FT, 2, P // 2], F32, mix2 + 24 * KB)
    rot = at("rot", [P, 2, 2, TOK], F32, mix2 + 24 * KB)
    st = at("st", [P, 2, 2, TOK], F32, mix2 + 28 * KB)
    bb = at("bb", [P, 2, UT, P], F32, base + 120 * KB)
    cc = at("cc", [P, 2, UT, P], F32, base + 124 * KB)
    b_raw = at("b_raw", [P, 2, ST, S5_CH], F32, mix1 + 20 * KB)
    b_pad = at("b_pad", [P, 2, ST, 2, S5_CH], F32, mix1 + 22 * KB)
    c_pad = at("c_pad", [P, 2, UT, 2, S5_N], F32, mix1 + 26 * KB)
    b_tmp = at("b_tmp", [P, 2, ST, S5_CH], F32, mix1 + 30 * KB)
    g_fin = at("g_fin", [P, D], F32, mix1)

    with ExitStack() as ctx:
        ps = ctx.enter_context(nc.psum_tensor("ps", [P, 8, COLS], F32))

        def sem(name):
            return ctx.enter_context(nc.semaphore(name))

        raw_loaded = [sem(f"raw_loaded{n}") for n in range(RING)]
        hi_ready, lo_ready, unit_used = sem("hi_ready"), sem("lo_ready"), sem("unit_used")
        acc_done, acc_free, half_copied = sem("acc_done"), sem("acc_free"), sem("half_copied")
        x_loaded = [sem(f"x_loaded{n}") for n in range(TT)]
        first_loaded, rows_loaded, small_loaded = sem("first_loaded"), sem("rows_loaded"), sem("small_loaded")
        consts_ready, rows_turned, params_ready = sem("consts_ready"), sem("rows_turned"), sem("params_ready")
        v_chain, a_chain, g_chain = sem("v_chain"), sem("a_chain"), sem("g_chain")
        ssq_ready, ms_ready, sd_ready = sem("ssq_ready"), sem("ms_ready"), sem("sd_ready")
        rstd_ready, xn0_ready, xn1_ready, turned = (
            sem("rstd_ready"), sem("xn0_ready"), sem("xn1_ready"), sem("turned"))
        y_hi_ready, y_lo_ready = sem("y_hi_ready"), sem("y_lo_ready")
        ffn_conv, ffn_act, ffn_h, ffn_hi, ffn_lo = (
            sem("ffn_conv"), sem("ffn_act"), sem("ffn_h"), sem("ffn_hi"), sem("ffn_lo"))
        xtap0, xconv, xact, z_act = sem("xtap0"), sem("xconv"), sem("xact"), sem("z_act")
        dt_abs, dt_exp, dt_w, dt_ln, dt_a, cs_ready = (
            sem("dt_abs"), sem("dt_exp"), sem("dt_w"), sem("dt_ln"), sem("dt_a"), sem("cs_ready"))
        cs_turned, cs_t_ready, x_turned, xdt_ready = (
            sem("cs_turned"), sem("cs_t_ready"), sem("x_turned"), sem("xdt_ready"))
        cb_done, cs_spread, decay_ready, decay_cut, m_ready, yh_done, ys_ready = (
            sem("cb_done"), sem("cs_spread"), sem("decay_ready"), sem("decay_cut"),
            sem("m_ready"), sem("yh_done"), sem("ys_ready"))
        sq_ready, sq_summed, gn_ms, gn_sd, gn_rstd = (
            sem("sq_ready"), sem("sq_summed"), sem("gn_ms"), sem("gn_sd"), sem("gn_rstd"))
        o_ready, o_hi, o_lo = sem("o_ready"), sem("o_hi"), sem("o_lo")
        zs_done, ln_ready, sp_ready, sp_cut, zs_full, w_exp, w_cut, att_done = (
            sem("zs_done"), sem("ln_ready"), sem("sp_ready"), sem("sp_cut"),
            sem("zs_full"), sem("w_exp"), sem("w_cut"), sem("att_done"))
        att_hi, att_lo = sem("att_hi"), sem("att_lo")
        wai_loaded, bc_loaded, glu_loaded = sem("wai_loaded"), sem("bc_loaded"), sem("glu_loaded")
        s5v, s5a, s5g, s5_pads, s5_turned, s5_mats = (
            sem("s5v"), sem("s5a"), sem("s5g"), sem("s5_pads"), sem("s5_turned"), sem("s5_mats"))
        phases_ready, bu_done, bu_free, scanned, st_ready, y5_done, y5_ready = (
            sem("phases_ready"), sem("bu_done"), sem("bu_free"), sem("scanned"), sem("st_ready"),
            sem("y5_done"), sem("y5_ready"))
        gelu_sq, gelu_u, gelu_th, glu_in, glu_done, glu_act = (
            sem("gelu_sq"), sem("gelu_u"), sem("gelu_th"), sem("glu_in"), sem("glu_done"), sem("glu_act"))
        g5_ready, g5_hi, g5_lo = sem("g5_ready"), sem("g5_hi"), sem("g5_lo")
        s5_sq, s5_u, s5_th = sem("s5_sq"), sem("s5_u"), sem("s5_th")
        tap0_ready, xc_ready, gates_done, gates_read, gx_ready, decayed, lru_q, lru_sd, hs_ready = (
            sem("tap0_ready"), sem("xc_ready"), sem("gates_done"), sem("gates_read"), sem("gx_ready"),
            sem("decayed"), sem("lru_q"), sem("lru_sd"), sem("hs_ready"))
        gfin_loaded, out_ready, stored = sem("gfin_loaded"), sem("out_ready"), sem("stored")

        def s5(n):
            return s5p[:, n, :]
        (LOGDT, DTV, LR, XDT, TH, MAG, THETA, TURN, SINH, SIN2, SIN, COS, E1, AM1, ABI, DEN, FR, FI,
         T0, T1, T2, T3) = range(22)

        def by_rows(w):
            return w.rearrange("(kt p) n -> p kt n", p=P)

        w_ab, w_cd = by_rows(t["ab_w_in"][0]), by_rows(t["cd_w_in"][0])
        w_out = [by_rows(t["ab_w_out"][0]), by_rows(t["cd_w_out"][0])]
        w_up = [by_rows(t["ffn_w_up"][n]) for n in range(2)]
        w_down = [by_rows(t["ffn_w_down"][n]) for n in range(2)]

        def plus(n, it, per):
            return n if it is None else it * per + n

        def flat(b):
            return b[:, :, :].rearrange("p a b -> p (a b)")

        def pcol(name, n):
            return params[:, COL[name] + n:COL[name] + n + 1]

        block = ctx.enter_context(nc.Block())

        @block.sync
        def _(sp):
            def load(u, src, it=None, per=0):
                if u >= RING:
                    sp.wait_ge(lo_ready, plus(u - RING + 1, it, per))
                    if it is not None:
                        sp.nop(nofuse=True)
                sp.dma_start(raw[:, u % RING, :].rearrange("p (k n) -> p k n", k=HK),
                             src).then_inc(raw_loaded[u % RING], 16)

            def in_proj(u, w, groups):
                for kind, col in groups:
                    if kind == "dt":
                        for k in range(DT_UNITS):
                            sp.wait_ge(lo_ready, u - RING + 1)
                            sp.dma_start(raw[:, u % RING, :].rearrange("p (k n) -> p k n", n=P)[:, :, 0:SSD_HEADS],
                                         w[:, k * KT // 2:(k + 1) * KT // 2, col:col + SSD_HEADS]
                                         ).then_inc(raw_loaded[u % RING], 16)
                            u += 1
                        continue
                    for k in range(PER_GROUP):
                        load(u, w[:, HK * k:HK * k + HK, col:col + COLS])
                        u += 1

            def out_proj(u, w, per):
                with sp.Fori(0, CHUNKS) as i:
                    for k in range(per):
                        load(u + k, w[:, HK * k:HK * k + HK, bass.ds(i * COLS, COLS)], i, per)

            def up_proj(u, w):
                with sp.Fori(0, UP_ITERS) as i:
                    for part in range(2):
                        for k in range(PER_GROUP):
                            load(u + part * PER_GROUP + k,
                                 w[:, HK * k:HK * k + HK, bass.ds(i * COLS + (1 - part) * DFF, COLS)],
                                 i, 2 * PER_GROUP)

            x_rows = t["x"][0].rearrange("(tt p) d -> p tt d", p=P)
            for tt in range(TT):
                sp.dma_start(res[:, tt, :], x_rows[:, tt, :]).then_inc(x_loaded[tt], 16)
            in_proj(U_AB, w_ab, AB_GROUPS)
            out_proj(U_OUT0, w_out[0], PER_GROUP)
            up_proj(U_UP0, w_up[0])
            out_proj(U_DOWN0, w_down[0], DOWN_PER)
            in_proj(U_CD, w_cd, CD_GROUPS)
            out_proj(U_OUT1, w_out[1], PER_GROUP)
            up_proj(U_UP1, w_up[1])
            out_proj(U_DOWN1, w_down[1], DOWN_PER)

        @block.tensor
        def _(pe):
            def unit(u, it=None, per=0):
                pe.wait_ge(lo_ready, plus(u + 1, it, per))

            def half(parts, u):
                return parts[:, u % RING, :].rearrange("p (k n) -> p k n", k=HK)

            def fm_unit(u, k, a, bank0, free_lag, it, per, aper, n):
                unit(u, it, per)
                for f in range(FT):
                    if bank0 == 0:
                        y_made(n, k, f, f)
                    if k == 0:
                        pe.wait_ge(acc_free, plus(a + f + 1 - free_lag, it, aper))
                    for kk in range(HK):
                        kt = HK * k + kk
                        cols = slice(f * P, f * P + P)
                        pe.matmul(ps[:, bank0 + f, :], half(w_hi, u)[:, kk, cols],
                                  y[:, kt, :, :].rearrange("p a b -> p (a b)"),
                                  start=kt == 0, stop=False)
                        mm = pe.matmul(ps[:, bank0 + f, 0:TOK], half(w_lo, u)[:, kk, cols], y[:, kt, 0, :],
                                       start=False, stop=kt == KT - 1)
                mm.then_inc(unit_used, 1)

            def tm_unit(u, k, per_acc, lhs, banks, it=None, per=0):
                unit(u, it, per)
                for tt in range(TT):
                    for kk in range(HK):
                        kt = HK * k + kk
                        hi = lhs[:, kt, 0, tt * P:tt * P + P]
                        lo = lhs[:, kt, 1, tt * P:tt * P + P]
                        pe.matmul(banks(tt), hi, half(w_hi, u)[:, kk, :], start=kt == 0, stop=False)
                        pe.matmul(banks(tt), hi, half(w_lo, u)[:, kk, :], start=False, stop=False)
                        mm = pe.matmul(banks(tt), lo, half(w_hi, u)[:, kk, :], start=False,
                                       stop=kt == HK * per_acc - 1)
                    if k == per_acc - 1 and tt < TT - 1:
                        mm.then_inc(acc_done, 1)
                mm.then_inc(unit_used, 1)

            def dt_units(u, a):
                for k in range(DT_UNITS):
                    unit(u + k)
                    if k == 0:
                        pe.wait_ge(acc_free, a - FT + 1)
                    for kk in range(KT // 2):
                        kt = k * KT // 2 + kk
                        w = [parts[:, (u + k) % RING, kk * P:kk * P + P] for parts in (w_hi, w_lo)]
                        pe.matmul(ps[:, mix_bank(a), :], w[0], y[:, kt, :, :].rearrange("p a b -> p (a b)"),
                                  start=kt == 0, stop=False)
                        mm = pe.matmul(ps[:, mix_bank(a), 0:TOK], w[1], y[:, kt, 0, :], start=False, stop=kt == KT - 1)
                    mm.then_inc(unit_used, 1)

            def out_proj(u, a, per, lhs, ready, free, aside=None):
                pe.wait_ge(acc_free, free)
                if aside is not None:
                    for k in range(per):
                        ready(k)
                        tm_unit(u + k, k, per, lhs, lambda tt: ps[:, tt, :])
                        if k == 1:
                            aside()
                with pe.Fori(0 if aside is None else 1, CHUNKS) as i:
                    def banks(tt):
                        return ps[:, bass.ds(i * TT + tt, 1), :]
                    for k in range(per):
                        ready(k)
                        tm_unit(u + k, k, per, lhs, banks, i, per)

            def up_proj(u, a, n):
                with pe.Fori(0, UP_ITERS) as i:
                    for part in range(2):
                        for k in range(PER_GROUP):
                            fm_unit(u + part * PER_GROUP + k, k, a + part * FT, part * FT, 2 * FT,
                                    i, 2 * PER_GROUP, 2 * FT, n)

            def norm(n):
                for b in range(KT // 2):
                    if b % 2 == 0:
                        pe.wait_ge(xn0_ready, CHUNKS * n + b // 2 + 1)
                        pe.wait_ge(xn1_ready, CHUNKS * n + b // 2 + 1)
                    for j in range(2):
                        kt = 2 * b + j
                        for tt in range(TT):
                            mm = pe.transpose(ps[:, b, j * TOK + tt * P:j * TOK + tt * P + P],
                                              xn[:, tt, kt * P:kt * P + P], ident[:, :])
                    mm.then_inc(turned, 1)

            def y_made(n, k, f, bank):
                if k == 0:
                    pe.wait_ge(y_lo_ready, KT * n + 2 * bank + 2)
                elif f == 0:
                    pe.wait_ge(y_lo_ready, KT * n + HK * k + HK)

            def turn_first_params():
                pe.wait_ge(consts_ready, 4)
                pe.wait_ge(first_loaded, 16 * len(pieces(True)))
                pe.transpose(ps[:, 0, 0:P], prow[:, 0, :], ident[:, :]).then_inc(rows_turned, 1)
                pe.wait_ge(params_ready, 1)

            def turn_params():
                pe.wait_ge(rows_loaded, 16 * len(pieces(False)))
                pe.wait_ge(y_lo_ready, KT)
                for n in range(1, PT):
                    rows = min(P, NPARAM - n * P)
                    mm = pe.transpose(ps[:, 4, (n - 1) * P:(n - 1) * P + rows], prow[0:rows, n, :],
                                      ident[0:rows, 0:rows])
                mm.then_inc(rows_turned, 1)

            def turn_dt():
                pe.wait_ge(cs_ready, 1)
                for tt in range(TT):
                    pe.transpose(ps[:, 7, tt * 32:tt * 32 + SSD_HEADS], dts[:, tt * P:tt * P + P],
                                 ident[0:SSD_HEADS, 0:SSD_HEADS])
                    mm = pe.transpose(ps[:, 7, 64 + tt * 32:64 + tt * 32 + SSD_HEADS], cs[:, tt * P:tt * P + P],
                                      ident[0:SSD_HEADS, 0:SSD_HEADS])
                mm.then_inc(cs_turned, 1)

            def turn_x(n):
                if n == 0:
                    pe.wait_ge(xact, 5)
                tt, q = n % TT, n // TT
                if n >= 3:
                    pe.wait_ge(xdt_ready, n - 2)
                for j in range(4):
                    mm = pe.transpose(ps[:, 4 + n % 3, j * P:j * P + P],
                                      xbc[:, 4 * q + j, tt * P:tt * P + P], ident[:, :])
                mm.then_inc(x_turned, 1)

            def ssd_spread(n):
                if n == 0:
                    pe.wait_ge(cs_t_ready, 1)
                    pe.wait_ge(xdt_ready, 6)
                if n % (RH // 2) == 0:
                    g = n // (RH // 2)
                    if g:
                        pe.wait_ge(m_ready, 2 * n)
                    b, c = xbc[:, XT + g, :], xbc[:, XT + SSD_GROUPS + g, :]
                    pe.matmul(ps[:, 4, 0:TOK], b[:, 0:P], c, start=True, stop=True, skip_group_check=True)
                    pe.matmul(ps[:, 4, TOK:TOK + P], b[:, P:TOK], c[:, P:TOK], start=False, stop=True,
                              skip_group_check=True).then_inc(cb_done, 1)
                if n:
                    pe.wait_ge(decay_ready, 2 * n)
                for j in range(2):
                    h = 2 * n + j
                    mm = pe.matmul(ps[:, 5, j * TOK:j * TOK + TOK],
                                   ident[0:SSD_HEADS, h:h + 1].broadcast_to([SSD_HEADS, P]), cs[:, :],
                                   start=j == 0, stop=True, skip_group_check=True)
                mm.then_inc(cs_spread, 1)

            def ssd_out(n):
                if n >= 2:
                    pe.wait_ge(ys_ready, n - 1)
                for j in range(2):
                    h = 2 * n + j
                    pe.wait_ge(m_ready, h + 1)
                    o = ps[j * SSD_P:(j + 1) * SSD_P, 6 + n % 2, 0:TOK]
                    m = decayed_cb[h % 4]
                    pe.matmul(o, xdt[:, 0, h * SSD_P:(h + 1) * SSD_P], m[:, 0:2, :].rearrange("p a b -> p (a b)"),
                              start=True, stop=False)
                    mm = pe.matmul(o[:, P:TOK], xdt[:, 1, h * SSD_P:(h + 1) * SSD_P], m[:, 2, :],
                                   start=False, stop=True)
                mm.then_inc(yh_done, 1)

            def ssd_norm():
                pe.wait_ge(sq_ready, XT)
                for n in range(XT):
                    mm = pe.matmul(ps[:, 4, 0:TOK], ones[:, :], zg[:, n, :], start=n == 0, stop=n == XT - 1)
                mm.then_inc(sq_summed, 1)

            def scores(h):
                if h == 0:
                    pe.wait_ge(acc_free, A_OUT0 - TT)
                    pe.wait_ge(gn_ms, 1)
                    pe.wait_ge(ys_ready, XT)
                q, k = qk[:, h, :], qk[:, SB_HEADS + h, :]
                pe.matmul(ps[:, 4 + h, 0:TOK], k[:, 0:P], q, start=True, stop=False, skip_group_check=True)
                pe.matmul(ps[:, 4 + h, TOK:TOK + P], k[:, P:TOK], q[:, P:TOK], start=False, stop=False,
                          skip_group_check=True).then_inc(zs_done, 1)

            def suffix_sums(h):
                pe.wait_ge(sp_cut, h + 1)
                pe.matmul(ps[:, 4 + h, 0:TOK], neg_tri[:, :], blk[h][:, 0:2, :].rearrange("p a b -> p (a b)"),
                          start=False, stop=False, skip_group_check=True)
                pe.matmul(ps[:, 4 + h, P:TOK], neg_ones[:, :], blk[h][:, 2, :], start=False, stop=False,
                          skip_group_check=True)
                pe.matmul(ps[:, 4 + h, TOK:TOK + P], neg_tri[:, :], blk[h][:, 2, :], start=False, stop=True,
                          skip_group_check=True).then_inc(zs_full, 1)

            def attend(h):
                pe.wait_ge(w_cut, h + 1)
                o = ps[:, 4 + h, 0:TOK]
                pe.matmul(o, v_t[:, 0, h * SB_DH:(h + 1) * SB_DH], probs[h][:, 0:2, :].rearrange("p a b -> p (a b)"),
                          start=True, stop=False)
                pe.matmul(o[:, P:TOK], v_t[:, 1, h * SB_DH:(h + 1) * SB_DH], probs[h][:, 2, :],
                          start=False, stop=True).then_inc(att_done, 1)

            def ab_step(m):
                if m == 6:
                    turn_params()
                if m == DT_AT + 7:
                    turn_dt()
                if m in XT_AT:
                    for n in range(3):
                        turn_x(3 * XT_AT.index(m) + n)
                for n, at_ in enumerate(PAIR_AT):
                    if m == at_ + 4:
                        ssd_out(n)
                    if m == at_:
                        ssd_spread(n)
                if m == GNORM_AT:
                    ssd_norm()
                for h, at_ in enumerate(HEAD_AT):
                    if m == at_ + 3:
                        suffix_sums(h)
                    if m == at_:
                        scores(h)

            def mix_ab():
                u, a, m = U_AB, A_AB, 0
                for kind, _ in AB_GROUPS:
                    if kind == "dt":
                        dt_units(u, a)
                        u, a, m = u + DT_UNITS, a + 1, m + DT_UNITS
                        continue
                    if kind == "v":
                        pe.wait_ge(acc_free, a - 2)
                    for k in range(PER_GROUP):
                        if kind == "v":
                            tm_unit(u + k, k, PER_GROUP, y, lambda tt: ps[:, mix_bank(a + tt), :])
                        else:
                            fm_rot(u + k, k, a, [mix_bank(a + f) for f in range(FT)], 0 if m == 0 else None)
                        ab_step(m + k)
                    u, a, m = u + PER_GROUP, a + (TT if kind == "v" else FT), m + PER_GROUP
                pe.wait_ge(acc_free, A_OUT0)
                for h in range(SB_HEADS):
                    attend(h)

            def fm_rot(u, k, a, bank, n=None):
                unit(u)
                for f in range(FT):
                    if n is not None:
                        y_made(n, k, f, bank[f])
                    if k == 0 and a + f + 1 > FT:
                        pe.wait_ge(acc_free, a + f + 1 - FT)
                    for kk in range(HK):
                        kt = HK * k + kk
                        cols = slice(f * P, f * P + P)
                        pe.matmul(ps[:, bank[f], :], half(w_hi, u)[:, kk, cols],
                                  y[:, kt, :, :].rearrange("p a b -> p (a b)"), start=kt == 0, stop=False)
                        mm = pe.matmul(ps[:, bank[f], 0:TOK], half(w_lo, u)[:, kk, cols], y[:, kt, 0, :],
                                       start=False, stop=kt == KT - 1)
                    if k == PER_GROUP - 1 and f < FT - 1:
                        mm.then_inc(acc_done, 1)
                mm.then_inc(unit_used, 1)

            def s5_turn():
                pe.wait_ge(s5_pads, 2)
                pe.wait_ge(y_lo_ready, 3 * KT)
                for ri in range(2):
                    for q in range(UT):
                        mm = pe.transpose(ps[:, 4 + ri, q * P:q * P + P],
                                          b_pad[:, ri, 4 * q:4 * q + 4, :, :].rearrange("p a b c -> p (a b c)"),
                                          ident[:, :])
                for ri in range(2):
                    for q in range(UT):
                        mm = pe.transpose(ps[:, 6 + ri, q * P:q * P + P],
                                          c_pad[:, ri, q, :, :].rearrange("p a b -> p (a b)"), ident[:, :])
                mm.then_inc(s5_turned, 1)

            def gates(g, tiles):
                if tiles[0] == 0:
                    pe.wait_ge(wai_loaded, 32 * (g + 1))
                    pe.wait_ge(xc_ready, g + 1)
                for f in tiles:
                    if FT * g + f >= 2:
                        pe.wait_ge(gates_read, FT * g + f - 1)
                    pe.matmul(ps[:, 4 + f % 2, 0:TOK], wai[:, 0, f, :], xc[g][:, f, :], start=True, stop=True,
                              skip_group_check=True)
                    pe.matmul(ps[:, 4 + f % 2, TOK:2 * TOK], wai[:, 1, f, :], xc[g][:, f, :], start=False, stop=True,
                              skip_group_check=True).then_inc(gates_done, 1)

            def s5_in(j):
                q, jj = j // 4, j % 4
                rows = slice(32 * jj, 32 * jj + 32)
                if j == 0:
                    pe.wait_ge(s5_mats, 2)
                    pe.wait_ge(acc_free, A_CD + FT)
                else:
                    pe.wait_ge(bu_free, j)
                for ri in range(2):
                    mm = pe.matmul(ps[:, 6, ri * TOK:ri * TOK + TOK], bb[rows, ri, q, :], ut[rows, q, :],
                                   start=ri == 0, stop=True, skip_group_check=True)
                mm.then_inc(bu_done, 1)

            def s5_out(j):
                q, jj = j // 4, j % 4
                rows = slice(32 * jj, 32 * jj + 32)
                pe.wait_ge(st_ready, j + 1)
                if q and jj == 0:
                    pe.wait_ge(y5_ready, q)
                for ri in range(2):
                    mm = pe.matmul(ps[rows, 7, 0:TOK], cc[:, ri, q, rows], st[:, j % 2, ri, :],
                                   start=ri == 0, stop=ri == 1)
                mm.then_inc(y5_done, 1)

            def glu():
                pe.wait_ge(glu_in, 1)
                pe.wait_ge(glu_loaded, 16)
                for f in range(UT):
                    for k in range(UT):
                        mm = pe.matmul(ps[:, 4 + f, 0:TOK], w_glu[:, k, f * P:f * P + P], ut[:, k, :],
                                       start=k == 0, stop=k == UT - 1)
                    mm.then_inc(glu_done, 1)

            def cd_step(m):
                if m == 3:
                    s5_turn()
                if m in S5_OUT:
                    s5_out(S5_OUT.index(m))
                if m in S5_AT:
                    s5_in(S5_AT.index(m))
                for g, at_ in enumerate(LRU_AT):
                    if m == at_ + 7:
                        gates(g, (0, 1))
                    if m == at_ + 7:
                        gates(g, (2, 3))

            def mix_cd():
                for n in range(len(CD_GROUPS)):
                    a = A_CD + FT * n
                    for k in range(PER_GROUP):
                        m = PER_GROUP * n + k
                        fm_rot(U_CD + m, k, a, [mix_bank(a + f) for f in range(FT)], 2 if n == 0 else None)
                        cd_step(m)

            def ab_ready(k):
                kt = HK * k + HK
                if kt <= SB_HEADS:
                    pe.wait_ge(att_lo, kt)
                else:
                    pe.wait_ge(o_lo, kt - SB_HEADS)

            def ffn_ready(layer, k):
                pe.wait_ge(ffn_lo, UP_ITERS * layer + HK * k // FT + 1)

            def cd_ready(k):
                kt = HK * k + HK
                if kt <= LT:
                    pe.wait_ge(o_lo, XT + kt)
                else:
                    pe.wait_ge(g5_lo, kt - LT)

            turn_first_params()
            norm(0)
            mix_ab()
            out_proj(U_OUT0, A_OUT0, PER_GROUP, cat, ab_ready, A_OUT0)
            norm(1)
            up_proj(U_UP0, A_UP0, 1)
            out_proj(U_DOWN0, A_DOWN0, DOWN_PER, hff, lambda k: ffn_ready(0, k), A_DOWN0 - FT)
            norm(2)
            mix_cd()
            out_proj(U_OUT1, A_OUT1, PER_GROUP, cat, cd_ready, A_OUT1 - TT, glu)
            norm(3)
            up_proj(U_UP1, A_UP1, 3)
            out_proj(U_DOWN1, A_DOWN1, DOWN_PER, hff, lambda k: ffn_ready(1, k), A_DOWN1 - FT)

        @block.scalar
        def _(act):
            chain = [0]

            def link(ins):
                chain[0] += 1
                ins.then_inc(a_chain, 1)
                act.wait_ge(a_chain, chain[0])

            def split(u, it=None, per=0):
                act.wait_ge(raw_loaded[u % RING], plus(16 * (u // RING + 1), it, 16 * per // RING))
                if u >= RING:
                    act.wait_ge(unit_used, plus(u - RING + 1, it, per))
                act.activation(w_hi[:, u % RING, :], raw[:, u % RING, :], ACT.Copy).then_inc(hi_ready, 1)

            def squares(i, free, count):
                act.wait_ge(ssq_ready, count)
                act.activation(tiny[:, 50:51], ones[:, 0:1], ACT.Sqrt)
                act.wait_ge(acc_free, free)
                for tt in range(TT):
                    act.activation(tmp[:, 2 * tt:2 * tt + 2, :].rearrange("p a b -> p (a b)"),
                                   res[:, tt, bass.ds(i * COLS, COLS)], ACT.Square,
                                   accum_out=ssq[:, tt, bass.ds(i, 1)]).then_inc(ssq_ready, 1)

            def out_proj(u, a, per, n_norm, last=False):
                n = CHUNKS - 1
                count = TT * CHUNKS * n_norm
                with act.Fori(0, n) as i:
                    for k in range(per):
                        split(u + k + RING, i, per)
                    squares(i, i * TT + (a + TT), i * TT + count)
                for k in range(per - (RING if last else 1)):
                    split(u + n * per + k + RING)
                squares(n, a + CHUNKS * TT, count + TT * n)

            def up_proj(u, layer):
                done = UP_ITERS * layer
                with act.Fori(0, UP_ITERS) as i:
                    for k in range(PER_GROUP - 1):
                        split(u + k + RING, i, 2 * PER_GROUP)
                    act.wait_ge(unit_used, i * 2 * PER_GROUP + (u + PER_GROUP))
                    act.activation(tmp[:, :, :], ps[:, 0:FT, TOK:2 * TOK], ACT.Copy).then_inc(half_copied, 1)
                    split(u + PER_GROUP - 1 + RING, i, 2 * PER_GROUP)
                    for k in range(PER_GROUP, 2 * PER_GROUP - 1):
                        split(u + k + RING, i, 2 * PER_GROUP)
                        if k == PER_GROUP + 1:
                            act.wait_ge(ffn_conv, i + (done + 1))
                            act.activation(cv[:, :, :], cv[:, :, :], ACT.Silu).then_inc(ffn_act, 1)
                    act.wait_ge(unit_used, i * 2 * PER_GROUP + (u + 2 * PER_GROUP))
                    act.activation(ffn_tv[:, :, :], ps[:, FT:2 * FT, TOK:2 * TOK], ACT.Copy).then_inc(half_copied, 1)
                    split(u + 2 * PER_GROUP - 1 + RING, i, 2 * PER_GROUP)
                    act.wait_ge(ffn_h, i + (done + 1))
                    act.activation(hff[:, bass.ds(i * FT, FT), 0, :], ffn_v[:, :, :], ACT.Copy).then_inc(ffn_hi, 1)

            def norm(n):
                if n == 0:
                    act.wait_ge(consts_ready, 1)
                    act.activation(tiny[:, 50:51], ones[:, 0:1], ACT.Sqrt)
                    for tt in range(TT):
                        act.wait_ge(x_loaded[tt], 16)
                        for i in range(CHUNKS):
                            cols = slice(i * COLS, (i + 1) * COLS)
                            act.activation(xn[:, tt, cols], res[:, tt, cols], ACT.Square,
                                           accum_out=ssq[:, tt, i:i + 1]).then_inc(ssq_ready, 1)
                act.wait_ge(ms_ready, n + 1)
                act.activation(tiny[:, 4:6], tiny[:, 2:4], ACT.Sqrt).then_inc(sd_ready, 1)
                act.wait_ge(rstd_ready, n + 1)
                if n == 4:
                    return

                def scale(c):
                    cols = slice(c * COLS, (c + 1) * COLS)
                    act.activation(xn[:, 0, cols], res[:, 0, cols], ACT.Copy, scale=tiny[:, 6:7]).then_inc(xn0_ready, 1)

                def highs(b):
                    act.wait_ge(turned, KT // 2 * n + b + 1)
                    name = ("norm_mix", "norm_ffn")[n % 2]
                    for j in range(2):
                        kt = 2 * b + j
                        act.activation(y[:, kt, 0, :], ps[:, b, j * TOK:(j + 1) * TOK], ACT.Copy,
                                       scale=pcol(name, KT * (n // 2) + kt)).then_inc(y_hi_ready, 1)

                scale(0)
                if n == 0:
                    split(0)
                for c in range(CHUNKS):
                    if c + 1 < CHUNKS:
                        scale(c + 1)
                        if n == 0:
                            split(c + 1)
                    if n == 0 and c == 0:
                        act.wait_ge(params_ready, 1)
                    highs(2 * c)
                    highs(2 * c + 1)
                    if n and c == 2:
                        split(NEXT[n] + RING - 1)

            def row_loads(rows_of, loaded):
                for name, r, tile, p, m in rows_of:
                    src = t[name]
                    dims = " ".join("abc"[:len(src.shape)])
                    rows = src.rearrange(f"{dims} -> ({dims})").rearrange("(r p) -> r p", p=P)
                    act.dma_start(prow[p:p + m, tile, :], rows[r:r + m, :]).then_inc(loaded, 16)

            def small_loads():
                act.dma_start(tiny[0:SSD_HEADS, 16:17], t["ab_dt_bias"].rearrange("a h -> h a")).then_inc(small_loaded, 16)
                act.dma_start(tiny[0:SSD_HEADS, 17:18], t["ab_a_log"].rearrange("a h -> h a")).then_inc(small_loaded, 16)
                heads = t["ab_d_skip"].rearrange("a (t j) -> a j t", j=2)
                steps = t["cd_log_dt"].rearrange("a (t j) -> a j t", j=2)
                with nc.allow_non_contiguous_dma(reason="two small vectors, once"):
                    for j in range(2):
                        act.dma_start(tiny[j * 64:j * 64 + 64, 20:20 + XT],
                                      heads[0, j:j + 1, :].broadcast_to([64, XT])).then_inc(small_loaded, 16)
                        act.dma_start(s5p[j * 64:j * 64 + 64, LOGDT, :],
                                      steps[0, j:j + 1, :].broadcast_to([64, ST])).then_inc(small_loaded, 16)

            def decays(h):
                act.wait_ge(cs_spread, h // 2 + 1)
                if h >= 4:
                    act.wait_ge(m_ready, h - 3)
                j = h % 2
                b = flat(blk[h % 4])
                act.activation(b[:, 0:TOK], ps[:, 5, j * TOK:j * TOK + TOK], ACT.Relu, scale=-1.0,
                               bias=cs_t[:, 0, h:h + 1])
                link(act.activation(b[:, TOK:3 * P], ps[:, 5, j * TOK + P:j * TOK + TOK], ACT.Relu, scale=-1.0,
                                    bias=cs_t[:, 1, h:h + 1]))
                act.activation(b, b, ACT.Exp, scale=-1.0).then_inc(decay_ready, 1)

            def log_scores(h):
                act.wait_ge(zs_done, h + 1)
                b = flat(z_ln[h])
                link(act.activation(b, ps[:, 4 + h, 0:3 * P], ACT.Abs))
                link(act.activation(b, b, ACT.Exp, scale=-1.0))
                act.activation(b, b, ACT.Ln, bias=1.0).then_inc(ln_ready, 1)

            def ab_step(m):
                if m < 5:
                    row_loads(pieces(False)[m::5], rows_loaded)
                if m == 5:
                    small_loads()
                for g, at_ in enumerate(CONV_AT):
                    if m == at_ + 1:
                        if g == 0:
                            act.wait_ge(params_ready, 2)
                        act.wait_ge(acc_free, A_AB + FT * (g + 1))
                        if g:
                            act.wait_ge(xact, g)
                        for f in range(FT):
                            n = FT * g + f
                            ins = act.activation(cv[:, f, :], xbc[:, n, :], ACT.Identity, bias=pcol("ab_conv_b", n),
                                                 scale=pcol("ab_conv_w", (SSD_CONV - 1) * 20 + n))
                        ins.then_inc(xtap0, 1)
                    if m == at_ + 4:
                        act.wait_ge(xconv, g + 1)
                        act.activation(xbc[:, FT * g:FT * g + FT, :], cv[:, :, :], ACT.Silu).then_inc(xact, 1)
                if m == DT_AT + 3:
                    act.wait_ge(small_loaded, 96)
                    act.activation(tiny[0:SSD_HEADS, 18:19], tiny[0:SSD_HEADS, 17:18], ACT.Exp).then_inc(dt_a, 1)
                    act.wait_ge(dt_abs, 1)
                    act.activation(dt_w1, dt_w1, ACT.Exp, scale=-1.0).then_inc(dt_exp, 1)
                if m == DT_AT + 3:
                    act.wait_ge(dt_w, 1)
                    act.activation(dt_w3, dt_w2, ACT.Ln).then_inc(dt_ln, 1)
                for g, at_ in enumerate(Z_AT):
                    if m == at_:
                        act.wait_ge(acc_free, A_AB + 5 * FT + 1 + FT * (g + 1))
                        act.activation(zg[:, FT * g:FT * g + FT, :],
                                       zg[:, FT * g:FT * g + FT, :], ACT.Silu).then_inc(z_act, 1)
                for n, at_ in enumerate(PAIR_AT):
                    if m == at_:
                        if n == 0:
                            act.wait_ge(cs_t_ready, 1)
                        decays(2 * n)
                        decays(2 * n + 1)
                for stage, at_ in enumerate((60, 65, 71)):
                    if m == at_:
                        s5_prep(stage)
                if m == GNORM_AT + 2:
                    act.wait_ge(gn_ms, 1)
                    act.activation(cv[:, 0, :], cv[:, 0, :], ACT.Sqrt).then_inc(gn_sd, 1)
                for q in range(XT // FT):
                    if m == GNORM_AT + 4 + q:
                        for n in range(FT * q, FT * q + FT):
                            act.wait_ge(o_ready, n + 1)
                            act.activation(cat[:, SB_HEADS + n, 0, :], zg[:, n, :], ACT.Copy).then_inc(o_hi, 1)
                for h, at_ in enumerate(HEAD_AT):
                    if m == at_ + 2:
                        act.wait_ge(zs_full, h + 1)
                        act.activation(flat(probs[h]), ps[:, 4 + h, 0:3 * P], ACT.Exp).then_inc(w_exp, 1)
                    if m == at_:
                        log_scores(h)

            def group(kind, u, a, d, step=None):
                per = DT_UNITS if kind == "dt" else PER_GROUP
                for k in range(per):
                    if k == per - 1 and kind != "v":
                        for f in range(1 if kind == "dt" else FT):
                            if kind == "dt" or f == FT - 1:
                                act.wait_ge(unit_used, u + per)
                            else:
                                act.wait_ge(acc_done, d + f + 1)
                            act.activation(tmp[:, mix_bank(a + f), :], ps[:, mix_bank(a + f), TOK:2 * TOK], ACT.Copy,
                                           scale=SB_DH ** -0.5 if kind == "q" else 1.0).then_inc(half_copied, 1)
                    split(u + k + RING)
                    if step is not None:
                        step(k)
                return u + per, a + {"dt": 1, "v": TT}.get(kind, FT), d + D_OF.get(kind, FT - 1)

            def mix_ab():
                u, a, d, m = U_AB, A_AB, D_AB, 0
                for kind, _ in AB_GROUPS:
                    u, a, d = group(kind, u, a, d, lambda k: ab_step(m + k))
                    m = u - U_AB
                for h in range(SB_HEADS):
                    act.wait_ge(att_done, h + 1)
                    act.activation(cat[:, h, 0, :], ps[:, 4 + h, 0:TOK], ACT.Copy).then_inc(att_hi, 1)

            def s5_prep(stage):
                if stage == 0:
                    act.wait_ge(small_loaded, 96)
                    act.activation(s5(DTV), s5(LOGDT), ACT.Exp).then_inc(s5a, 1)
                elif stage == 1:
                    act.wait_ge(s5v, 1)
                    act.activation(s5(TH), s5(XDT), ACT.Tanh, scale=0.5)
                    act.activation(s5(MAG), s5(XDT), ACT.Exp)
                    act.activation(s5(SINH), s5(TURN), ACT.Sin, scale=0.5)
                    act.activation(s5(SIN), s5(TURN), ACT.Sin).then_inc(s5a, 1)
                    lam = params[:, COL["cd_lambda"]:COL["cd_lambda"] + LT]
                    link(act.activation(tiny[:, 32:44], lam, ACT.Abs))
                    act.activation(s5p[:, T0, 0:LT], tiny[:, 32:44], ACT.Exp, scale=-1.0).then_inc(s5a, 1)
                else:
                    act.wait_ge(s5v, 2)
                    act.activation(s5p[:, T1, 0:LT], s5p[:, T2, 0:LT], ACT.Ln).then_inc(s5a, 1)

            def bc_loads():
                for ri, name in enumerate(("cd_b_re", "cd_b_im")):
                    act.dma_start(b_raw[:, ri, :, :], t[name][0].rearrange("(j g) n c -> (g n) j c", g=2)
                                  ).then_inc(bc_loaded, 16)
                for ri, name in enumerate(("cd_c_re", "cd_c_im")):
                    for gl in range(2):
                        act.dma_start(c_pad[:, ri, :, gl, :], t[name][0].rearrange("g c n -> (g c) n").rearrange(
                            "(q p) n -> p q n", p=P)).then_inc(bc_loaded, 16)

            def load_gate_weights(g):
                for m, name in enumerate(("cd_w_a", "cd_w_i")):
                    act.dma_start(wai[:, m, :, :], t[name][0, FT * g:FT * g + FT].rearrange("b i j -> i b j")
                                  ).then_inc(wai_loaded, 16)

            def gate_sigmoids(g, tiles):
                for f in tiles:
                    n = FT * g + f
                    act.wait_ge(gates_done, n + 1)
                    act.activation(lru_r[:, f, :], ps[:, 4 + f % 2, 0:TOK], ACT.Sigmoid, bias=pcol("cd_b_a", n))
                    act.activation(lru_i[:, f, :], ps[:, 4 + f % 2, TOK:2 * TOK], ACT.Sigmoid,
                                   bias=pcol("cd_b_i", n)).then_inc(gates_read, 1)

            def lru_decay(g):
                act.wait_ge(gates_read, FT * (g + 1))
                for f in range(FT):
                    n = FT * g + f
                    ins = act.activation(hs[:, n, :], lru_r[:, f, :], ACT.Exp, scale=c8[:, n:n + 1])
                link(ins)

            def lru_complement(g):
                for f in range(FT):
                    n = FT * g + f
                    act.activation(lru_r[:, f, :], lru_r[:, f, :], ACT.Tanh, scale=c8[:, n:n + 1])
                act.wait_ge(gx_ready, g + 1)
                act.activation(lru_i[:, :, :], hs[:, FT * g:FT * g + FT, :], ACT.Square).then_inc(decayed, 1)

            def cd_step(m):
                for g, at_ in enumerate(LRU_AT):
                    if m == at_ + 1:
                        if g == 2:
                            act.wait_ge(hs_ready, FT)
                        act.wait_ge(acc_free, A_CD + FT * (g + 2))
                        for f in range(FT):
                            n = FT * g + f
                            ins = act.activation(xc[g][:, f, :], xin[:, f, :], ACT.Identity, bias=pcol("cd_conv_b", n),
                                                 scale=pcol("cd_conv_w", (LRU_CONV - 1) * LT + n))
                        ins.then_inc(tap0_ready, 1)
                    if m == at_ + 6:
                        gate_sigmoids(g, (0, 1))
                    if m == at_ + 7:
                        gate_sigmoids(g, (2, 3))
                        if g + 1 < LT // FT:
                            load_gate_weights(g + 1)
                    if m == at_ + 8:
                        lru_decay(g)
                    if m == at_ + 9:
                        lru_complement(g)
                    if m == at_ + 11:
                        act.wait_ge(lru_q, g + 1)
                        act.activation(lru_r[:, :, :], lru_r[:, :, :], ACT.Sqrt, scale=-1.0).then_inc(lru_sd, 1)
                if m == S5_END:
                    act.wait_ge(y5_ready, UT)
                    link(act.activation(s5_gelu[:, :, :], ut[:, :, :], ACT.Square))
                    act.activation(s5_gelu[:, :, :], s5_gelu[:, :, :], ACT.Copy, bias=1.0, scale=GELU_K
                                   ).then_inc(s5_sq, 1)
                if m == S5_END + 1:
                    act.wait_ge(s5_u, 1)
                    act.activation(s5_gelu[:, :, :], s5_gelu[:, :, :], ACT.Tanh, scale=GELU_C).then_inc(s5_th, 1)
                for g, at_ in enumerate(GATE_AT):
                    if m == at_:
                        act.wait_ge(acc_free, A_CD + FT * (g + 5))
                        link(act.activation(cd_tmp[:, :, :], xin[:, :, :], ACT.Square))
                        act.activation(cd_tmp[:, :, :], cd_tmp[:, :, :], ACT.Copy, bias=1.0, scale=GELU_K
                                       ).then_inc(gelu_sq, 1)
                    if m == at_ + 3:
                        act.wait_ge(gelu_u, g + 1)
                        act.activation(cd_tmp[:, :, :], cd_tmp[:, :, :], ACT.Tanh, scale=GELU_C).then_inc(gelu_th, 1)
                    if m == at_ + 6:
                        if g == 0:
                            act.wait_ge(hs_ready, LT)
                            act.dma_start(w_glu[:, :, :], t["cd_w_glu"][0].rearrange("(k p) n -> p k n", p=P)
                                          ).then_inc(glu_loaded, 16)
                        for f in range(FT):
                            act.wait_ge(o_ready, XT + FT * g + f + 1)
                            act.activation(cat[:, FT * g + f, 0, :], xin[:, f, :], ACT.Copy, scale=0.5
                                           ).then_inc(o_hi, 1)

            def mix_cd():
                u, a, d = U_CD, A_CD, D_CD
                for n, (kind, _) in enumerate(CD_GROUPS):
                    u, a, d = group(kind, u, a, d, lambda k: cd_step(PER_GROUP * n + k))
                for m in range(CD_UNITS, CD_STEPS):
                    cd_step(m)
                for f in range(UT):
                    act.wait_ge(glu_done, f + 1)
                    act.activation(s5_gate[:, f, :], ps[:, 4 + f, 0:TOK], ACT.Sigmoid,
                                   bias=pcol("cd_b_glu", f)).then_inc(glu_act, 1)
                for f in range(UT):
                    act.wait_ge(g5_ready, f + 1)
                    act.activation(cat[:, LT + f, 0, :], ut[:, f, :], ACT.Copy).then_inc(g5_hi, 1)

            row_loads(pieces(True), first_loaded)
            norm(0)
            mix_ab()
            out_proj(U_OUT0, A_OUT0, PER_GROUP, 1)
            norm(1)
            bc_loads()
            load_gate_weights(0)
            up_proj(U_UP0, 0)
            out_proj(U_DOWN0, A_DOWN0, DOWN_PER, 2)
            norm(2)
            mix_cd()
            out_proj(U_OUT1, A_OUT1, PER_GROUP, 3)
            norm(3)
            up_proj(U_UP1, 1)
            act.wait_ge(ffn_lo, 2 * UP_ITERS)
            act.dma_start(g_fin[:, :], t["norm_final"].rearrange("(a d) -> a d", a=1).broadcast_to([P, D])
                          ).then_inc(gfin_loaded, 16)
            out_proj(U_DOWN1, A_DOWN1, DOWN_PER, 4, last=True)
            norm(4)
            for tt in range(TT):
                for c in range(CHUNKS):
                    act.wait_ge(out_ready, CHUNKS * tt + c + 1)
                    act.dma_start(out[0, tt * P:tt * P + P, c * COLS:(c + 1) * COLS],
                                  xn[:, tt, c * COLS:(c + 1) * COLS]).then_inc(stored, 16)
            act.wait_ge(stored, 16 * TT * CHUNKS)

        @block.vector
        def _(dve):
            made, base_at = [0], [None]

            def mark(ins):
                made[0] += 1
                return ins.then_inc(v_chain, 1)

            def join():
                dve.wait_ge(v_chain, made[0] if base_at[0] is None else base_at[0] + made[0])

            def link(ins):
                mark(ins)
                join()

            def split(u, it=None, per=0):
                dve.wait_ge(hi_ready, plus(u + 1, it, per))
                dve.tensor_tensor(w_lo[:, u % RING, :], raw[:, u % RING, :], w_hi[:, u % RING, :],
                                  ALU.subtract).then_inc(lo_ready, 1)

            def out_proj(u, d, per, last=False):
                n = CHUNKS - 1

                def add(i, cols, banks, done):
                    for tt in range(TT):
                        if tt < TT - 1:
                            dve.wait_ge(acc_done, plus(d + done + 1, i, 1))
                        else:
                            dve.wait_ge(unit_used, plus(u + (done + 1) * per, i, per))
                        r = res[:, tt, cols]
                        dve.tensor_tensor(r, banks(tt), r, ALU.add).then_inc(acc_free, 1)

                with dve.Fori(0, n) as i:
                    for k in range(per - 1):
                        split(u + k + RING, i, per)
                    add(i, bass.ds(i * COLS, COLS), lambda tt: ps[:, bass.ds(i * TT + tt, 1), :], 0)
                    split(u + per - 1 + RING, i, per)
                for k in range(per - (RING if last else 1)):
                    split(u + n * per + k + RING)
                add(None, slice(n * COLS, D), lambda tt: ps[:, n * TT + tt, :], n)

            def up_proj(u, a, h, layer):
                done = UP_ITERS * layer
                per = 2 * PER_GROUP
                chain0 = made[0]
                with dve.Fori(0, UP_ITERS) as i:
                    base_at[0] = i * 2

                    def weight(tap, f):
                        c = COL["ffn_conv_w"] + (layer * FFN_CONV + tap) * HT + f
                        return params[:, bass.ds(i * FT + c, 1)]

                    for k in range(PER_GROUP - 1):
                        split(u + k + RING, i, per)
                    dve.wait_ge(half_copied, i * 2 + (h + 1))
                    for f in range(FT):
                        dve.tensor_tensor(ffn_g[:, f, :], ps[:, f, 0:TOK], tmp[:, f, :], ALU.add).then_inc(acc_free, 1)
                    dve.wait_ge(acc_free, i * 2 * FT + (a + FT))
                    for f in range(FT):
                        bias = params[:, bass.ds(i * FT + (COL["ffn_conv_b"] + layer * HT + f), 1)]
                        ins = dve.tensor_scalar(cv[:, f, :], ffn_g[:, f, :], weight(2, f), bias, ALU.mult, ALU.add)
                    link(ins)
                    for lag in (1, 2):
                        for f in range(FT):
                            c = cv[:, f, lag:TOK]
                            ins = dve.scalar_tensor_tensor(out=c, in0=ffn_g[:, f, 0:TOK - lag], scalar=weight(2 - lag, f),
                                                           in1=c, op0=ALU.mult, op1=ALU.add)
                        if lag == 1:
                            link(ins)
                            split(u + PER_GROUP - 1 + RING, i, per)
                    ins.then_inc(ffn_conv, 1)
                    for k in range(PER_GROUP, per - 1):
                        split(u + k + RING, i, per)
                    dve.wait_ge(half_copied, i * 2 + (h + 2))
                    for f in range(FT):
                        dve.tensor_tensor(ffn_v[:, f, :], ps[:, FT + f, 0:TOK], ffn_tv[:, f, :], ALU.add
                                          ).then_inc(acc_free, 1)
                    dve.wait_ge(ffn_act, i + (done + 1))
                    dve.wait_ge(acc_free, i * 2 * FT + (a + 2 * FT))
                    dve.tensor_tensor(ffn_v[:, :, :], ffn_v[:, :, :], cv[:, :, :], ALU.mult).then_inc(ffn_h, 1)
                    split(u + per - 1 + RING, i, per)
                    dve.wait_ge(ffn_hi, i + (done + 1))
                    dve.tensor_tensor(hff[:, bass.ds(i * FT, FT), 1, :], ffn_v[:, :, :],
                                      hff[:, bass.ds(i * FT, FT), 0, :], ALU.subtract).then_inc(ffn_lo, 1)
                assert made[0] - chain0 == 2
                made[0] = chain0 + 2 * UP_ITERS
                base_at[0] = None

            def norm(n):
                dve.wait_ge(ssq_ready, TT * CHUNKS * (n + 1))
                link(dve.reduce_sum(tiny[:, 0:2], ssq[:, :, :], axis=mybir.AxisListType.X))
                dve.tensor_scalar(tiny[:, 2:4], tiny[:, 0:2], 1.0 / D, EPS, ALU.mult, ALU.add).then_inc(ms_ready, 1)
                dve.wait_ge(sd_ready, n + 1)
                dve.reciprocal(tiny[:, 6:8], tiny[:, 4:6]).then_inc(rstd_ready, 1)
                dve.wait_ge(rstd_ready, n + 1)
                if n == 4:
                    dve.wait_ge(gfin_loaded, 16)
                    for tt in range(TT):
                        for c in range(CHUNKS):
                            cols = slice(c * COLS, (c + 1) * COLS)
                            dve.scalar_tensor_tensor(
                                out=xn[:, tt, cols], in0=res[:, tt, cols], scalar=tiny[:, 6 + tt:7 + tt],
                                in1=g_fin[:, cols], op0=ALU.mult, op1=ALU.mult).then_inc(out_ready, 1)
                    return
                for c in range(CHUNKS):
                    cols = slice(c * COLS, (c + 1) * COLS)
                    dve.tensor_scalar(xn[:, 1, cols], res[:, 1, cols], tiny[:, 7:8], None, ALU.mult).then_inc(xn1_ready, 1)
                if n == 0:
                    dve.wait_ge(rows_turned, 1)
                    dve.tensor_copy(params[:, 0:P], ps[:, 0, 0:P]).then_inc(params_ready, 1)
                    dve.wait_ge(params_ready, 1)
                name = ("norm_mix", "norm_ffn")[n % 2]
                for kt in range(KT):
                    if n == 0 and kt % 4 == 0:
                        split(kt // 4)
                    if n and kt == 12:
                        split(NEXT[n] + RING - 1)
                    dve.wait_ge(y_hi_ready, KT * n + kt // 2 * 2 + 2)
                    dve.scalar_tensor_tensor(out=y[:, kt, 1, :], in0=ps[:, kt // 2, kt % 2 * TOK:(kt % 2 + 1) * TOK],
                                             scalar=pcol(name, KT * (n // 2) + kt), in1=y[:, kt, 0, :],
                                             op0=ALU.mult, op1=ALU.subtract).then_inc(y_lo_ready, 1)

            def param_columns():
                dve.wait_ge(rows_turned, 2)
                dve.tensor_copy(params[:, P:NPARAM], ps[:, 4, 0:NPARAM - P]).then_inc(params_ready, 1)
                dve.wait_ge(params_ready, 2)
                dve.wait_ge(consts_ready, 5)
                link(dve.reduce_sum(parity, strips.rearrange("p (k g) -> p g k", g=2), axis=mybir.AxisListType.X))

            def group(kind, u, a, d, h, dst, step=None):
                per = DT_UNITS if kind == "dt" else PER_GROUP
                for k in range(per):
                    if k == per - 1:
                        if kind == "v":
                            for tt in range(TT):
                                if tt < TT - 1:
                                    dve.wait_ge(acc_done, d + tt + 1)
                                else:
                                    dve.wait_ge(unit_used, u + per)
                                dve.tensor_copy(dst(tt), ps[:, mix_bank(a + tt), :]).then_inc(acc_free, 1)
                        else:
                            for f in range(1 if kind == "dt" else FT):
                                dve.wait_ge(half_copied, h + f + 1)
                                rows = slice(0, SSD_HEADS) if kind == "dt" else slice(0, P)
                                dve.scalar_tensor_tensor(
                                    out=dst(f), in0=ps[rows, mix_bank(a + f), 0:TOK],
                                    scalar=SB_DH ** -0.5 if kind == "q" else 1.0, in1=tmp[rows, mix_bank(a + f), :],
                                    op0=ALU.mult, op1=ALU.add).then_inc(acc_free, 1)
                    split(u + k + RING)
                    if step is not None:
                        step(k)
                a += {"dt": 1, "v": TT}.get(kind, FT)
                d += D_OF.get(kind, FT - 1)
                h += {"dt": 1, "v": 0}.get(kind, FT)
                dve.wait_ge(acc_free, a)
                return u + per, a, d, h

            def conv_tap(g, lag):
                for f in range(FT):
                    n = FT * g + f
                    c = cv[:, f, lag:TOK]
                    ins = dve.scalar_tensor_tensor(out=c, in0=xbc[:, n, 0:TOK - lag],
                                                   scalar=pcol("ab_conv_w", (SSD_CONV - 1 - lag) * 20 + n), in1=c,
                                                   op0=ALU.mult, op1=ALU.add)
                if lag < SSD_CONV - 1:
                    link(ins)
                else:
                    ins.then_inc(xconv, 1)

            def dt_step(k):
                d, eq = dts[:, :], cs[:, :]
                if k == 2:
                    dve.wait_ge(small_loaded, 96)
                    link(dve.tensor_scalar(dt_w0, dt_w0, tiny[0:SSD_HEADS, 16:17], None, ALU.add))
                    dve.scalar_tensor_tensor(out=dt_w1, in0=dt_w0, scalar=-1.0, in1=dt_w0, op0=ALU.mult, op1=ALU.max
                                             ).then_inc(dt_abs, 1)
                if k == 3:
                    dve.wait_ge(dt_exp, 1)
                    dve.tensor_scalar(dt_w2, dt_w1, 1.0, None, ALU.add).then_inc(dt_w, 1)
                    dve.wait_ge(dt_w, 1)
                    link(dve.tensor_scalar(d, dt_w2, -1.0, None, ALU.add))
                    link(dve.tensor_scalar(eq, d, 0.0, None, ALU.is_equal))
                    link(dve.tensor_tensor(d, d, eq, ALU.add))
                    link(dve.reciprocal(d, d))
                if k == 4:
                    dve.wait_ge(dt_ln, 1)
                    link(dve.tensor_tensor(dt_w2, dt_w1, d, ALU.mult))
                    link(dve.tensor_tensor(dt_w3, dt_w3, dt_w2, ALU.mult))
                    link(dve.tensor_tensor(dt_w2, dt_w1, eq, ALU.mult))
                    link(dve.tensor_tensor(dt_w3, dt_w3, dt_w2, ALU.add))
                    link(dve.scalar_tensor_tensor(out=d, in0=dt_w0, scalar=0.0, in1=dt_w3, op0=ALU.max, op1=ALU.add))
                    dve.wait_ge(dt_a, 1)
                    link(dve.tensor_scalar(dt_w1, d, tiny[0:SSD_HEADS, 18:19], -1.0, ALU.mult, ALU.mult))
                    dve.tensor_tensor_scan(eq, ones[0:SSD_HEADS, 0:1].broadcast_to([SSD_HEADS, TOK]), dt_w1, 0.0,
                                           ALU.mult, ALU.add).then_inc(cs_ready, 1)
                if k == 8:
                    dve.wait_ge(cs_turned, 1)
                    dve.tensor_copy(dt_t[:, :, :], ps[:, 7, 0:64].rearrange("p (a b) -> p a b", a=TT)[:, :, 0:SSD_HEADS])
                    dve.tensor_copy(cs_t[:, :, :], ps[:, 7, 64:128].rearrange("p (a b) -> p a b", a=TT)[:, :, 0:SSD_HEADS]
                                    ).then_inc(cs_t_ready, 1)
                    dve.wait_ge(cs_t_ready, 1)

            def x_times_dt(n):
                tt, q = n % TT, n // TT
                dve.wait_ge(x_turned, n + 1)
                dve.tensor_tensor(
                    xdt[:, tt, q * COLS:(q + 1) * COLS].rearrange("p (h c) -> p h c", c=SSD_P),
                    ps[:, 4 + n % 3, :].rearrange("p (h c) -> p h c", c=SSD_P),
                    dt_t[:, tt, 8 * q:8 * q + 8].unsqueeze(2).broadcast_to([P, 8, SSD_P]),
                    ALU.mult).then_inc(xdt_ready, 1)

            def decayed_products(n):
                for h in (2 * n, 2 * n + 1):
                    dve.wait_ge(cb_done, h // RH + 1)
                    dve.wait_ge(decay_cut, h + 1)
                    if n >= 2:
                        dve.wait_ge(yh_done, n - 1)
                    dve.tensor_tensor(flat(decayed_cb[h % 4]), ps[:, 4, 0:3 * P], flat(blk[h % 4]),
                                      ALU.mult).then_inc(m_ready, 1)

            def skip_and_gate(n):
                dve.wait_ge(yh_done, n + 1)
                dve.scalar_tensor_tensor(out=xbc[:, n, :], in0=xbc[:, n, :], scalar=tiny[:, 20 + n:21 + n],
                                         in1=ps[:, 6 + n % 2, 0:TOK], op0=ALU.mult, op1=ALU.add).then_inc(ys_ready, 1)
                dve.wait_ge(ys_ready, n + 1)
                dve.wait_ge(z_act, n // FT + 1)
                link(dve.tensor_tensor(xbc[:, n, :], xbc[:, n, :], zg[:, n, :], ALU.mult))
                dve.tensor_tensor(zg[:, n, :], xbc[:, n, :], xbc[:, n, :], ALU.mult).then_inc(sq_ready, 1)

            def gnorm_step(k):
                if k == 1:
                    dve.wait_ge(sq_summed, 1)
                    dve.tensor_scalar(cv[:, 0, :], ps[:, 4, 0:TOK], 1.0 / SSD_W, EPS, ALU.mult, ALU.add).then_inc(gn_ms, 1)
                if k == 2:
                    dve.wait_ge(gn_sd, 1)
                    dve.reciprocal(cv[:, 1, :], cv[:, 0, :]).then_inc(gn_rstd, 1)
                for q in range(XT // FT):
                    tiles = range(FT * q, FT * q + FT)
                    if k == 3 + q:
                        dve.wait_ge(gn_rstd, 1)
                        for n in tiles:
                            dve.scalar_tensor_tensor(out=zg[:, n, :], in0=xbc[:, n, :], scalar=pcol("ab_ssd_norm", n),
                                                     in1=cv[:, 1, :], op0=ALU.mult, op1=ALU.mult).then_inc(o_ready, 1)
                    if k == 4 + q:
                        for n in tiles:
                            dve.wait_ge(o_hi, n + 1)
                            dve.tensor_tensor(cat[:, SB_HEADS + n, 1, :], zg[:, n, :], cat[:, SB_HEADS + n, 0, :],
                                              ALU.subtract).then_inc(o_lo, 1)

            def ab_step(m):
                for g, at_ in enumerate(CONV_AT):
                    if m == at_ + 2:
                        dve.wait_ge(xtap0, g + 1)
                        conv_tap(g, 1)
                        conv_tap(g, 2)
                    if m == at_ + 3:
                        conv_tap(g, 3)
                if m == 6:
                    param_columns()
                dt_step(m - DT_AT)
                for lot, at_ in enumerate((DT_AT + 8, XT_AT[1] + 1)):
                    if m == at_:
                        for n in range(3):
                            x_times_dt(3 * lot + n)
                for n, at_ in enumerate(PAIR_AT):
                    if m == at_ + 1:
                        decayed_products(n)
                    if m == at_ + 4:
                        skip_and_gate(n)
                for stage, at_ in enumerate((62, 70, 76)):
                    if m == at_:
                        (s5_angles, lru_rates, s5_factors)[stage]()
                gnorm_step(m - GNORM_AT)
                for h, at_ in enumerate(HEAD_AT):
                    if m == at_ + 1:
                        dve.wait_ge(ln_ready, h + 1)
                        dve.scalar_tensor_tensor(out=flat(blk[h]), in0=ps[:, 4 + h, 0:3 * P], scalar=0.0,
                                                 in1=flat(z_ln[h]), op0=ALU.max, op1=ALU.add).then_inc(sp_ready, 1)

            def mix_ab():
                u, a, d, h = U_AB, A_AB, D_AB, H_AB
                n_x = n_z = m = 0
                for kind, _ in AB_GROUPS:
                    dst = {
                        "x": lambda f: xbc[:, FT * n_x + f, :],
                        "dt": lambda f: dt_w0,
                        "q": lambda f: qk[:, f, :],
                        "k": lambda f: qk[:, SB_HEADS + f, :],
                        "v": lambda tt: v_t[:, tt, :],
                        "z": lambda f: zg[:, FT * n_z + f, :],
                    }[kind]
                    u, a, d, h = group(kind, u, a, d, h, dst, lambda k: ab_step(m + k))
                    m = u - U_AB
                    n_x += kind == "x"
                    n_z += kind == "z"
                for h in range(SB_HEADS):
                    dve.wait_ge(att_hi, h + 1)
                    dve.tensor_tensor(cat[:, h, 1, :], ps[:, 4 + h, 0:TOK], cat[:, h, 0, :],
                                      ALU.subtract).then_inc(att_lo, 1)

            def tt_(o, a, b, op):
                link(dve.tensor_tensor(o, a, b, op))

            def ts_(o, a, x, op, x2=None, op2=None):
                if op2 is None:
                    link(dve.tensor_scalar(o, a, x, None, op))
                else:
                    link(dve.tensor_scalar(o, a, x, x2, op, op2))

            def s5_angles():
                li = params[:, COL["cd_a_im"]:COL["cd_a_im"] + ST]
                dve.wait_ge(s5a, 1)
                ts_(s5(LR), params[:, COL["cd_a_re"]:COL["cd_a_re"] + ST], -1e-4, ALU.min)
                tt_(s5(XDT), s5(LR), s5(DTV), ALU.mult)
                tt_(s5(THETA), li, s5(DTV), ALU.mult)
                ts_(s5(T0), s5(THETA), 0.15915494309189535, ALU.mult)
                ts_(s5(T0), s5(T0), ROUND, ALU.add)
                ts_(s5(T0), s5(T0), -ROUND, ALU.add)
                src = s5(THETA)
                for part in TWO_PI:
                    link(dve.scalar_tensor_tensor(out=s5(TURN), in0=s5(T0), scalar=-part, in1=src,
                                                  op0=ALU.mult, op1=ALU.add))
                    src = s5(TURN)
                dve.tensor_scalar(s5(TURN), s5(TURN), 3.1415925, -3.1415925, ALU.min, ALU.max).then_inc(s5v, 1)

            def lru_rates():
                lam = params[:, COL["cd_lambda"]:COL["cd_lambda"] + LT]
                dve.wait_ge(s5a, 3)
                e, w, t3, eq, low = (s5p[:, n, 0:LT] for n in (T0, T2, T3, FR, FI))
                dve.tensor_scalar(w, e, 1.0, None, ALU.add).then_inc(s5v, 1)
                dve.wait_ge(s5v, 2)
                ts_(t3, w, -1.0, ALU.add)
                ts_(eq, t3, 0.0, ALU.is_equal)
                tt_(t3, t3, eq, ALU.add)
                link(dve.reciprocal(t3, t3))
                tt_(t3, e, t3, ALU.mult)
                tt_(eq, e, eq, ALU.mult)
                ts_(low, lam, -1.0, ALU.mult, 0.0, ALU.max)

            def s5_factors():
                li = params[:, COL["cd_a_im"]:COL["cd_a_im"] + ST]
                ln, t3, eq, low = (s5p[:, n, 0:LT] for n in (T1, T3, FR, FI))
                dve.wait_ge(s5a, 4)
                tt_(ln, ln, t3, ALU.mult)
                tt_(ln, ln, eq, ALU.add)
                tt_(ln, ln, low, ALU.add)
                ts_(c8[:, :], ln, -LRU_C, ALU.mult)
                tt_(s5(SIN2), s5(SINH), s5(SINH), ALU.mult)
                dve.tensor_scalar(s5(COS), s5(SIN2), -2.0, 1.0, ALU.mult, ALU.add).then_inc(s5v, 1)
                dve.wait_ge(s5v, 3)
                ts_(s5(T2), s5(TH), -1.0, ALU.mult, 1.0, ALU.add)
                link(dve.reciprocal(s5(T2), s5(T2)))
                tt_(s5(E1), s5(TH), s5(T2), ALU.mult)
                ts_(s5(E1), s5(E1), 2.0, ALU.mult)
                tt_(s5(AM1), s5(E1), s5(COS), ALU.mult)
                link(dve.scalar_tensor_tensor(out=s5(AM1), in0=s5(SIN2), scalar=-2.0, in1=s5(AM1),
                                              op0=ALU.mult, op1=ALU.add))
                tt_(s5(ABI), s5(MAG), s5(SIN), ALU.mult)
                tt_(s5(DEN), s5(LR), s5(LR), ALU.mult)
                tt_(s5(T2), li, li, ALU.mult)
                tt_(s5(DEN), s5(DEN), s5(T2), ALU.add)
                tt_(s5(T2), s5(AM1), s5(LR), ALU.mult)
                tt_(s5(T3), s5(ABI), li, ALU.mult)
                tt_(s5(T2), s5(T2), s5(T3), ALU.add)
                link(dve.reciprocal(s5(DEN), s5(DEN)))
                tt_(s5(FR), s5(T2), s5(DEN), ALU.mult)
                tt_(s5(T2), s5(ABI), s5(LR), ALU.mult)
                tt_(s5(T3), s5(AM1), li, ALU.mult)
                tt_(s5(T2), s5(T2), s5(T3), ALU.subtract)
                tt_(s5(FI), s5(T2), s5(DEN), ALU.mult)

            def s5_inputs():
                dve.wait_ge(bc_loaded, 96)
                dve.wait_ge(s5g, 1)
                fr = s5(FR).unsqueeze(2).broadcast_to([P, ST, S5_CH])
                fi = s5(FI).unsqueeze(2).broadcast_to([P, ST, S5_CH])
                for ri, op in enumerate((ALU.subtract, ALU.add)):
                    mark(dve.tensor_tensor(b_tmp[:, 0, :, :], b_raw[:, ri, :, :], fr, ALU.mult))
                    tt_(b_tmp[:, 1, :, :], b_raw[:, 1 - ri, :, :], fi, ALU.mult)
                    for gl in range(2):
                        rows = slice(64 * gl, 64 * gl + 64)
                        ins = dve.tensor_tensor(b_pad[rows, ri, :, gl, :], b_tmp[rows, 0, :, :], b_tmp[rows, 1, :, :], op)
                    if ri:
                        ins.then_inc(s5_pads, 1)
                    else:
                        link(ins)
                for gl in range(2):
                    dve.tensor_scalar(c_pad[:, 0, :, gl, :], c_pad[:, 0, :, gl, :], parity[:, gl:gl + 1], None, ALU.mult)
                    ins = dve.tensor_scalar(c_pad[:, 1, :, gl, :], c_pad[:, 1, :, gl, :], parity[:, gl:gl + 1], -1.0,
                                            ALU.mult, ALU.mult)
                ins.then_inc(s5_pads, 1)

            def s5_matrices():
                dve.wait_ge(s5_turned, 1)
                for ri in range(2):
                    dve.tensor_copy(bb[:, ri, :, :], ps[:, 4 + ri, :].rearrange("p (q n) -> p q n", n=P))
                    dve.tensor_copy(cc[:, ri, :, :], ps[:, 6 + ri, :].rearrange("p (q n) -> p q n", n=P)
                                    ).then_inc(s5_mats, 1)

            def lru_tap(g, lag):
                for f in range(FT):
                    c = xc[g][:, f, lag:TOK]
                    ins = dve.scalar_tensor_tensor(
                        out=c, in0=xin[:, f, 0:TOK - lag], scalar=pcol("cd_conv_w", (LRU_CONV - 1 - lag) * LT + FT * g + f),
                        in1=c, op0=ALU.mult, op1=ALU.add)
                if lag < LRU_CONV - 1:
                    link(ins)
                else:
                    ins.then_inc(xc_ready, 1)

            def lru_step(g, k):
                if k == 1:
                    dve.wait_ge(tap0_ready, g + 1)
                    lru_tap(g, 1)
                if k == 4:
                    lru_tap(g, 2)
                if k == 4:
                    lru_tap(g, 3)
                if k == 7:
                    dve.wait_ge(gates_read, FT * (g + 1))
                    dve.wait_ge(xc_ready, g + 1)
                    dve.tensor_tensor(xc[g][:, :, :], xc[g][:, :, :], lru_i[:, :, :], ALU.mult).then_inc(gx_ready, 1)
                if k == 9:
                    dve.wait_ge(decayed, g + 1)
                    dve.scalar_tensor_tensor(out=lru_r[:, :, :], in0=lru_i[:, :, :], scalar=1.0, in1=lru_r[:, :, :],
                                             op0=ALU.add, op1=ALU.mult).then_inc(lru_q, 1)
                if k == 11:
                    dve.wait_ge(gx_ready, g + 1)
                    dve.wait_ge(lru_sd, g + 1)
                    link(dve.tensor_tensor(xc[g][:, :, :], xc[g][:, :, :], lru_r[:, :, :], ALU.mult))
                    for f in range(FT):
                        h = hs[:, FT * g + f, :]
                        dve.tensor_tensor_scan(h, h, xc[g][:, f, :], 0.0, ALU.mult, ALU.add).then_inc(hs_ready, 1)

            def gelu_argument(x, u, squared, count, ready):
                dve.wait_ge(squared, count)
                dve.tensor_tensor(u[:, :, :], u[:, :, :], x[:, :, :], ALU.mult).then_inc(ready, 1)

            def gelu_product(x, u, tanh_ready, count):
                dve.wait_ge(tanh_ready, count)
                link(dve.scalar_tensor_tensor(out=x[:, :, :], in0=u[:, :, :], scalar=1.0, in1=x[:, :, :],
                                              op0=ALU.add, op1=ALU.mult))

            def gate_step(g, k):
                if k == 1:
                    gelu_argument(xin, cd_tmp, gelu_sq, g + 1, gelu_u)
                if k == 4:
                    gelu_product(xin, cd_tmp, gelu_th, g + 1)
                    dve.wait_ge(hs_ready, LT)
                    for f in range(FT):
                        dve.tensor_tensor(xin[:, f, :], xin[:, f, :], hs[:, FT * g + f, :], ALU.mult).then_inc(o_ready, 1)
                if k == 6:
                    dve.wait_ge(o_ready, XT + FT * (g + 1))
                    for f in range(FT):
                        n = FT * g + f
                        dve.wait_ge(o_hi, XT + n + 1)
                        dve.scalar_tensor_tensor(out=cat[:, n, 1, :], in0=xin[:, f, :], scalar=0.5, in1=cat[:, n, 0, :],
                                                 op0=ALU.mult, op1=ALU.subtract).then_inc(o_lo, 1)
                    dve.wait_ge(o_lo, XT + FT * (g + 1))

            def s5_states(j):
                q, jj, slot = j // 4, j % 4, j % 2
                pr, pi = (ph[1 - q % 2][:, jj:jj + 1, ri, :].broadcast_to([P, 2, TOK]) for ri in range(2))
                x = ps[:, 6, :].rearrange("p (r n) -> p r n", r=2)
                dve.wait_ge(bu_done, j + 1)
                dve.wait_ge(phases_ready, q + 1)
                dve.tensor_tensor(bq[:, 0, :, :], x, pr, ALU.mult)
                dve.tensor_tensor(bq[:, 1, :, :], x, pi, ALU.mult).then_inc(bu_free, 1)
                dve.wait_ge(bu_free, j + 1)
                if j >= 2:
                    dve.wait_ge(st_ready, j - 1)
                mark(dve.tensor_tensor(gs[:, slot, 0, :], bq[:, 0, 0, :], bq[:, 1, 1, :], ALU.add))
                link(dve.tensor_tensor(gs[:, slot, 1, :], bq[:, 0, 1, :], bq[:, 1, 0, :], ALU.subtract))
                mag = s5p[:, MAG, j:j + 1].broadcast_to([P, TOK])
                for ri in range(2):
                    ins = dve.tensor_tensor_scan(gs[:, slot, ri, :], mag, gs[:, slot, ri, :], 0.0, ALU.mult, ALU.add)
                ins.then_inc(scanned, 1)

            def s5_skip(q):
                dve.wait_ge(y5_done, 4 * (q + 1))
                dve.scalar_tensor_tensor(out=ut[:, q, :], in0=ut[:, q, :], scalar=pcol("cd_d_skip", q),
                                         in1=ps[:, 7, 0:TOK], op0=ALU.mult, op1=ALU.add).then_inc(y5_ready, 1)

            def cd_step(m):
                if m == 0:
                    s5_inputs()
                if m == 4:
                    s5_matrices()
                if m in S5_AT:
                    s5_states(S5_AT.index(m))
                if m in S5_OUT[3::4]:
                    s5_skip(S5_OUT[3::4].index(m))
                for g, at_ in enumerate(LRU_AT):
                    lru_step(g, m - at_)
                if m == S5_END:
                    dve.wait_ge(y5_ready, UT)
                    gelu_argument(ut, s5_gelu, s5_sq, 1, s5_u)
                if m == S5_END + 1:
                    gelu_product(ut, s5_gelu, s5_th, 1)
                    dve.tensor_scalar(ut[:, :, :], ut[:, :, :], 0.5, None, ALU.mult).then_inc(glu_in, 1)
                for g, at_ in enumerate(GATE_AT):
                    gate_step(g, m - at_)

            def glu():
                dve.wait_ge(glu_in, 1)
                for f in range(UT):
                    dve.wait_ge(glu_act, UT)
                    dve.tensor_tensor(ut[:, f, :], ut[:, f, :], s5_gate[:, f, :], ALU.mult).then_inc(g5_ready, 1)
                for f in range(UT):
                    dve.wait_ge(g5_hi, f + 1)
                    dve.tensor_tensor(cat[:, LT + f, 1, :], ut[:, f, :], cat[:, LT + f, 0, :],
                                      ALU.subtract).then_inc(g5_lo, 1)

            def mix_cd():
                u, a, d, h = U_CD, A_CD, D_CD, H_CD
                for n, (kind, _) in enumerate(CD_GROUPS):
                    dst = ut if kind == "u" else xin
                    u, a, d, h = group(kind, u, a, d, h, lambda f: dst[:, f, :],
                                       lambda k: cd_step(PER_GROUP * n + k))
                for m in range(CD_UNITS, CD_STEPS):
                    cd_step(m)
                glu()

            norm(0)
            mix_ab()
            out_proj(U_OUT0, D_OUT0, PER_GROUP)
            norm(1)
            up_proj(U_UP0, A_UP0, H_UP0, 0)
            out_proj(U_DOWN0, D_DOWN0, DOWN_PER)
            norm(2)
            mix_cd()
            out_proj(U_OUT1, D_OUT1, PER_GROUP)
            norm(3)
            up_proj(U_UP1, A_UP1, H_UP1, 1)
            out_proj(U_DOWN1, D_DOWN1, DOWN_PER, last=True)
            norm(4)

        @block.gpsimd
        def _(pool):
            chain = [0]

            def mark(ins):
                chain[0] += 1
                ins.then_inc(g_chain, 1)

            def link(ins):
                mark(ins)
                pool.wait_ge(g_chain, chain[0])

            def constants():
                mark(pool.memset(ident[:, :], 0.0))
                mark(pool.memset(neg_tri[:, :], -1.0))
                mark(pool.memset(strips, 1.0))
                pool.memset(ones[:, :], 1.0).then_inc(consts_ready, 1)
                pool.memset(neg_ones[:, :], -1.0).then_inc(consts_ready, 1)
                pool.wait_ge(g_chain, chain[0])
                pool.affine_select(out=ident[:, :], in_=ident[:, :], compare_op=ALU.not_equal, fill=1.0, base=0,
                                   pattern=[[-1, P]], channel_multiplier=1).then_inc(consts_ready, 1)
                pool.affine_select(out=neg_tri[:, :], in_=neg_tri[:, :], compare_op=ALU.is_ge, fill=0.0, base=0,
                                   pattern=[[-1, P]], channel_multiplier=1).then_inc(consts_ready, 1)
                link(pool.affine_select(out=strips, in_=strips, compare_op=ALU.is_ge, fill=0.0, base=0,
                                        pattern=[[-S5_CH, 8]], channel_multiplier=1))
                pool.affine_select(out=strips, in_=strips, compare_op=ALU.is_ge, fill=0.0, base=S5_CH - 1,
                                   pattern=[[S5_CH, 8]], channel_multiplier=-1).then_inc(consts_ready, 1)

            def cut(dst, src, least, done):
                pool.affine_select(out=dst[:, 0:3:2, :], in_=src[:, 0:3:2, :], compare_op=ALU.is_ge, fill=0.0,
                                   base=-least, pattern=[[0, 2], [1, P]], channel_multiplier=-1).then_inc(done, 1)

            def phases(q):
                ph_q = ph[1 - q % 2]
                if q >= 2:
                    pool.wait_ge(scanned, 4 * (q - 1))
                    pool.wait_ge(st_ready, 4 if q == 2 else 9)
                for ri, src in enumerate((COS, SIN)):
                    mark(pool.tensor_copy(ph_q[:, :, ri, 0:1], s5p[:, src, 4 * q:4 * q + 4].unsqueeze(2)))
                pool.wait_ge(g_chain, chain[0])
                n = 1
                while n < TOK:
                    half = min(n, P // 2)
                    for at_ in range(0, n, half):
                        for ri in range(2):
                            mark(pool.tensor_tensor(pt[:, ri, :, :, 0:half], ph_q[:, :, :, at_:at_ + half],
                                                    ph_q[:, :, ri:ri + 1, n - 1:n].broadcast_to([P, FT, 2, half]),
                                                    ALU.mult))
                        pool.wait_ge(g_chain, chain[0])
                        to = slice(n + at_, n + at_ + half)
                        mark(pool.tensor_tensor(ph_q[:, :, 0, to], pt[:, 0, :, 0, 0:half], pt[:, 1, :, 1, 0:half],
                                                ALU.subtract))
                        ins = pool.tensor_tensor(ph_q[:, :, 1, to], pt[:, 0, :, 1, 0:half], pt[:, 1, :, 0, 0:half],
                                                 ALU.add)
                        if to.stop < TOK:
                            link(ins)
                        else:
                            ins.then_inc(phases_ready, 1)
                            pool.wait_ge(phases_ready, q + 1)
                    n *= 2

            def turn_states(j):
                q, jj, slot = j // 4, j % 4, j % 2
                pr, pi = (ph[1 - q % 2][:, jj:jj + 1, ri, :].broadcast_to([P, 2, TOK]) for ri in range(2))
                pool.wait_ge(scanned, j + 1)
                if j >= 1:
                    pool.wait_ge(st_ready, j)
                mark(pool.tensor_tensor(rot[:, 0, :, :], gs[:, slot, :, :], pr, ALU.mult))
                link(pool.tensor_tensor(rot[:, 1, :, :], gs[:, slot, :, :], pi, ALU.mult))
                if j >= 2:
                    pool.wait_ge(y5_done, j - 1)
                pool.tensor_tensor(st[:, slot, 0, :], rot[:, 0, 0, :], rot[:, 1, 1, :], ALU.subtract)
                pool.tensor_tensor(st[:, slot, 1, :], rot[:, 0, 1, :], rot[:, 1, 0, :], ALU.add).then_inc(st_ready, 1)

            constants()
            for h in range(SSD_HEADS):
                pool.wait_ge(decay_ready, h + 1)
                cut(blk[h % 4], blk[h % 4], 0, decay_cut)
            for h in range(SB_HEADS + 2):
                if h < SB_HEADS:
                    pool.wait_ge(sp_ready, h + 1)
                    cut(blk[h], blk[h], 1, sp_cut)
                if h >= 2:
                    pool.wait_ge(w_exp, h - 1)
                    cut(probs[h - 2], probs[h - 2], 1, w_cut)
            pool.wait_ge(acc_free, A_UP0)
            pool.memset(b_pad[:, :, :, :, :], 0.0).then_inc(s5g, 1)
            pool.wait_ge(acc_free, A_CD)
            pool.wait_ge(s5v, 3)
            phases(0)
            pool.wait_ge(y_lo_ready, 3 * KT)
            phases(1)
            for j in range(ST):
                turn_states(j)
                if j == 3:
                    phases(2)
                if j == 8:
                    phases(3)


_INS = ["x", "norm_mix", "norm_ffn", "norm_final", "ab_w_in", "ab_conv_w", "ab_conv_b", "ab_dt_bias", "ab_a_log",
        "ab_d_skip", "ab_ssd_norm", "ab_w_out", "cd_w_in", "cd_conv_w", "cd_conv_b", "cd_w_a", "cd_b_a", "cd_w_i",
        "cd_b_i", "cd_lambda", "cd_log_dt", "cd_a_re", "cd_a_im", "cd_b_re", "cd_b_im", "cd_c_re", "cd_c_im",
        "cd_d_skip", "cd_w_glu", "cd_b_glu", "cd_w_out", "ffn_w_up", "ffn_conv_w", "ffn_conv_b", "ffn_w_down"]


def kernel(**inputs):
    import numpy as np
    import concourse.bacc as bacc
    from concourse.bass_utils import run_bass_kernel_spmd

    nc = bacc.Bacc("TRN2", target_bir_lowering=False, num_devices=1)
    arrays, tensors = {}, {}
    for name in _INS:
        a = np.ascontiguousarray(inputs[name])
        arrays[f"in_{name}"] = a
        tensors[name] = nc.dram_tensor(f"in_{name}", a.shape, mybir.dt.from_np(a.dtype), kind="ExternalInput").ap()
    out = nc.dram_tensor("out_0", (1, TOK, D), F32, kind="ExternalOutput").ap()
    trunk(nc, tensors, out)
    r = run_bass_kernel_spmd(nc, [arrays], core_ids=[0])
    return r.results[0]["out_0"]
```
